# Optimizing a Trainium2 kernel written in Bass

```python
import jax, jax.numpy as jnp
from jax import lax
import numpy as np

'''One layer of a hybrid decoder trunk: gated parallel token mixers (RWKV-7 time mixing | causal Conformer conv module),
PEER product-key expert FFN, Gemma-3n style per-layer input embedding, final RMSNorm.
Inputs: x (BATCH, SEQ, D_MODEL), p (DEPTH, BATCH, SEQ, PLE_DIM); output (BATCH, SEQ, D_MODEL).'''

D_MODEL = 1024
BATCH = 1
SEQ = 1024
DEPTH = 1

RWKV_HEADS = 8
RWKV_HEAD_DIM = 64
RWKV_WIDTH = RWKV_HEADS * RWKV_HEAD_DIM
DECAY_LORA = 64
AAA_LORA = 64
GATE_LORA = 128
RWKV_COLS = 3 * RWKV_WIDTH + DECAY_LORA + AAA_LORA + GATE_LORA
GN_EPS = 64e-5
CONV_WIDTH = 512
CONV_GROUPS = 8
CONV_K = 31
CONV_COLS = 2 * CONV_WIDTH
GATE_COLS = 2 * D_MODEL
IN_COLS = RWKV_COLS + CONV_COLS + GATE_COLS
LN_EPS = 1e-5
RMS_EPS = 1e-6
PEER_HEADS = 8
N_KEYS = 128
N_EXPERTS = N_KEYS * N_KEYS
PEER_QDIM = 128
PEER_HALF = PEER_QDIM // 2
PEER_TOPK = 16
PEER_CHUNK = 128
PLE_DIM = 256

kernel_name = 'hybrid_rwkv7_conformer_peer'

def rms_norm(x, g):
    xf = x.astype(jnp.float32)
    y = xf * lax.rsqrt(jnp.mean(xf * xf, axis=-1, keepdims=True) + RMS_EPS)
    return (y * g.astype(jnp.float32)).astype(x.dtype)

def token_shift(z):
    return jnp.pad(z, ((0, 0), (1, 0), (0, 0)))[:, :-1]

def rwkv7_recurrence(r, w, k, v, kk, a):
    B, T, H, N = r.shape

    def step(S, inp):
        r_t, w_t, k_t, v_t, kk_t, a_t = inp
        sa = jnp.einsum('bhvk,bhk->bhv', S, -kk_t)
        S = (S * w_t[:, :, None, :] + sa[..., None] * (kk_t * a_t)[:, :, None, :]
             + v_t[..., None] * k_t[:, :, None, :])
        return S, jnp.einsum('bhvk,bhk->bhv', S, r_t)

    xs = tuple(jnp.moveaxis(t, 1, 0) for t in (r, w, k, v, kk, a))
    S0 = jnp.zeros((B, H, N, N), jnp.float32)
    _, y = lax.scan(step, S0, xs)
    return jnp.moveaxis(y, 0, 1)

def rwkv7_branch(z, mu, w0, w_up, a0, a_up, g_up, k_k, k_a, r_k, lnx_g, lnx_b, w_o):
    B, T, _ = z.shape
    f32 = jnp.float32
    z = z + (token_shift(z) - z) * mu
    s0 = RWKV_WIDTH
    splits = [s0, 2 * s0, 3 * s0, 3 * s0 + DECAY_LORA, 3 * s0 + DECAY_LORA + AAA_LORA]
    r, k, v, wl, al, gl = jnp.split(z, splits, axis=-1)
    w_log = -jax.nn.softplus(-(w0 + jnp.tanh(wl) @ w_up)) - 0.5
    decay = jnp.exp(-jnp.exp(w_log.astype(f32)))
    a = jax.nn.sigmoid(a0 + al @ a_up)
    g = jax.nn.sigmoid(gl) @ g_up
    hd = lambda t: t.astype(f32).reshape(B, T, RWKV_HEADS, RWKV_HEAD_DIM)
    kk = hd(k * k_k)
    kk = kk * lax.rsqrt(jnp.maximum(jnp.sum(kk * kk, -1, keepdims=True), 1e-24))
    k = k * (1.0 + (a - 1.0) * k_a)
    rh, kh, vh, ah = hd(r), hd(k), hd(v), hd(a)
    y = rwkv7_recurrence(rh, hd(decay), kh, vh, kk, ah)
    mean = jnp.mean(y, -1, keepdims=True)
    var = jnp.mean(jnp.square(y - mean), -1, keepdims=True)
    y = ((y - mean) * lax.rsqrt(var + GN_EPS)).reshape(B, T, RWKV_WIDTH)
    y = y * lnx_g.astype(f32) + lnx_b.astype(f32)
    bonus = jnp.sum(rh * kh * r_k.astype(f32), -1, keepdims=True) * vh
    y = (y + bonus.reshape(B, T, RWKV_WIDTH)) * g.astype(f32)
    return y.astype(z.dtype) @ w_o

def conformer_conv_branch(z, dw_w, dw_b, ln_g, ln_b, w_o):
    u, gate = jnp.split(z, 2, axis=-1)
    h = u * jax.nn.sigmoid(gate)
    hp = jnp.pad(h, ((0, 0), (CONV_K - 1, 0), (0, 0)))
    h = lax.conv_general_dilated(hp, dw_w[:, None, :].astype(h.dtype), window_strides=(1,), padding='VALID',
                                 dimension_numbers=('NWC', 'WIO', 'NWC'),
                                 feature_group_count=CONV_WIDTH) + dw_b
    hf = h.astype(jnp.float32)
    mean = jnp.mean(hf, -1, keepdims=True)
    var = jnp.mean(jnp.square(hf - mean), -1, keepdims=True)
    hf = (hf - mean) * lax.rsqrt(var + LN_EPS) * ln_g.astype(jnp.float32) + ln_b.astype(jnp.float32)
    h = jax.nn.silu(hf).astype(z.dtype)
    return h @ w_o

def peer_ffn(c, w_q, sub_keys, u_tab, v_tab):
    B, T, D = c.shape
    q = (c @ w_q).reshape(B, T, PEER_HEADS, 2, PEER_HALF)
    s = jnp.einsum('bthpd,hpnd->bthpn', q, sub_keys).astype(jnp.float32)
    s1, i1 = lax.top_k(s[..., 0, :], PEER_TOPK)
    s2, i2 = lax.top_k(s[..., 1, :], PEER_TOPK)
    n_cand = PEER_TOPK * PEER_TOPK
    cand_s = (s1[..., :, None] + s2[..., None, :]).reshape(B, T, PEER_HEADS, n_cand)
    cand_i = (i1[..., :, None] * N_KEYS + i2[..., None, :]).reshape(B, T, PEER_HEADS, n_cand)
    best_s, pos = lax.top_k(cand_s, PEER_TOPK)
    idx = jnp.take_along_axis(cand_i, pos, axis=-1)
    gates = jax.nn.softmax(best_s, axis=-1)
    n_tok = B * T
    n_sel = PEER_HEADS * PEER_TOPK
    n_blk = n_tok // PEER_CHUNK
    xs = c.reshape(n_blk, PEER_CHUNK, D)
    idx = idx.reshape(n_blk, PEER_CHUNK, n_sel)
    gates = gates.reshape(n_blk, PEER_CHUNK, n_sel).astype(c.dtype)

    def block(args):
        xb, ib, gb = args
        u = jnp.take(u_tab, ib, axis=0)
        coef = gb * jax.nn.gelu(jnp.einsum('cd,ced->ce', xb, u), approximate=False)
        return jnp.einsum('ce,ced->cd', coef, jnp.take(v_tab, ib, axis=0))

    return lax.map(block, (xs, idx, gates)).reshape(B, T, D)

def setup_inputs(seed: int = 0) -> dict:
    key = jax.random.key(seed)
    ks = jax.random.split(key, 32)
    L, D = DEPTH, D_MODEL
    n = lambda k, shape, scale: jax.random.normal(k, shape, jnp.float32) * scale
    gain = lambda k, shape: 1.0 + 0.05 * jax.random.normal(k, shape, jnp.float32)
    return {
        'x': n(ks[0], (BATCH, SEQ, D), 1.0),
        'p': n(ks[1], (DEPTH, BATCH, SEQ, PLE_DIM), 1.0),
        'norm_mix_g': gain(ks[2], (L, D)),
        'w_in': n(ks[3], (L, D, IN_COLS), D ** -0.5),
        'rwkv_mu': jax.random.uniform(ks[4], (L, RWKV_COLS), jnp.float32),
        'rwkv_w0': jax.random.uniform(ks[5], (L, RWKV_WIDTH), jnp.float32, -6.0, 0.0),
        'rwkv_w_up': n(ks[6], (L, DECAY_LORA, RWKV_WIDTH), 0.1),
        'rwkv_a0': n(ks[7], (L, RWKV_WIDTH), 0.5),
        'rwkv_a_up': n(ks[8], (L, AAA_LORA, RWKV_WIDTH), 0.5 * AAA_LORA ** -0.5),
        'rwkv_g_up': n(ks[9], (L, GATE_LORA, RWKV_WIDTH), GATE_LORA ** -0.5),
        'rwkv_k_k': 0.85 + n(ks[10], (L, RWKV_WIDTH), 0.05),
        'rwkv_k_a': gain(ks[11], (L, RWKV_WIDTH)),
        'rwkv_r_k': n(ks[12], (L, RWKV_HEADS, RWKV_HEAD_DIM), 0.1),
        'rwkv_lnx_g': gain(ks[13], (L, RWKV_WIDTH)),
        'rwkv_lnx_b': n(ks[14], (L, RWKV_WIDTH), 0.01),
        'rwkv_w_o': n(ks[15], (L, RWKV_WIDTH, D), RWKV_WIDTH ** -0.5),
        'conv_dw_w': n(ks[16], (L, CONV_K, CONV_WIDTH), CONV_K ** -0.5),
        'conv_dw_b': n(ks[17], (L, CONV_WIDTH), 0.01),
        'conv_ln_g': gain(ks[18], (L, CONV_WIDTH)),
        'conv_ln_b': n(ks[19], (L, CONV_WIDTH), 0.01),
        'conv_w_o': n(ks[20], (L, CONV_WIDTH, D), CONV_WIDTH ** -0.5),
        'w_out': n(ks[21], (L, D, D), D ** -0.5),
        'norm_ffn_g': gain(ks[22], (L, D)),
        'peer_w_q': n(ks[23], (L, D, PEER_HEADS * PEER_QDIM), D ** -0.5),
        'peer_sub_keys': n(ks[24], (L, PEER_HEADS, 2, N_KEYS, PEER_HALF), PEER_HALF ** -0.5),
        'peer_u': n(ks[25], (L, N_EXPERTS, D), D ** -0.5),
        'peer_v': n(ks[26], (L, N_EXPERTS, D), 0.5),
        'ple_w_proj': n(ks[27], (L, PLE_DIM, D), PLE_DIM ** -0.5),
        'ple_norm_g': gain(ks[28], (L, D)),
        'ple_w_gate': n(ks[29], (L, D, D), D ** -0.5),
        'final_norm_g': gain(ks[30], (D,)),
    }

def reference(x, p, norm_mix_g, w_in, rwkv_mu, rwkv_w0, rwkv_w_up, rwkv_a0, rwkv_a_up, rwkv_g_up,
              rwkv_k_k, rwkv_k_a, rwkv_r_k, rwkv_lnx_g, rwkv_lnx_b, rwkv_w_o, conv_dw_w, conv_dw_b,
              conv_ln_g, conv_ln_b, conv_w_o, w_out, norm_ffn_g, peer_w_q, peer_sub_keys, peer_u, peer_v,
              ple_w_proj, ple_norm_g, ple_w_gate, final_norm_g):
    h = x
    for i in range(DEPTH):
        a = rms_norm(h, norm_mix_g[i])
        z = a @ w_in[i]
        z_rwkv, z_conv, z_gate = jnp.split(z, [RWKV_COLS, RWKV_COLS + CONV_COLS], axis=-1)
        o_r = rwkv7_branch(z_rwkv, rwkv_mu[i], rwkv_w0[i], rwkv_w_up[i], rwkv_a0[i], rwkv_a_up[i],
                           rwkv_g_up[i], rwkv_k_k[i], rwkv_k_a[i], rwkv_r_k[i], rwkv_lnx_g[i],
                           rwkv_lnx_b[i], rwkv_w_o[i])
        o_c = conformer_conv_branch(z_conv, conv_dw_w[i], conv_dw_b[i], conv_ln_g[i], conv_ln_b[i], conv_w_o[i])
        g_r, g_c = jnp.split(jax.nn.sigmoid(z_gate), 2, axis=-1)
        h = h + (g_r * o_r + g_c * o_c) @ w_out[i]
        h = h + peer_ffn(rms_norm(h, norm_ffn_g[i]), peer_w_q[i], peer_sub_keys[i], peer_u[i], peer_v[i])
        ple_gate = jax.nn.sigmoid(rms_norm(h, ple_norm_g[i]) @ ple_w_gate[i])
        h = h + ple_gate * (p[i] @ ple_w_proj[i])
    return rms_norm(h, final_norm_g)


_drawn_inputs = setup_inputs


def setup_inputs(seed=0):
    import zlib

    import numpy as np

    out = dict(_drawn_inputs(seed))
    spreads = {}
    factors = {'rwkv_lnx_b': 4.638, 'conv_dw_b': 3.223, 'conv_ln_b': 4.412, 'ple_norm_g': 6.457}
    for name, (base, spread) in spreads.items():
        noise = np.random.default_rng([zlib.crc32(name.encode()), seed]).standard_normal(out[name].shape)
        drawn = base * np.exp(spread * noise) if base else spread * noise
        out[name] = __import__('jax').numpy.asarray(drawn.astype(out[name].dtype))
    for name, factor in factors.items():
        out[name] = (out[name] * factor).astype(out[name].dtype)
    return out
```

```python
from contextlib import ExitStack, contextmanager

import numpy as np

import concourse.bass as bass
from concourse import mybir

F32 = mybir.dt.float32
U32 = mybir.dt.uint32
ALU = mybir.AluOpType
ACT = mybir.ActivationFunctionType
AX = mybir.AxisListType

P = 128
D = 1024
T = 1024
KT = D // P
NT = T // P
HALF = 512
NH = T // HALF

HEADS, HD = 8, 64
RW = HEADS * HD
PAIRS = RW // P
RWKV_TILES = (3 * RW + 64 + 64 + 128) // P
RWKV_COLS = RWKV_TILES * P
CONV_W = 512
CONV_TILES = CONV_W // P
TAPS = 31
PADT = TAPS - 1
GATE_TILES = 2 * D // P
GN_EPS, LN_EPS, RMS_EPS = 64e-5, 1e-5, 1e-6
CH = 64
NC = T // CH
DECAY = float(np.exp(-0.5))

PH, NKEY, PHALF, TOPK = 8, 128, 64, 16
NSEL = PH * TOPK
NEXP = NKEY * NKEY
PLE = 256
LOWEST = -3.0e38

VECS = [("mu", RWKV_TILES), ("w0", PAIRS), ("a0", PAIRS), ("k_k", PAIRS), ("k_a", PAIRS),
        ("r_k", PAIRS), ("lnx_g", PAIRS), ("lnx_b", PAIRS), ("dw_b", CONV_TILES),
        ("ln_g", CONV_TILES), ("ln_b", CONV_TILES), ("mix_g", KT), ("ffn_g", KT), ("ple_g", KT)]
COL, _n = {}, 0
for _name, _rows in VECS:
    COL[_name] = _n
    _n += _rows
NVEC = _n


def ds(start, size):
    return bass.ds(start, size)


def at(tile, i):
    return tile[:, ds(i, 1), :].rearrange("p a t -> p (a t)")


def one(tensor, i):
    if isinstance(i, int):
        return tensor[i]
    axes = "abcd"[:len(tensor.shape) - 1]
    return tensor[ds(i, 1)].rearrange(f"i {' '.join(axes)} -> (i {axes[0]}) {' '.join(axes[1:])}")


def col(tile, i):
    return tile[:, ds(i, 1)]


@contextmanager
def semaphores(nc):
    taken = []

    def sem(name):
        taken.append(nc.alloc_semaphore(name))
        return taken[-1]

    yield sem
    nc.clear_and_free_semaphores(taken)
    nc.all_engine_barrier()


class Link:

    def __init__(self, eng, sem, turn=0, each=0, start=0):
        self.eng, self.sem, self.turn, self.each, self.start, self.k = eng, sem, turn, each, start, 0

    def value(self, k):
        return self.turn * self.each + (self.start + k) if self.each else self.start + k

    def mark(self, ins):
        self.k += 1
        ins.then_inc(self.sem, 1)
        return self.k

    def wait(self, k=None):
        self.eng.wait_ge(self.sem, self.value(self.k if k is None else k))

    def __call__(self, ins):
        self.mark(ins)
        self.wait()


def bcast(ap, axis, n):
    return ap.unsqueeze(axis).to_broadcast([*ap.shape[:axis], n, *ap.shape[axis:]])


def project_in(nc, io, sb, dram):
    with ExitStack() as ctx:
        def buf(name, shape, dt=F32):
            return ctx.enter_context(nc.sbuf_tensor(name, shape, dt))

        sem = ctx.enter_context(semaphores(nc))

        ident, vec, cw, zs, cv = sb["ident"], sb["vec"], sb["cw"], sb["zs"], sb["cv"]
        ones = buf("a_ones", [P, P])
        sq = buf("a_sq", [P, 2, T])
        rstd = buf("a_rstd", [P, T])
        aT = buf("a_aT", [P, KT, T])
        w = [buf(f"a_w{i}", [P, KT, P]) for i in range(4)]
        zp = [buf(f"a_zp{i}", [P, T + 1]) for i in range(2)]
        dz = [buf(f"a_dz{i}", [P, T]) for i in range(2)]
        cg = buf("a_cg", [P, T])
        hp = buf("a_hp", [P, CONV_TILES, PADT + T])
        gt = [buf(f"a_gt{i}", [P, T]) for i in range(2)]
        ps = [ctx.enter_context(nc.psum_tensor(f"a_ps{i}", [P, T], F32)) for i in range(4)]

        s_ident = sem("a_identity_made")
        s_ones = sem("a_ones_made")
        s_vec = sem("a_constants_in")
        s_x = [sem(f"a_x_in{i}") for i in range(KT)]
        s_sq = sem("a_x_squared")
        s_sum = sem("a_squares_summed")
        s_var = sem("a_variance_inverted")
        s_rstd = sem("a_rstd_ready")
        s_aT = sem("a_aT_ready")
        s_w = [sem(f"a_w_in{i}") for i in range(4)]
        s_mm = sem("a_z_tile_in_psum")
        s_free = [sem(f"a_psum_tile_free{i}") for i in range(4)]
        s_pad = sem("a_pads_zeroed")
        s_zcp = sem("a_z_tile_copied")
        s_dz = sem("a_z_difference_ready")
        s_zs = sem("a_z_shifted")
        s_sig = sem("a_conv_gate_ready")
        s_h = sem("a_conv_input_ready")
        s_tap = sem("a_conv_tap_done")
        s_dve = sem("a_vector_step")
        s_act = sem("a_scalar_step")
        s_gate = sem("a_mixer_gate_ready")
        s_gout = [sem(f"a_mixer_gate_out{i}") for i in range(2)]

        TILES = RWKV_TILES + 2 * CONV_TILES + GATE_TILES
        cols = [m * P for m in range(RWKV_TILES)]
        for i in range(CONV_TILES):
            cols += [RWKV_COLS + i * P, RWKV_COLS + CONV_W + i * P]
        gates_at = RWKV_COLS + 2 * CONV_W
        win = io["w_in"]
        block = ctx.enter_context(nc.Block())

        @block.gpsimd
        def _(pool):
            pool.memset(ident[:, :], 0.0).then_inc(s_ident, 1)
            pool.memset(ones[:, :], 1.0).then_inc(s_ones, 1)
            for i in range(2):
                pool.memset(zp[i][:, 0:1], 0.0).then_inc(s_pad, 1)
            pool.memset(hp[:, :, 0:PADT], 0.0).then_inc(s_pad, 1)
            pool.wait_ge(s_ident, 1)
            pool.affine_select(out=ident[:, :], in_=ident[:, :], compare_op=ALU.not_equal, fill=1.0,
                               base=0, pattern=[[-1, P]], channel_multiplier=1).then_inc(s_ident, 1)

        @block.sync
        def _(sp):
            for k in range(KT):
                sp.dma_start(aT[:, k, :], io["xT"][k]).then_inc(s_x[k], 16)
            sp.dma_start(vec[:, :], io["vec"]).then_inc(s_vec, 16)
            sp.dma_start(cw[:, :], io["dw_w"]).then_inc(s_vec, 16)
            for m in range(4):
                sp.dma_start(w[m][:, :, :], win[cols[m] // P]).then_inc(s_w[m], 16)
            for m in range(4, len(cols)):
                sp.wait_ge(s_mm, m - 3)
                sp.dma_start(w[m % 4][:, :, :], win[cols[m] // P]).then_inc(s_w[m % 4], 16)
            first = len(cols)
            with sp.Fori(0, GATE_TILES // 4) as q:
                for i in range(4):
                    slot = (first + i) % 4
                    sp.wait_ge(s_mm, q * 4 + (first + i - 3))
                    sp.dma_start(w[slot][:, :, :], win[ds(q * 4 + (gates_at // P + i), 1)].rearrange("a p k c -> (a p) k c"))\
                        .then_inc(s_w[slot], 16)

        @block.tensor
        def _(pe):
            pe.wait_ge(s_ones, 1)
            for k in range(KT):
                pe.wait_ge(s_sq, k + 1)
                for h in range(NH):
                    last = pe.matmul(ps[0][:, h * HALF:(h + 1) * HALF], ones[:, :], sq[:, k % 2, h * HALF:(h + 1) * HALF],
                                     start=(k == 0), stop=(k == KT - 1))
                last.then_inc(s_sum, 1)
            pe.wait_ge(s_aT, KT)

            def z_tile(m, q):
                pe.wait_ge(s_w[m % 4], q * 16 + 16 * (m // 4 + 1))
                pe.wait_ge(s_free[m % 4], q + (m // 4 + 1))
                for h in range(NH):
                    for k in range(KT):
                        last = pe.matmul(ps[m % 4][:, h * HALF:(h + 1) * HALF], w[m % 4][:, k, :],
                                         aT[:, k, h * HALF:(h + 1) * HALF], start=(k == 0), stop=(k == KT - 1))
                last.then_inc(s_mm, 1)

            with pe.Fori(0, TILES // 4) as q:
                for m in range(4):
                    z_tile(m, q)
            for m in range(TILES // 4 * 4, TILES):
                z_tile(m, 0)

        @block.scalar
        def _(act):
            for i in range(4):
                act.sem_inc(s_free[i], 1)
            for k in range(KT):
                act.wait_ge(s_x[k], 16)
                if k >= 2:
                    act.wait_ge(s_sum, k - 1)
                act.activation(sq[:, k % 2, :], aT[:, k, :], ACT.Square).then_inc(s_sq, 1)
            act.wait_ge(s_var, 1)
            act.activation(rstd[:, :], rstd[:, :], ACT.Sqrt).then_inc(s_rstd, 1)

            def z_copy(q, m):
                act.wait_ge(s_mm, q * 4 + (m + 1))
                act.wait_ge(s_dz, q * 4 + (m + 1))
                act.activation(zp[m % 2][:, 1:T + 1], ps[m % 4][:, :], ACT.Copy).then_inc(s_zcp, 1)
                act.wait_ge(s_zcp, q * 4 + (m + 1))
                act.sem_inc(s_free[m % 4], 1)

            with act.Fori(0, RWKV_TILES // 4) as q:
                for m in range(4):
                    z_copy(q, m)
            for m in range(RWKV_TILES // 4 * 4, RWKV_TILES):
                z_copy(0, m)
            for i in range(CONV_TILES):
                m = RWKV_TILES + 2 * i
                act.wait_ge(s_mm, m + 2)
                if i:
                    act.wait_ge(s_h, i)
                act.activation(cg[:, :], ps[(m + 1) % 4][:, :], ACT.Sigmoid).then_inc(s_sig, 1)
            first = RWKV_TILES + 2 * CONV_TILES
            with act.Fori(0, GATE_TILES // 4) as q:
                for i in range(4):
                    m = first + i
                    act.wait_ge(s_mm, q * 4 + (m + 1))
                    act.wait_ge(s_gout[i % 2], q * 32 + 16 * (i // 2 + 1))
                    act.activation(gt[i % 2][:, :], ps[m % 4][:, :], ACT.Sigmoid).then_inc(s_gate, 1)
                    act.wait_ge(s_gate, q * 4 + (i + 1))
                    act.sem_inc(s_free[m % 4], 1)
                    act.dma_start(dram["gates"][ds(q * 4 + i, 1), :, :].rearrange("a p t -> (a p) t"),
                                  gt[i % 2][:, :]).then_inc(s_gout[i % 2], 16)
            for i in range(2):
                act.wait_ge(s_gout[i], 16 * (GATE_TILES // 2 + 1))

        @block.vector
        def _(dve):
            dve.sem_inc(s_dz, 2)
            for i in range(2):
                dve.sem_inc(s_gout[i], 16)
            link = Link(dve, s_dve)
            dve.wait_ge(s_sum, KT)
            link(dve.tensor_scalar(rstd[:, :], ps[0][:, :], 1.0 / D, RMS_EPS, ALU.mult, ALU.add))
            link(dve.reciprocal(rstd[:, :], rstd[:, :]))
            dve.sem_inc(s_var, 1)
            dve.wait_ge(s_rstd, 1)
            dve.wait_ge(s_vec, 32)
            for k in range(KT):
                g = vec[:, COL["mix_g"] + k:COL["mix_g"] + k + 1]
                dve.scalar_tensor_tensor(out=aT[:, k, :], in0=aT[:, k, :], scalar=g, in1=rstd[:, :],
                                         op0=ALU.mult, op1=ALU.mult).then_inc(s_aT, 1)

            def z_shift(q, m):
                dve.wait_ge(s_zcp, q * 4 + (m + 1))
                a = dz[m % 2]
                dve.tensor_tensor(a[:, :], zp[m % 2][:, 0:T], zp[m % 2][:, 1:T + 1], ALU.subtract).then_inc(s_tap, 1)
                dve.wait_ge(s_tap, q * 4 + (m + 1))
                dve.scalar_tensor_tensor(out=at(zs, q * 4 + m),
                                         in0=a[:, :],
                                         scalar=col(vec, q * 4 + (COL["mu"] + m)),
                                         in1=zp[m % 2][:, 1:T + 1], op0=ALU.mult, op1=ALU.add).then_inc(s_dz, 1)

            dve.wait_ge(s_pad, 3)
            with dve.Fori(0, RWKV_TILES // 4) as q:
                for m in range(4):
                    z_shift(q, m)
                    dve.wait_ge(s_dz, q * 4 + (m + 3))
            for m in range(RWKV_TILES // 4 * 4, RWKV_TILES):
                z_shift(0, m)
                dve.wait_ge(s_dz, m + 3)
            for i in range(CONV_TILES):
                m = RWKV_TILES + 2 * i
                dve.wait_ge(s_sig, i + 1)
                dve.tensor_tensor(hp[:, i, PADT:PADT + T], ps[m % 4][:, :], cg[:, :], ALU.mult).then_inc(s_h, 1)
                dve.wait_ge(s_h, i + 1)
                for k in range(2):
                    dve.sem_inc(s_free[(m + k) % 4], 1)
            taps = RWKV_TILES
            with dve.Fori(0, CONV_TILES) as i:
                link = Link(dve, s_tap, i, TAPS, start=taps)

                def tap(j):
                    return col(cw, i + j * CONV_TILES)

                hin = at(hp, i)
                acc = at(cv, i)
                link(dve.tensor_scalar(acc, hin[:, 0:T], tap(0), col(vec, i + COL["dw_b"]), ALU.mult, ALU.add))
                for j in range(1, TAPS):
                    link(dve.scalar_tensor_tensor(out=acc, in0=hin[:, j:j + T], scalar=tap(j), in1=acc,
                                                  op0=ALU.mult, op1=ALU.add))




def prepare_recurrence(nc, io, sb):
    with ExitStack() as ctx:
        def buf(name, shape, dt=F32):
            return ctx.enter_context(nc.sbuf_tensor(name, shape, dt))

        sem = ctx.enter_context(semaphores(nc))

        vec, zs, cv = sb["vec"], sb["zs"], sb["cv"]
        qq, bb, gg, bv, pc = sb["qq"], sb["bb"], sb["gg"], sb["bv"], sb["pc"]
        wa_up = buf("b_wa_up", [P, RW])
        g_up = buf("b_g_up", [P, RW])
        headones = sb["headones"]
        ones = buf("b_ones", [P, P])
        keep = buf("b_keep", [P, T])
        kk = buf("b_kk", [P, T])
        sq = buf("b_sq", [P, T])
        nrm = buf("b_nrm", [P, T])
        am = buf("b_am", [P, T])
        rk = buf("b_rk", [P, T])
        run = buf("b_run", [P, T])
        bef = buf("b_bef", [P, T])
        dec = buf("b_dec", [P, T])
        inv = buf("b_inv", [P, T])
        ps = [ctx.enter_context(nc.psum_tensor(f"b_ps{i}", [P, T], F32)) for i in range(4)]

        s_const = sem("b_constants_made")
        s_up = sem("b_up_weights_in")
        s_lora = sem("b_lora_inputs_ready")
        s_wmm, s_amm, s_gmm = sem("b_w_in_psum"), sem("b_a_in_psum"), sem("b_g_in_psum")
        s_w, s_a, s_g = sem("b_w_ready"), sem("b_a_ready"), sem("b_g_ready")
        s_kk, s_sq, s_ssum = sem("b_kk_raw"), sem("b_kk_squared"), sem("b_kk_square_sum")
        s_nrm, s_rn = sem("b_kk_norm_inverted"), sem("b_kk_norm_ready")
        s_rk, s_rsum, s_bv = sem("b_rk_ready"), sem("b_bonus_sum"), sem("b_bonus_ready")
        s_run, s_bef, s_exp = sem("b_running_sum"), sem("b_sum_before"), sem("b_exponentials")
        s_used = sem("b_exponentials_used")
        s_dve = sem("b_vector_step")
        s_mean, s_diff, s_dsq = sem("b_conv_mean"), sem("b_conv_centred"), sem("b_conv_squared")
        s_var, s_vinv, s_rstd = sem("b_conv_variance"), sem("b_conv_variance_inverted"), sem("b_conv_rstd")
        s_nc, s_silu = sem("b_conv_normed"), sem("b_conv_silu")
        block = ctx.enter_context(nc.Block())

        def vcol(name, i, rows=slice(0, P)):
            return vec[rows, COL[name] + i:COL[name] + i + 1]

        @block.sync
        def _(sp):
            sp.dma_start(wa_up[:, :], io["wa_up"]).then_inc(s_up, 16)
            sp.dma_start(g_up[:, :], io["g_up"]).then_inc(s_up, 16)

        @block.gpsimd
        def _(pool):
            pool.memset(keep[:, :], 1.0).then_inc(s_const, 1)
            pool.memset(ones[:, :], 1.0).then_inc(s_const, 1)
            pool.memset(headones[:, :], 0.0).then_inc(s_const, 1)
            pool.wait_ge(s_const, 3)
            pool.memset(keep[:, :].rearrange("p (c t) -> p c t", t=CH)[:, :, 0:1], 0.0).then_inc(s_const, 1)
            for e in range(2):
                pool.wait_ge(s_const, 4 + e)
                pool.memset(headones[e * HD:(e + 1) * HD, e * HD:(e + 1) * HD], 1.0).then_inc(s_const, 1)

        @block.tensor
        def _(pe):
            pe.wait_ge(s_up, 32)
            pe.wait_ge(s_lora, 2)
            for i in range(PAIRS):
                c = slice(i * P, (i + 1) * P)
                if i:
                    pe.wait_ge(s_w, i)
                for h in range(NH):
                    t = slice(h * HALF, (h + 1) * HALF)
                    last = pe.matmul(ps[0][:, t], wa_up[0:64, c], zs[0:64, 12, t], start=True, stop=True)
                last.then_inc(s_wmm, 1)
                if i:
                    pe.wait_ge(s_a, i)
                for h in range(NH):
                    t = slice(h * HALF, (h + 1) * HALF)
                    last = pe.matmul(ps[1][:, t], wa_up[64:P, c], zs[64:P, 12, t], start=True, stop=True)
                last.then_inc(s_amm, 1)
                if i:
                    pe.wait_ge(s_nrm, i)
                for h in range(NH):
                    t = slice(h * HALF, (h + 1) * HALF)
                    last = pe.matmul(ps[2][:, t], g_up[:, c], zs[:, 13, t], start=True, stop=True)
                last.then_inc(s_gmm, 1)
                pe.wait_ge(s_const, 6)
                pe.wait_ge(s_sq, i + 1)
                pe.wait_ge(s_g, i + 1)
                for h in range(NH):
                    t = slice(h * HALF, (h + 1) * HALF)
                    last = pe.matmul(ps[2][:, t], headones[:, :], sq[:, t], start=True, stop=True)
                last.then_inc(s_ssum, 1)
                pe.wait_ge(s_rk, i + 1)
                if i:
                    pe.wait_ge(s_bv, i)
                for h in range(NH):
                    t = slice(h * HALF, (h + 1) * HALF)
                    last = pe.matmul(ps[3][:, t], headones[:, :], rk[:, t], start=True, stop=True)
                last.then_inc(s_rsum, 1)
            pe.wait_ge(s_w, PAIRS)
            for i in range(CONV_TILES):
                for h in range(NH):
                    t = slice(h * HALF, (h + 1) * HALF)
                    last = pe.matmul(ps[0][:, t], ones[:, :], cv[:, i, t], start=(i == 0), stop=(i == CONV_TILES - 1),
                                     skip_group_check=True)
            last.then_inc(s_mean, 1)
            pe.wait_ge(s_a, PAIRS)
            for i in range(CONV_TILES):
                pe.wait_ge(s_dsq, i + 1)
                for h in range(NH):
                    t = slice(h * HALF, (h + 1) * HALF)
                    last = pe.matmul(ps[1][:, t], ones[:, :], (sq, rk)[i % 2][:, t], start=(i == 0), stop=(i == CONV_TILES - 1),
                                     skip_group_check=True)
                last.then_inc(s_var, 1)

        @block.scalar
        def _(act):
            act.activation(zs[0:64, 12, :], zs[0:64, 12, :], ACT.Tanh).then_inc(s_lora, 1)
            act.activation(zs[:, 13, :], zs[:, 13, :], ACT.Sigmoid).then_inc(s_lora, 1)
            for i in range(PAIRS):
                act.wait_ge(s_wmm, i + 1)
                act.activation(qq[:, i, :], ps[0][:, :], ACT.Sigmoid, bias=vcol("w0", i)).then_inc(s_w, 1)
                act.wait_ge(s_amm, i + 1)
                act.activation(bb[:, i, :], ps[1][:, :], ACT.Sigmoid, bias=vcol("a0", i)).then_inc(s_a, 1)
                act.wait_ge(s_gmm, i + 1)
                act.activation(gg[:, i, :], ps[2][:, :], ACT.Copy).then_inc(s_g, 1)
                act.wait_ge(s_kk, i + 1)
                if i:
                    act.wait_ge(s_ssum, i)
                act.activation(sq[:, :], kk[:, :], ACT.Square).then_inc(s_sq, 1)
                act.wait_ge(s_bef, i + 1)
                if i:
                    act.wait_ge(s_used, i)
                act.activation(dec[:, :], run[:, :], ACT.Exp, scale=-DECAY).then_inc(s_exp, 1)
                act.activation(inv[:, :], run[:, :], ACT.Exp, scale=DECAY).then_inc(s_exp, 1)
                act.activation(bef[:, :], bef[:, :], ACT.Exp, scale=-DECAY).then_inc(s_exp, 1)
                act.wait_ge(s_nrm, i + 1)
                act.activation(nrm[:, :], nrm[:, :], ACT.Sqrt).then_inc(s_rn, 1)
            for i in range(CONV_TILES):
                act.wait_ge(s_diff, i + 1)
                if i == 0:
                    act.wait_ge(s_ssum, PAIRS)
                if i == 1:
                    act.wait_ge(s_rsum, PAIRS)
                if i >= 2:
                    act.wait_ge(s_var, i - 1)
                act.activation((sq, rk)[i % 2][:, :], cv[:, i, :], ACT.Square).then_inc(s_dsq, 1)
            act.wait_ge(s_vinv, 1)
            act.activation(nrm[:, :], nrm[:, :], ACT.Sqrt).then_inc(s_rstd, 1)
            for i in range(CONV_TILES):
                act.wait_ge(s_nc, i + 1)
                act.activation(cv[:, i, :], cv[:, i, :], ACT.Silu, scale=vcol("ln_g", i), bias=vcol("ln_b", i)).then_inc(s_silu, 1)

        @block.vector
        def _(dve):
            link = Link(dve, s_dve)
            for i in range(PAIRS):
                r, k, v = zs[:, i, :], zs[:, PAIRS + i, :], zs[:, 2 * PAIRS + i, :]
                dve.tensor_scalar(kk[:, :], k, vcol("k_k", i), None, ALU.mult).then_inc(s_kk, 1)
                dve.wait_ge(s_const, 6)
                dve.wait_ge(s_w, i + 1)
                dve.tensor_tensor_scan(run[:, :], keep[:, :], qq[:, i, :], 0.0, ALU.mult, ALU.add).then_inc(s_run, 1)
                dve.wait_ge(s_run, i + 1)
                dve.tensor_tensor(bef[:, :], run[:, :], qq[:, i, :], ALU.subtract).then_inc(s_bef, 1)
                dve.wait_ge(s_a, i + 1)
                link(dve.tensor_scalar(am[:, :], bb[:, i, :], -1.0, vcol("k_a", i), ALU.add, ALU.mult))
                dve.wait_ge(s_kk, i + 1)
                link(dve.scalar_tensor_tensor(out=k, in0=am[:, :], scalar=1.0, in1=k, op0=ALU.add, op1=ALU.mult))
                if i:
                    dve.wait_ge(s_rsum, i)
                dve.scalar_tensor_tensor(out=rk[:, :], in0=r, scalar=vcol("r_k", i), in1=k, op0=ALU.mult,
                                         op1=ALU.mult).then_inc(s_rk, 1)
                dve.wait_ge(s_ssum, i + 1)
                link(dve.tensor_scalar(nrm[:, :], ps[2][:, :], 1e-24, None, ALU.max))
                dve.reciprocal(nrm[:, :], nrm[:, :]).then_inc(s_nrm, 1)
                dve.wait_ge(s_rsum, i + 1)
                dve.tensor_tensor(bv[:, i, :], ps[3][:, :], v, ALU.mult).then_inc(s_bv, 1)
                dve.wait_ge(s_exp, 3 * (i + 1))
                dve.wait_ge(s_rk, i + 1)
                link(dve.tensor_tensor(r, r, dec[:, :], ALU.mult))
                link(dve.tensor_copy(pc[:, i, :], dec[:, :].rearrange("p (c t) -> p c t", t=CH)[:, :, CH - 1]))
                link(dve.tensor_tensor(k, k, inv[:, :], ALU.mult))
                dve.wait_ge(s_rn, i + 1)
                link(dve.tensor_tensor(kk[:, :], kk[:, :], nrm[:, :], ALU.mult))
                link(dve.tensor_tensor(bb[:, i, :], bb[:, i, :], kk[:, :], ALU.mult))
                link(dve.tensor_tensor(bb[:, i, :], bb[:, i, :], inv[:, :], ALU.mult))
                link(dve.scalar_tensor_tensor(out=qq[:, i, :], in0=kk[:, :], scalar=-1.0, in1=bef[:, :], op0=ALU.mult,
                                              op1=ALU.mult))
                dve.sem_inc(s_used, 1)
            dve.wait_ge(s_mean, 1)
            link(dve.tensor_scalar(am[:, :], ps[0][:, :], 1.0 / CONV_W, None, ALU.mult))
            for i in range(CONV_TILES):
                dve.tensor_tensor(cv[:, i, :], cv[:, i, :], am[:, :], ALU.subtract).then_inc(s_diff, 1)
            dve.wait_ge(s_var, CONV_TILES)
            link(dve.tensor_scalar(nrm[:, :], ps[1][:, :], 1.0 / CONV_W, LN_EPS, ALU.mult, ALU.add))
            dve.reciprocal(nrm[:, :], nrm[:, :]).then_inc(s_vinv, 1)
            dve.wait_ge(s_rstd, 1)
            for i in range(CONV_TILES):
                dve.wait_ge(s_diff, i + 1)
                dve.wait_ge(s_dsq, i + 1)
                dve.tensor_tensor(cv[:, i, :], cv[:, i, :], nrm[:, :], ALU.mult).then_inc(s_nc, 1)



MASKS = 16
SUB = 16


def recurrence(nc, io, sb):
    with ExitStack() as ctx:
        def buf(name, shape, dt=F32):
            return ctx.enter_context(nc.sbuf_tensor(name, shape, dt))

        sem = ctx.enter_context(semaphores(nc))

        ident, zs, qq, bb, pc = sb["ident"], sb["zs"], sb["qq"], sb["bb"], sb["pc"]
        U = 2 * PAIRS
        qr = buf("c_qr", [P, PAIRS, 2, 2, CH])
        bk = buf("c_bk", [P, PAIRS, 2, 2, CH])
        vs = buf("c_vs", [P, PAIRS, CH + P])
        gs = buf("c_gs", [P, 2, 2, PAIRS, P])
        bt = buf("c_bt", [P, 2, PAIRS, P])
        xs = buf("c_xs", [P, 2, PAIRS, 2, HD])
        rs = buf("c_rs", [CH, PAIRS, 2, HD])
        st = buf("c_st", [P, PAIRS, 2, HD])
        tmp = buf("c_tmp", [P, PAIRS, HD])
        m_g, m_dt = buf("c_m_g", [P, P]), buf("c_m_dt", [CH, CH])
        m_d, m_e = buf("c_m_d", [CH, CH]), buf("c_m_e", [CH, CH])
        names = ("d", "dt", "e", "z", "d2", "d2t", "ift")
        inv = [{n: buf(f"c_{n}{e}", [CH, U, CH]) for n in names} for e in range(2)]
        pg = [ctx.enter_context(nc.psum_tensor(f"c_pg{e}", [P, 2 * HALF], F32)) for e in range(2)]
        pi = [[ctx.enter_context(nc.psum_tensor(f"c_pi{e}{j}", [P, HALF], F32)) for j in range(2)] for e in range(2)]

        s_pe, s_pool = sem("c_tensor_waits_passed"), sem("c_gpsimd_waits_passed")
        s_mask = sem("c_masks_ready")
        s_ops = sem("c_operands_copied")
        s_g = sem("c_products_in_psum")
        s_gs = sem("c_products_masked")
        s_i = [sem(f"c_inverse_step{e}") for e in range(2)]
        s_ia = [sem(f"c_inverse_copied{e}") for e in range(2)]
        s_id = [sem(f"c_inverse_added{e}") for e in range(2)]
        s_tr, s_trc = sem("c_turned"), sem("c_turned_copied")
        s_seq = sem("c_chain_step")
        s_cp = sem("c_chain_copied")
        s_y = sem("c_y_copied")
        s_sum, s_st = sem("c_state_summed"), sem("c_state_ready")
        block = ctx.enter_context(nc.Block())

        def pin(eng):
            eng.sem_inc(s_pe if eng.engine == nc.tensor.engine else s_pool, 1)

        @block.gpsimd
        def _(pool):
            k = 0

            def step(ins):
                nonlocal k
                k += 1
                ins.then_inc(s_mask, 1)
                pool.wait_ge(s_mask, k)

            step(pool.memset(st[:, :, :, :], 0.0))
            step(pool.memset(xs[:, :, :, :, :], 0.0))
            step(pool.memset(vs[:, :, :], 0.0))
            for m in (m_g, m_dt, m_d, m_e):
                step(pool.memset(m[:, :], 1.0))
            step(pool.memset(m_g[0:CH, 0:CH], 0.0))
            step(pool.affine_select(out=m_g[0:CH, CH:P], in_=m_g[0:CH, CH:P], compare_op=ALU.is_ge, fill=0.0, base=0,
                                    pattern=[[1, CH]], channel_multiplier=-1))
            step(pool.affine_select(out=m_g[CH:P, 0:CH], in_=m_g[CH:P, 0:CH], compare_op=ALU.is_gt, fill=0.0, base=0,
                                    pattern=[[1, CH]], channel_multiplier=-1))
            step(pool.affine_select(out=m_g[CH:P, CH:P], in_=m_g[CH:P, CH:P], compare_op=ALU.is_ge, fill=0.0, base=0,
                                    pattern=[[1, CH]], channel_multiplier=-1))
            NB = CH // SUB

            def blocks(m):
                return m[:, :].rearrange("p (b j) -> p b j", j=SUB)

            step(pool.affine_select(out=blocks(m_dt), in_=blocks(m_dt), compare_op=ALU.is_gt, fill=0.0, base=0,
                                    pattern=[[SUB, NB], [1, SUB]], channel_multiplier=-1))
            step(pool.affine_select(out=blocks(m_dt), in_=blocks(m_dt), compare_op=ALU.is_ge, fill=0.0, base=0,
                                    pattern=[[-SUB, NB], [0, SUB]], channel_multiplier=1))
            step(pool.affine_select(out=blocks(m_d), in_=blocks(m_d), compare_op=ALU.is_gt, fill=0.0, base=0,
                                    pattern=[[-SUB, NB], [-1, SUB]], channel_multiplier=1))
            step(pool.affine_select(out=blocks(m_d), in_=blocks(m_d), compare_op=ALU.is_ge, fill=0.0, base=SUB - 1,
                                    pattern=[[SUB, NB], [0, SUB]], channel_multiplier=-1))
            step(pool.affine_select(out=blocks(m_e), in_=blocks(m_e), compare_op=ALU.is_ge, fill=0.0, base=-SUB,
                                    pattern=[[-SUB, NB], [0, SUB]], channel_multiplier=1))
            masks = k
            assert masks == MASKS
            with pool.Fori(0, NT) as t:
                pool.wait_ge(s_seq, t * 8 + 1)
                pin(pool)
                tok = ds(t * P, P)

                def chunks(a):
                    return a[:, :, tok].rearrange("p i (c t) -> p i c t", t=CH)

                pool.tensor_copy(qr[:, :, :, 0, :], chunks(qq)).then_inc(s_ops, 1)
                pool.tensor_copy(bk[:, :, :, 0, :], chunks(bb)).then_inc(s_ops, 1)
                pool.tensor_copy(qr[:, :, :, 1, :], chunks(zs[:, 0:PAIRS, :])).then_inc(s_ops, 1)
                pool.tensor_copy(bk[:, :, :, 1, :], chunks(zs[:, PAIRS:2 * PAIRS, :])).then_inc(s_ops, 1)
                pool.tensor_copy(vs[:, :, CH:], zs[:, 2 * PAIRS:3 * PAIRS, tok]).then_inc(s_ops, 1)

        @block.tensor
        def _(pe):
            pe.sem_inc(s_seq, 1)
            with pe.Fori(0, NT) as t:
                def inverse(e, step, *products):
                    for out, a, b in products:
                        for u in range(U):
                            o = pi[e][out][0:CH, u * CH:(u + 1) * CH]
                            if b is None:
                                last = pe.transpose(o, inv[e][a][:, u, :], ident[0:CH, 0:CH])
                            else:
                                last = pe.matmul(o, inv[e][a][:, u, :], inv[e][b][:, u, :], start=True, stop=True)
                    last.then_inc(s_i[e], 1)

                def after_copy(e, n):
                    pe.wait_ge(s_ia[e], t * 10 + n)
                    pin(pe)

                def after_add(e, n):
                    pe.wait_ge(s_id[e], t * 9 + n)
                    pin(pe)

                pe.wait_ge(s_ops, t * 5 + 4)
                pe.wait_ge(s_y, t * 2 + 1)
                pe.wait_ge(s_sum, t * 4 + 1)
                pin(pe)
                for e in range(2):
                    h = slice(e * HD, (e + 1) * HD)
                    for c in range(2):
                        for i in range(PAIRS):
                            u = c * PAIRS + i
                            last = pe.matmul(pg[e][:, u * P:(u + 1) * P], bk[h, i, c, :, :], qr[h, i, c, :, :],
                                             start=True, stop=True)
                    last.then_inc(s_g, 1)
                for e in range(2):
                    h = slice(e * HD, (e + 1) * HD)
                    for c in range(2):
                        for i in range(PAIRS):
                            u = c * PAIRS + i
                            last = pe.matmul(pi[e][0][0:CH, u * CH:(u + 1) * CH], qr[h, i, c, 0, :], bk[h, i, c, 0, :],
                                             start=True, stop=True)
                    last.then_inc(s_i[e], 1)
                for e in range(2):
                    after_add(e, 4)
                    inverse(e, 2, (0, "dt", "d"), (1, "d", "dt"))
                pe.wait_ge(s_ops, t * 5 + 5)
                pe.wait_ge(s_gs, t * 2 + 2)
                pin(pe)
                for c in range(2):
                    for i in range(PAIRS):
                        u = c * PAIRS + i
                        last = pe.transpose(pg[0][:, u * P:(u + 1) * P], bk[:, i, c, :, :].rearrange("p a t -> p (a t)"), ident[:, :])
                last.then_inc(s_tr, 1)
                for c in range(2):
                    for i in range(PAIRS):
                        u = c * PAIRS + i
                        last = pe.transpose(pg[1][:, u * P:(u + 1) * P], vs[:, i, c * CH:c * CH + P], ident[:, :])
                last.then_inc(s_tr, 1)
                for e in range(2):
                    after_copy(e, 2)
                    inverse(e, 3, (0, "d2t", "d2"), (1, "d2", "d2t"))
                for e in range(2):
                    after_copy(e, 4)
                    inverse(e, 4, (0, "d2", "z"), (1, "dt", "d"))
                for e in range(2):
                    after_copy(e, 5)
                    after_add(e, 5)
                    inverse(e, 5, (0, "d", "z"))
                for e in range(2):
                    after_add(e, 6)
                    inverse(e, 6, (1, "d2t", "z"))
                for e in range(2):
                    after_add(e, 7)
                    inverse(e, 7, (0, "z", "e"), (1, "e", "z"))
                for e in range(2):
                    after_copy(e, 7)
                    after_add(e, 8)
                    inverse(e, 8, (0, "dt", "d2"), (1, "z", None))
                for e in range(2):
                    after_copy(e, 9)
                    inverse(e, 9, (0, "d2t", "ift"))
                for e in range(2):
                    after_add(e, 9)
                    inverse(e, 10, (1, "d", "ift"))
                for c in range(2):
                    pe.wait_ge(s_trc, t * 2 + 2)
                    pe.wait_ge(s_st, t * 4 + (2 * c + 1) if c == 0 else t * 4 + 3)
                    pe.wait_ge(s_st, t * 4 + 2 * c + 2)
                    pin(pe)
                    for i in range(PAIRS):
                        pe.matmul(pg[0][0:CH, i * P:(i + 1) * P], qr[:, i, c, 0, :], st[:, i, :, :], start=True, stop=False)
                        for e in range(2):
                            last = pe.matmul(pg[0][0:CH, i * P + e * HD:i * P + (e + 1) * HD], gs[:, e, c, i, 0:CH],
                                             xs[:, c, i, e, :], start=False, stop=(e == 1))
                    last.then_inc(s_seq, 1)
                    pe.wait_ge(s_cp, t * 4 + (2 * c + 1))
                    if c == 0:
                        for e in range(2):
                            pe.wait_ge(s_ia[e], t * 10 + 10)
                    pin(pe)
                    for i in range(PAIRS):
                        for e in range(2):
                            last = pe.matmul(pg[0][0:CH, HALF + i * P + e * HD:HALF + i * P + (e + 1) * HD],
                                             inv[e]["e"][:, c * PAIRS + i, :], rs[:, i, e, :], start=True, stop=True)
                    last.then_inc(s_seq, 1)
                    pe.wait_ge(s_cp, t * 4 + (2 * c + 2))
                    if c == 1:
                        pe.wait_ge(s_y, t * 2 + 2)
                    pin(pe)
                    for i in range(PAIRS):
                        pe.matmul(pg[1][:, i * CH:(i + 1) * CH], st[:, i, :, :].rearrange("p e v -> p (e v)"), qr[:, i, c, 1, :],
                                  start=(i == 0), stop=False, skip_group_check=True)
                    for i in range(PAIRS):
                        for e in range(2):
                            last = pe.matmul(pg[1][e * HD:(e + 1) * HD, i * CH:(i + 1) * CH], xs[:, c, i, e, :],
                                             gs[:, e, c, i, CH:P], start=False, stop=(i == PAIRS - 1), skip_group_check=True)
                    last.then_inc(s_seq, 1)
                    for i in range(PAIRS):
                        for e in range(2):
                            last = pe.matmul(pg[1][e * HD:(e + 1) * HD, HALF + i * HD:HALF + (i + 1) * HD],
                                             bt[:, c, i, e * HD:(e + 1) * HD], xs[:, c, i, e, :], start=True, stop=True)
                    last.then_inc(s_seq, 1)

        @block.scalar
        def _(act):
            act.sem_inc(s_y, 1)
            with act.Fori(0, NT) as t:
                def copies(e, step, *pairs):
                    act.wait_ge(s_i[e], t * 10 + step)
                    for src, dst in pairs:
                        act.activation(inv[e][dst][:, :, :], pi[e][src][0:CH, :].rearrange("p (u t) -> p u t", t=CH),
                                       ACT.Copy).then_inc(s_ia[e], 1)

                for e in range(2):
                    copies(e, 2, (0, "d2"), (1, "d2t"))
                act.wait_ge(s_tr, t * 2 + 2)
                act.activation(bt[:, :, :, :], pg[0][:, :].rearrange("p (c i k) -> p c i k", c=2, i=PAIRS), ACT.Copy).then_inc(s_trc, 1)
                act.activation(xs[CH:P, :, :, :, :].rearrange("p c i e v -> p (c i e v)"), pg[1][CH:P, :], ACT.Copy).then_inc(s_trc, 1)
                for e in range(2):
                    copies(e, 3, (0, "d"), (1, "dt"))
                for e in range(2):
                    copies(e, 4, (1, "d2t"))
                for e in range(2):
                    copies(e, 7, (0, "d2"), (1, "dt"))
                for e in range(2):
                    copies(e, 8, (0, "d2t"), (1, "d"))
                for e in range(2):
                    copies(e, 10, (1, "e"))
                for c in range(2):
                    act.wait_ge(s_seq, t * 8 + (4 * c + 2))
                    act.activation(rs[:, :, :, :].rearrange("p i e v -> p (i e v)"), pg[0][0:CH, 0:HALF], ACT.Copy).then_inc(s_cp, 1)
                    act.wait_ge(s_seq, t * 8 + (4 * c + 3))
                    act.activation(xs[0:CH, c, :, :, :].rearrange("p i e v -> p (i e v)"), pg[0][0:CH, HALF:], ACT.Copy).then_inc(s_cp, 1)
                    act.wait_ge(s_seq, t * 8 + (4 * c + 4))
                    act.activation(zs[:, 0:PAIRS, ds(t * P + c * CH, CH)], pg[1][:, 0:PAIRS * CH].rearrange("p (i t) -> p i t", t=CH),
                                   ACT.Copy).then_inc(s_y, 1)

        @block.vector
        def _(dve):
            dve.wait_ge(s_mask, MASKS)
            dve.sem_inc(s_st, 2)
            dve.sem_inc(s_sum, 1)
            with dve.Fori(0, NT) as t:
                def mask(m, shape):
                    return m.unsqueeze(1).to_broadcast(shape)

                def add(e, step, src, other, dst, n):
                    dve.wait_ge(s_i[e], t * 10 + step)
                    dve.wait_ge(s_id[e], t * 9 + n - 1)
                    dve.tensor_tensor(inv[e][dst][:, :, :], pi[e][src][0:CH, :].rearrange("p (u t) -> p u t", t=CH),
                                      inv[e][other][:, :, :], ALU.add).then_inc(s_id[e], 1)

                for e in range(2):
                    g = pg[e][:, :].rearrange("p (u t) -> p u t", t=P)
                    dve.wait_ge(s_g, t * 2 + (e + 1))
                    dve.tensor_tensor(gs[:, e, :, :, :].rearrange("p c i t -> p (c i) t"), g, mask(m_g[:, :], [P, U, P]),
                                      ALU.mult).then_inc(s_gs, 1)
                    dve.tensor_tensor(inv[e]["dt"][:, :, :], g[0:CH, :, 0:CH], mask(m_dt[:, :], [CH, U, CH]),
                                      ALU.mult).then_inc(s_id[e], 1)
                for e in range(2):
                    p = pi[e][0][0:CH, :].rearrange("p (u t) -> p u t", t=CH)
                    dve.wait_ge(s_i[e], t * 10 + 1)
                    dve.tensor_tensor(inv[e]["d"][:, :, :], p, mask(m_d[:, :], [CH, U, CH]), ALU.mult).then_inc(s_id[e], 1)
                    dve.tensor_tensor(inv[e]["e"][:, :, :], p, mask(m_e[:, :], [CH, U, CH]), ALU.mult).then_inc(s_id[e], 1)
                    dve.wait_ge(s_id[e], t * 9 + 1)
                    dve.tensor_tensor(inv[e]["z"][:, :, :], inv[e]["dt"][:, :, :], mask(ident[0:CH, 0:CH], [CH, U, CH]),
                                      ALU.add).then_inc(s_id[e], 1)
                for e in range(2):
                    add(e, 4, 0, "z", "z", 5)
                for e in range(2):
                    add(e, 5, 0, "z", "z", 6)
                for e in range(2):
                    add(e, 6, 1, "z", "z", 7)
                for e in range(2):
                    dve.wait_ge(s_ia[e], t * 10 + 7)
                    dve.tensor_tensor(inv[e]["ift"][:, :, :], inv[e]["dt"][:, :, :],
                                      mask(ident[0:CH, 0:CH], [CH, U, CH]), ALU.add).then_inc(s_id[e], 1)
                for e in range(2):
                    add(e, 9, 0, "ift", "ift", 9)
                for c in range(2):
                    dve.wait_ge(s_seq, t * 8 + (4 * c + 5))
                    for e in range(2):
                        h = slice(e * HD, (e + 1) * HD)
                        dve.tensor_tensor(tmp[h, :, :], pg[1][h, HALF:HALF + PAIRS * HD].rearrange("p (i v) -> p i v", v=HD),
                                          st[h, :, e, :], ALU.add).then_inc(s_sum, 1)
                    for e in range(2):
                        h = slice(e * HD, (e + 1) * HD)
                        dve.wait_ge(s_sum, t * 4 + (2 * c + e + 2))
                        dve.tensor_tensor(st[h, :, e, :], tmp[h, :, :], pc[h, :, ds(t * 2 + c, 1)].to_broadcast([HD, PAIRS, HD]),
                                          ALU.mult).then_inc(s_st, 1)




def mix(nc, io, sb, dram):
    with ExitStack() as ctx:
        def buf(name, shape, dt=F32):
            return ctx.enter_context(nc.sbuf_tensor(name, shape, dt))

        sem = ctx.enter_context(semaphores(nc))

        vec, zs, cv, gg, bv, headones = (sb[n] for n in ("vec", "zs", "cv", "gg", "bv", "headones"))
        sq = buf("d_sq", [P, T])
        rstd = buf("d_rstd", [P, T])
        wr = [buf(f"d_wr{i}", [P, PAIRS, P]) for i in range(2)]
        wc = [buf(f"d_wc{i}", [P, CONV_TILES, P]) for i in range(2)]
        gr = [buf(f"d_gr{i}", [P, T]) for i in range(2)]
        gc = [buf(f"d_gc{i}", [P, T]) for i in range(2)]
        pr = [ctx.enter_context(nc.psum_tensor(f"d_pr{i}", [P, T], F32)) for i in range(2)]
        pc = [ctx.enter_context(nc.psum_tensor(f"d_pc{i}", [P, T], F32)) for i in range(2)]
        s_mean, s_cen, s_sq = sem("d_y_mean"), sem("d_y_centred"), sem("d_y_squared")
        s_var, s_vinv, s_rstd = sem("d_y_variance"), sem("d_y_variance_inverted"), sem("d_y_rstd")
        s_norm, s_y = sem("d_y_normed"), sem("d_y_ready")
        s_dve = sem("d_vector_step")
        s_wr = [sem(f"d_w_r_in{i}") for i in range(2)]
        s_wc = [sem(f"d_w_c_in{i}") for i in range(2)]
        s_gr = [sem(f"d_gate_r_in{i}") for i in range(2)]
        s_gc = [sem(f"d_gate_c_in{i}") for i in range(2)]
        s_mm = sem("d_outputs_in_psum")
        s_free = sem("d_psum_free")
        s_mul, s_mix = sem("d_gated"), sem("d_mixed")
        s_out = [sem(f"d_mix_out{i}") for i in range(2)]
        block = ctx.enter_context(nc.Block())

        @block.sync
        def _(sp):
            def loads(m, i):
                sp.dma_start(wr[i][:, :, :], one(io["w_r"], m)).then_inc(s_wr[i], 16)
                sp.dma_start(wc[i][:, :, :], one(io["w_c"], m)).then_inc(s_wc[i], 16)

            def gate_loads(m, i):
                sp.dma_start(gr[i][:, :], one(dram["gates"], m)).then_inc(s_gr[i], 16)
                sp.dma_start(gc[i][:, :], one(dram["gates"], m + KT)).then_inc(s_gc[i], 16)

            for i in range(2):
                loads(i, i)
                gate_loads(i, i)
            with sp.Fori(0, KT // 2 - 1) as q:
                for i in range(2):
                    sp.wait_ge(s_mm, q * 2 + (i + 1))
                    loads(q * 2 + (i + 2), i)
                    sp.wait_ge(s_out[i], q * 16 + 16)
                    gate_loads(q * 2 + (i + 2), i)

        @block.tensor
        def _(pe):
            for i in range(PAIRS):
                y = zs[:, i, :]
                if i >= 2:
                    pe.wait_ge(s_cen, i - 1)
                for h in range(NH):
                    t = slice(h * HALF, (h + 1) * HALF)
                    last = pe.matmul(pr[i % 2][:, t], headones[:, :], y[:, t], start=True, stop=True)
                last.then_inc(s_mean, 1)
                pe.wait_ge(s_sq, i + 1)
                if i >= 2:
                    pe.wait_ge(s_vinv, i - 1)
                for h in range(NH):
                    t = slice(h * HALF, (h + 1) * HALF)
                    last = pe.matmul(pc[i % 2][:, t], headones[:, :], sq[:, t], start=True, stop=True)
                last.then_inc(s_var, 1)
            pe.wait_ge(s_y, PAIRS)
            with pe.Fori(0, KT // 2) as q:
                for i in range(2):
                    pe.wait_ge(s_wr[i], q * 16 + 16)
                    pe.wait_ge(s_wc[i], q * 16 + 16)
                    pe.wait_ge(s_free, q * 2 + (i + 1))
                    for w, x, p, n in ((wr, zs, pr, PAIRS), (wc, cv, pc, CONV_TILES)):
                        for h in range(NH):
                            t = slice(h * HALF, (h + 1) * HALF)
                            for k in range(n):
                                last = pe.matmul(p[i][:, t], w[i][:, k, :], x[:, k, t], start=(k == 0), stop=(k == n - 1))
                    last.then_inc(s_mm, 1)

        @block.scalar
        def _(act):
            for i in range(PAIRS):
                act.wait_ge(s_cen, i + 1)
                if i:
                    act.wait_ge(s_var, i)
                act.activation(sq[:, :], zs[:, i, :], ACT.Square).then_inc(s_sq, 1)
                act.wait_ge(s_vinv, i + 1)
                act.activation(rstd[:, :], rstd[:, :], ACT.Sqrt).then_inc(s_rstd, 1)
            with act.Fori(0, KT // 2) as q:
                for i in range(2):
                    act.wait_ge(s_mix, q * 2 + (i + 1))
                    act.dma_start(dram["mix"][:, :, ds(q * 2 + i, 1), :].rearrange("t p a c -> p t (a c)"),
                                  gr[i][:, :].rearrange("p (t c) -> p t c", c=P)).then_inc(s_out[i], 16)
            for i in range(2):
                act.wait_ge(s_out[i], 16 * (KT // 2))

        @block.vector
        def _(dve):
            link = Link(dve, s_dve)
            for i in range(PAIRS):
                y = zs[:, i, :]
                dve.wait_ge(s_mean, i + 1)
                dve.scalar_tensor_tensor(out=y, in0=pr[i % 2][:, :], scalar=-1.0 / HD, in1=y, op0=ALU.mult,
                                         op1=ALU.add).then_inc(s_cen, 1)
                dve.wait_ge(s_var, i + 1)
                link(dve.tensor_scalar(rstd[:, :], pc[i % 2][:, :], 1.0 / HD, GN_EPS, ALU.mult, ALU.add))
                dve.reciprocal(rstd[:, :], rstd[:, :]).then_inc(s_vinv, 1)
                dve.wait_ge(s_rstd, i + 1)
                link(dve.scalar_tensor_tensor(out=y, in0=y, scalar=vec[:, COL["lnx_g"] + i:COL["lnx_g"] + i + 1],
                                              in1=rstd[:, :], op0=ALU.mult, op1=ALU.mult))
                link(dve.scalar_tensor_tensor(out=y, in0=y, scalar=vec[:, COL["lnx_b"] + i:COL["lnx_b"] + i + 1],
                                              in1=bv[:, i, :], op0=ALU.add, op1=ALU.add))
                dve.tensor_tensor(y, y, gg[:, i, :], ALU.mult).then_inc(s_y, 1)
            dve.sem_inc(s_free, 2)
            with dve.Fori(0, KT // 2) as q:
                for i in range(2):
                    dve.wait_ge(s_mm, q * 2 + (i + 1))
                    dve.wait_ge(s_gr[i], q * 16 + 16)
                    dve.wait_ge(s_gc[i], q * 16 + 16)
                    dve.tensor_tensor(gr[i][:, :], gr[i][:, :], pr[i][:, :], ALU.mult).then_inc(s_mul, 1)
                    dve.tensor_tensor(gc[i][:, :], gc[i][:, :], pc[i][:, :], ALU.mult).then_inc(s_mul, 1)
                    dve.wait_ge(s_mul, q * 4 + (2 * i + 2))
                    dve.sem_inc(s_free, 1)
                    dve.tensor_tensor(gr[i][:, :], gr[i][:, :], gc[i][:, :], ALU.add).then_inc(s_mix, 1)



GRP = 8
GROUPS = NSEL // GRP
UR, VR, DR = 4, GRP, 4
SEG = GROUPS // 4
KS = TOPK // 2


def experts(nc, io, dram):
    with ExitStack() as ctx:
        def buf(name, shape, dt=F32):
            return ctx.enter_context(nc.sbuf_tensor(name, shape, dt))

        sem = ctx.enter_context(semaphores(nc))

        def psum(name, shape):
            return ctx.enter_context(nc.psum_tensor(name, shape, F32))

        ident, vec = buf("e_ident", [P, P]), buf("e_vec", [P, NVEC])
        w_out, w_q, w_ple = (buf(f"e_{n}", [P, KT, D]) for n in ("w_out", "w_q", "w_ple"))
        w_proj = buf("e_w_proj", [P, PLE // P, D])
        keys = buf("e_keys", [P, PH, NKEY])
        g_ffn, g_fin = buf("e_g_ffn", [P, D]), buf("e_g_fin", [P, D])
        mixt = buf("e_mix", [P, KT, P])
        qT = mixt
        xin = buf("e_x", [P, D])
        actT = buf("e_actT", [P, KT, P])
        c = buf("e_c", [P, D])
        hh, gt = buf("e_hh", [P, D]), buf("e_gt", [P, D])
        pt = buf("e_pt", [P, PLE // P, P])
        u = [buf(f"e_u{i}", [P, D]) for i in range(UR)]
        v = [buf(f"e_v{i}", [P, D]) for i in range(VR)]
        dg = [buf(f"e_dg{i}", [P, P]) for i in range(DR)]
        dots, gl, coef = buf("e_dots", [P, GRP]), buf("e_gelu", [P, GRP]), buf("e_coef", [P, GRP])
        zero = buf("e_zero", [P, HALF], mybir.dt.bfloat16)
        st = buf("e_stats", [P, 8])
        sc = [buf(f"e_sc{e}", [P, 2, NKEY]) for e in range(2)]
        sc2 = buf("e_sc2", [P, 2, NKEY])
        cand, cand2 = buf("e_cand", [P, TOPK, TOPK]), buf("e_cand2", [P, TOPK * TOPK])
        tv, ti = buf("e_tv", [P, 2, TOPK]), buf("e_ti", [P, 2, TOPK], U32)
        tb, tp = buf("e_tb", [P, TOPK]), buf("e_tp", [P, TOPK], U32)
        ix = buf("e_ix", [P, 2, PH, TOPK])
        best, pos = buf("e_best", [P, PH, TOPK]), buf("e_pos", [P, PH, TOPK], U32)
        half = buf("e_half", [P, PH, TOPK], U32)
        halff = buf("e_halff", [P, PH, TOPK])
        pick = buf("e_pick", [P, 2, PH, TOPK])
        iot, ioti = buf("e_iota", [P, TOPK]), buf("e_iotai", [P, TOPK], mybir.dt.int32)
        ex = buf("e_exp", [P, PH, TOPK])
        ssum = buf("e_ssum", [P, PH])
        gates_n, gates = buf("e_gates_next", [P, PH, TOPK]), buf("e_gates", [P, NSEL])
        idx_n, idx = buf("e_idx_next", [P, NSEL], U32), buf("e_idx", [P, NSEL], U32)
        stage = [buf(f"e_idx_group{e}", [P, GRP], U32) for e in range(2)]
        oh = gt

        pd = psum("e_pd", [P, D])
        acc = psum("e_acc", [P, D])
        ps = psum("e_ps", [P, 2, PH, NKEY])

        s_const, s_w, s_iota = sem("e_constants"), sem("e_weights_in"), sem("e_iota")
        s_ident = sem("e_identity_made")
        s_zero = sem("e_sum_cleared")
        s_mixin, s_xin = sem("e_mix_in"), sem("e_x_in")
        s_hps, s_h, s_hout = sem("e_h_in_psum"), sem("e_h_ready"), sem("e_h_out")
        s_sq, s_var, s_rstd = sem("e_h_squared"), sem("e_h_variance"), sem("e_h_rstd")
        s_hn, s_ctr, s_cT = sem("e_h_normed"), sem("e_c_turned"), sem("e_cT_ready")
        s_qps, s_qT, s_sc = sem("e_q_in_psum"), sem("e_qT_ready"), sem("e_scores_in_psum")
        s_head, s_topk = sem("e_head_copied"), sem("e_head_used")
        s_k = sem("e_topk_step")
        s_sub, s_exp, s_gn, s_in = sem("e_score_less_max"), sem("e_exp"), sem("e_gates_ready"), sem("e_indices_ready")
        s_fin = sem("e_select_step")
        s_icp, s_istage = sem("e_indices_copied"), sem("e_group_indices")
        s_pool = sem("e_gpsimd_waits_passed")
        s_dve = sem("e_vector_waits_passed")
        s_sp = sem("e_sync_waits_passed")
        s_cur = sem("e_tile_switched")
        s_u = [sem(f"e_u_in{i}") for i in range(UR)]
        s_v = [sem(f"e_v_in{i}") for i in range(VR)]
        s_dot, s_gelu, s_coef = sem("e_dot"), sem("e_gelu"), sem("e_coef")
        s_diag, s_vmm = sem("e_diag"), sem("e_v_added")
        s_hhin, s_hh, s_ptin = sem("e_tail_h_in"), sem("e_tail_h_ready"), sem("e_p_in")
        s_tsq, s_tvar, s_trstd = sem("e_tail_squared"), sem("e_tail_variance"), sem("e_tail_rstd")
        s_tn, s_ttr, s_tT = sem("e_tail_normed"), sem("e_tail_turned"), sem("e_tailT_ready")
        s_gps, s_gate = sem("e_gate_in_psum"), sem("e_gate_ready")
        s_pps, s_gp, s_h3 = sem("e_proj_in_psum"), sem("e_gated_proj"), sem("e_last_h")
        s_out, s_outd = sem("e_out_ready"), sem("e_out_stored")

        block = ctx.enter_context(nc.Block())

        @block.sync
        def _(sp):
            for dst, name in ((w_out, "w_out"), (w_q, "w_q"), (keys, "keys"), (w_ple, "w_ple"), (w_proj, "w_proj")):
                sp.dma_start(dst[:, :, :], io[name]).then_inc(s_w, 16)
            sp.dma_start(vec[:, :], io["vec"]).then_inc(s_w, 16)
            sp.dma_start(g_ffn[:, :], io["g_ffn"].to_broadcast([P, D])).then_inc(s_w, 16)
            sp.dma_start(g_fin[:, :], io["g_fin"].to_broadcast([P, D])).then_inc(s_w, 16)
            sp.dma_start(pt[:, :, :], io["pT"][NT - 1]).then_inc(s_ptin, 16)

            def after(semaphore, count):
                sp.wait_ge(semaphore, count)
                sp.sem_inc(s_sp, 1)

            def front_loads(n, tile):
                after(s_sc, n)
                sp.dma_start(mixt[:, :, :], one(dram["mix"], tile)).then_inc(s_mixin, 16)
                sp.dma_start(xin[:, :], one(io["x"], tile)).then_inc(s_xin, 16)

            def h_store(n, tile):
                after(s_h, n + 1)
                sp.dma_start(one(dram["h"], tile), xin[:, :]).then_inc(s_hout, 16)

            sp.dma_start(hh[:, :], io["x"][NT - 1]).then_inc(s_hhin, 16)
            front_loads(0, 0)
            h_store(0, 0)
            with sp.Fori(0, NT) as t:
                after(s_ttr, t + 1)
                front_loads(t + 1, (t + 1) & (NT - 1))
                after(s_pps, t + 1)
                sp.dma_start(pt[:, :, :], one(io["pT"], t)).then_inc(s_ptin, 16)
                after(s_out, t + 1)
                sp.dma_start(one(dram["out"], (t + (NT - 1)) & (NT - 1)), gt[:, :]).then_inc(s_outd, 16)
                after(s_hout, t * 16 + 16)
                sp.dma_start(hh[:, :], one(dram["h"], t)).then_inc(s_hhin, 16)
                h_store(t + 1, (t + 1) & (NT - 1))
            sp.wait_ge(s_out, NT + 1)
            sp.wait_ge(s_outd, 16 * NT)
            sp.dma_start(one(dram["out"], NT - 1), gt[:, :]).then_inc(s_outd, 16)
            sp.wait_ge(s_outd, 16 * (NT + 1))
            sp.wait_ge(s_hout, 16 * (NT + 1))

        @block.gpsimd
        def _(pool):
            pool.memset(zero[:, :], 0.0).then_inc(s_const, 1)
            pool.memset(ident[:, :], 0.0).then_inc(s_ident, 1)
            pool.wait_ge(s_ident, 1)
            pool.affine_select(out=ident[:, :], in_=ident[:, :], compare_op=ALU.not_equal, fill=1.0,
                               base=0, pattern=[[-1, P]], channel_multiplier=1).then_inc(s_ident, 1)
            pool.iota(ioti[:, :], [[1, TOPK]], base=0, channel_multiplier=0).then_inc(s_const, 1)
            pool.wait_ge(s_const, 2)
            pool.tensor_copy(iot[:, :], ioti[:, :]).then_inc(s_iota, 1)
            pool.sem_inc(s_istage, 1)
            with pool.Fori(0, NT) as t:
                pool.wait_ge(s_in, t + 1)
                pool.wait_ge(s_istage, t * GROUPS + 1)
                pool.sem_inc(s_pool, 1)
                pool.tensor_copy(idx[:, :], idx_n[:, :]).then_inc(s_icp, 1)
                with pool.Fori(0, GROUPS // 2) as pair:
                    for e in range(2):
                        n = t * GROUPS + pair * 2 + e
                        pool.wait_ge(s_icp, t + 1)
                        pool.sem_inc(s_pool, 1)
                        pool.tensor_copy(stage[e][:, :], idx[:, ds(pair * (2 * GRP) + e * GRP, GRP)]).then_inc(s_istage, 1)
                        pool.wait_ge(s_istage, n + 2)
                        for s in range(GRP):
                            pool.wait_ge(s_dot, n * GRP + (s + 1))
                            pool.sem_inc(s_pool, 1)
                            pool.indirect_dma_start(out=u[s % UR][:, :], out_offset=None, in_=io["u_tab"],
                                                    in_offset=bass.IndirectOffsetOnAxis(ap=stage[e][:, s:s + 1], axis=0))\
                                .then_inc(s_u[s % UR], 16)
                        for s in range(GRP):
                            pool.wait_ge(s_vmm, n * GRP + (s + 1))
                            pool.sem_inc(s_pool, 1)
                            pool.indirect_dma_start(out=v[s][:, :], out_offset=None, in_=io["v_tab"],
                                                    in_offset=bass.IndirectOffsetOnAxis(ap=stage[e][:, s:s + 1], axis=0))\
                                .then_inc(s_v[s], 16)

        @block.tensor
        def _(pe):
            def turned(src, n, s_src, s_dst):
                pe.wait_ge(s_src, n + 1)
                for k in range(KT):
                    last = pe.transpose(pd[:, k * P:(k + 1) * P], src[:, k * P:(k + 1) * P], ident[:, :])
                last.then_inc(s_dst, 1)

            def product(lhs, w, kt, s_dst):
                for h in range(D // HALF):
                    for k in range(kt):
                        last = pe.matmul(pd[:, h * HALF:(h + 1) * HALF], lhs[:, k, :], w[:, k, h * HALF:(h + 1) * HALF],
                                         start=(k == 0), stop=(k == kt - 1))
                last.then_inc(s_dst, 1)

            def front_h(n, tails):
                pe.wait_ge(s_mixin, n * 16 + 16)
                pe.wait_ge(s_gp, tails)
                product(mixt, w_out, KT, s_hps)
                turned(xin, n, s_hn, s_ctr)

            def front_q(n):
                pe.wait_ge(s_cT, n + 1)
                for h in range(PH):
                    for k in range(KT):
                        last = pe.matmul(pd[:, h * P:(h + 1) * P], w_q[:, k, h * P:(h + 1) * P], actT[:, k, :],
                                         start=(k == 0), stop=(k == KT - 1))
                last.then_inc(s_qps, 1)
                pe.wait_ge(s_qT, n + 1)
                pe.wait_ge(s_head, n * PH)
                for p in range(2):
                    r = slice(p * PHALF, (p + 1) * PHALF)
                    for h in range(PH):
                        last = pe.matmul(ps[:, p, h, :], qT[r, h, :], keys[r, h, :], start=True, stop=True)
                last.then_inc(s_sc, 1)

            def tail(n):
                pe.wait_ge(s_qT, n + 1)
                turned(xin, n, s_tn, s_ttr)
                pe.wait_ge(s_tT, n + 1)
                product(actT, w_ple, KT, s_gps)
                pe.wait_ge(s_ptin, n * 16 + 16)
                pe.wait_ge(s_gate, n + 1)
                product(pt, w_proj, PLE // P, s_pps)

            def group(n):
                for s in range(GRP):
                    pe.wait_ge(s_diag, n * GRP + (s + 2))
                    pe.wait_ge(s_v[s], n * 16 + 16)
                    for h in range(D // HALF):
                        cols = slice(h * HALF, (h + 1) * HALF)
                        last = pe.matmul(acc[:, cols], dg[s % DR][:, :], v[s][:, cols], start=False, stop=False,
                                         skip_group_check=True)
                    last.then_inc(s_vmm, 1)

            def clear(n):
                for h in range(D // HALF):
                    last = pe.matmul(acc[:, h * HALF:(h + 1) * HALF], zero[:, 0:P], zero[:, :], start=True, stop=False,
                                     skip_group_check=True)
                last.then_inc(s_zero, 1)

            pe.sem_inc(s_vmm, VR)
            pe.wait_ge(s_w, 16 * 8)
            pe.wait_ge(s_const, 2)
            pe.wait_ge(s_ident, 2)
            clear(0)
            front_h(0, 0)
            front_q(0)
            with pe.Fori(0, NT) as t:
                pe.wait_ge(s_hh, t + 1)
                clear(t + 1)
                tail(t)
                for seg in range(4):
                    with pe.Fori(seg * SEG, (seg + 1) * SEG) as g:
                        group(t * GROUPS + g)
                    if seg == 0:
                        front_h(t + 1, t + 1)
                    if seg == 1:
                        front_q(t + 1)
            tail(NT)

        @block.scalar
        def _(act):
            def rms(n, src, scratch, col, s_src, s_sq, s_var, s_rstd, use):
                act.wait_ge(s_src, n + 1)
                act.activation(scratch[:, :], src[:, :], ACT.Square, accum_out=st[:, col:col + 1]).then_inc(s_sq, 1)
                act.wait_ge(s_var, use)
                act.activation(st[:, col + 1:col + 2], st[:, col + 1:col + 2], ACT.Sqrt).then_inc(s_rstd, 1)

            def front_h(n):
                rms(n, xin, gt, 0, s_h, s_sq, s_var, s_rstd, n + 1)
                act.wait_ge(s_ctr, n + 1)
                for k in range(KT):
                    last = act.activation(actT[:, k, :], pd[:, k * P:(k + 1) * P], ACT.Copy,
                                          scale=vec[:, COL["ffn_g"] + k:COL["ffn_g"] + k + 1])
                last.then_inc(s_cT, 1)

            def front_q(n):
                act.wait_ge(s_qps, n + 1)
                act.activation(qT[:, :, :].rearrange("p h t -> p (h t)"), pd[:, :], ACT.Copy).then_inc(s_qT, 1)

            def heads(n, j):
                act.wait_ge(s_sc, n + 1)
                for e in range(2):
                    act.wait_ge(s_topk, n * PH + j * 2 + (e + 1))
                    act.activation(sc[e][:, :, :].unsqueeze(2), ps[:, :, ds(j * 2 + e, 1), :], ACT.Copy).then_inc(s_head, 1)

            def gate_exp(n):
                act.wait_ge(s_sub, n + 1)
                act.activation(ex[:, :, :], ex[:, :, :], ACT.Exp).then_inc(s_exp, 1)

            def tail(n):
                rms(n, hh, gt, 2, s_hh, s_tsq, s_tvar, s_trstd, n * 2 + 1)
                act.wait_ge(s_gps, n + 1)
                act.activation(gt[:, :], pd[:, :], ACT.Sigmoid).then_inc(s_gate, 1)
                act.wait_ge(s_h3, n + 1)
                act.activation(gt[:, :], hh[:, :], ACT.Square, accum_out=st[:, 4:5]).then_inc(s_tsq, 1)
                act.wait_ge(s_tvar, n * 2 + 2)
                act.activation(st[:, 5:6], st[:, 5:6], ACT.Sqrt).then_inc(s_trstd, 1)

            def group(n):
                act.wait_ge(s_dot, n * GRP + (GRP + UR))
                act.activation(gl[:, :], dots[:, :], ACT.Gelu).then_inc(s_gelu, 1)
                act.wait_ge(s_coef, n + 1)
                for s in range(GRP):
                    act.wait_ge(s_vmm, n * GRP + (s + 1 + VR - DR))
                    act.activation(dg[s % DR][:, :], ident[:, :], ACT.Copy, scale=coef[:, s:s + 1]).then_inc(s_diag, 1)

            act.wait_ge(s_w, 16 * 8)
            act.wait_ge(s_ident, 2)
            act.sem_inc(s_gelu, 1)
            act.sem_inc(s_diag, 1)
            front_h(0)
            front_q(0)
            with act.Fori(0, PH // 2) as j:
                heads(0, j)
            gate_exp(0)
            with act.Fori(0, NT) as t:
                tail(t)
                for seg in range(4):
                    with act.Fori(seg * SEG, (seg + 1) * SEG) as g:
                        if seg == 2:
                            heads(t + 1, g - 2 * SEG)
                        group(t * GROUPS + g)
                    if seg == 0:
                        act.wait_ge(s_outd, t * 16 + 16)
                        front_h(t + 1)
                    if seg == 1:
                        front_q(t + 1)
                    if seg == 2:
                        gate_exp(t + 1)
            act.wait_ge(s_outd, NT * 16)
            tail(NT)

        @block.vector
        def _(dve):
            def variance(n, col, s_sq, use, s_var, s_own):
                dve.wait_ge(s_sq, use)
                dve.tensor_scalar(st[:, col + 1:col + 2], st[:, col:col + 1], 1.0 / D, RMS_EPS, ALU.mult, ALU.add).then_inc(s_own[0], 1)
                dve.wait_ge(s_own[0], s_own[1])
                dve.reciprocal(st[:, col + 1:col + 2], st[:, col + 1:col + 2]).then_inc(s_var, 1)

            def pinned():
                dve.sem_inc(s_dve, 1)

            def front_h(n):
                dve.wait_ge(s_hps, n + 1)
                dve.wait_ge(s_xin, n * 16 + 16)
                dve.tensor_tensor(xin[:, :], pd[:, :], xin[:, :], ALU.add).then_inc(s_h, 1)
                variance(n, 0, s_sq, n + 1, s_var, (s_fv, n + 1))
                dve.wait_ge(s_rstd, n + 1)
                dve.wait_ge(s_hout, n * 16 + 16)
                dve.tensor_scalar(xin[:, :], xin[:, :], st[:, 1:2], None, ALU.mult).then_inc(s_hn, 1)

            def head(n, j, e):
                link = Link(dve, s_k, n * (PH // 2) + j, 2 * HEAD_STEPS, start=e * HEAD_STEPS)

                def step(ins):
                    link(ins)
                    pinned()

                dve.wait_ge(s_head, n * PH + j * 2 + (e + 1))
                pinned()
                for p in range(2):
                    link.mark(dve.max(tv[:, p, 0:KS], sc[e][:, p, :]))
                link.wait()
                pinned()
                for p in range(2):
                    link.mark(dve.max_index(ti[:, p, 0:KS], tv[:, p, 0:KS], sc[e][:, p, :]))
                    link.mark(dve.match_replace(sc2[:, p, :], tv[:, p, 0:KS], sc[e][:, p, :], LOWEST))
                link.wait()
                pinned()
                for p in range(2):
                    link.mark(dve.max(tv[:, p, KS:], sc2[:, p, :]))
                link.wait()
                pinned()
                for p in range(2):
                    link.mark(dve.max_index(ti[:, p, KS:], tv[:, p, KS:], sc2[:, p, :]))
                link.mark(dve.tensor_tensor(cand[:, :, :], tv[:, 0, :].unsqueeze(2).to_broadcast([P, TOPK, TOPK]),
                                            tv[:, 1, :].unsqueeze(1).to_broadcast([P, TOPK, TOPK]), ALU.add))
                link.wait()
                dve.tensor_copy(ix[:, :, ds(j * 2 + e, 1), :], ti[:, :, :].unsqueeze(2)).then_inc(s_ix, 1)
                flat = cand[:, :, :].rearrange("p a b -> p (a b)")
                pinned()
                step(dve.max(tb[:, 0:KS], flat))
                link.mark(dve.max_index(tp[:, 0:KS], tb[:, 0:KS], flat))
                step(dve.match_replace(cand2[:, :], tb[:, 0:KS], flat, LOWEST))
                step(dve.max(tb[:, KS:], cand2[:, :]))
                link(dve.max_index(tp[:, KS:], tb[:, KS:], cand2[:, :]))
                link.mark(dve.tensor_copy(best[:, ds(j * 2 + e, 1), :], tb[:, :].unsqueeze(1)))
                link(dve.tensor_copy(pos[:, ds(j * 2 + e, 1), :], tp[:, :].unsqueeze(1)))
                dve.wait_ge(s_ix, n * PH + j * 2 + (e + 1))
                dve.sem_inc(s_topk, 1)
                assert link.k == HEAD_STEPS, link.k

            def select(n):
                link = Link(dve, s_fin, n, SELECT_STEPS)
                dve.tensor_tensor(ex[:, :, :], best[:, :, :], best[:, :, 0:1].to_broadcast([P, PH, TOPK]), ALU.subtract)\
                    .then_inc(s_sub, 1)
                dve.wait_ge(s_outd, n * 16)
                for p in range(2):
                    op, by = ((ALU.logical_shift_right, 4), (ALU.bitwise_and, TOPK - 1))[p]
                    link(dve.tensor_scalar(half[:, :, :], pos[:, :, :], by, None, op))
                    link(dve.tensor_copy(halff[:, :, :], half[:, :, :]))
                    for q in range(2):
                        hs = slice(q * (PH // 2), (q + 1) * (PH // 2))
                        rows = oh[:, :].rearrange("p (h j c) -> p h j c", h=PH // 2, j=TOPK)
                        shape = [P, PH // 2, TOPK, TOPK]
                        link(dve.tensor_tensor(rows, halff[:, hs, :].unsqueeze(3).to_broadcast(shape),
                                               iot[:, :].unsqueeze(1).unsqueeze(1).to_broadcast(shape), ALU.is_equal))
                        link(dve.tensor_tensor(rows, rows, ix[:, p, hs, :].unsqueeze(2).to_broadcast(shape), ALU.mult))
                        link(dve.tensor_reduce(pick[:, p, hs, :], rows, AX.X, ALU.add))
                dve.wait_ge(s_icp, n)
                dve.scalar_tensor_tensor(out=idx_n[:, :], in0=pick[:, 0, :, :].rearrange("p h j -> p (h j)"),
                                         scalar=float(NKEY), in1=pick[:, 1, :, :].rearrange("p h j -> p (h j)"),
                                         op0=ALU.mult, op1=ALU.add).then_inc(s_in, 1)
                dve.wait_ge(s_exp, n + 1)
                link(dve.tensor_reduce(ssum[:, :], ex[:, :, :], AX.X, ALU.add))
                link(dve.reciprocal(ssum[:, :], ssum[:, :]))
                dve.tensor_tensor(gates_n[:, :, :], ex[:, :, :], ssum[:, :].unsqueeze(2).to_broadcast([P, PH, TOPK]),
                                  ALU.mult).then_inc(s_gn, 1)
                assert link.k == SELECT_STEPS, link.k

            def switch(n):
                dve.wait_ge(s_hn, n + 1)
                dve.wait_ge(s_ctr, n + 1)
                dve.tensor_tensor(c[:, :], xin[:, :], g_ffn[:, :], ALU.mult).then_inc(s_cur, 1)
                dve.wait_ge(s_gn, n + 1)
                dve.tensor_copy(gates[:, :], gates_n[:, :, :].rearrange("p h j -> p (h j)")).then_inc(s_cur, 1)

            def sum_read(n, adds):
                dve.wait_ge(s_hhin, n * 16 + 16)
                dve.wait_ge(s_vmm, adds)
                dve.wait_ge(s_zero, n + 1)
                dve.tensor_tensor(hh[:, :], hh[:, :], acc[:, :], ALU.add).then_inc(s_hh, 1)

            def tail(n, switches):
                variance(n, 2, s_tsq, n * 2 + 1, s_tvar, (s_tv, n * 2 + 1))
                dve.wait_ge(s_trstd, n * 2 + 1)
                dve.wait_ge(s_cur, switches * 2)
                dve.tensor_scalar(xin[:, :], hh[:, :], st[:, 3:4], None, ALU.mult).then_inc(s_tn, 1)
                dve.wait_ge(s_ttr, n + 1)
                dve.tensor_tensor(actT[:, :, :], pd[:, :].rearrange("p (k c) -> p k c", k=KT),
                                  bcast(vec[:, COL["ple_g"]:COL["ple_g"] + KT], 2, P), ALU.mult).then_inc(s_tT, 1)
                dve.wait_ge(s_pps, n + 1)
                dve.wait_ge(s_gate, n + 1)
                dve.tensor_tensor(gt[:, :], gt[:, :], pd[:, :], ALU.mult).then_inc(s_gp, 1)
                dve.wait_ge(s_gp, n + 1)
                dve.tensor_tensor(hh[:, :], hh[:, :], gt[:, :], ALU.add).then_inc(s_h3, 1)
                variance(n, 4, s_tsq, n * 2 + 2, s_tvar, (s_tv, n * 2 + 2))
                dve.wait_ge(s_trstd, n * 2 + 2)
                dve.scalar_tensor_tensor(out=gt[:, :], in0=hh[:, :], scalar=st[:, 5:6], in1=g_fin[:, :],
                                         op0=ALU.mult, op1=ALU.mult).then_inc(s_out, 1)

            def group(n, between=None):
                dve.wait_ge(s_gelu, n + 1)
                for s in range(GRP):
                    dve.wait_ge(s_u[s % UR], n * (16 * GRP // UR) + 16 * (s // UR + 1))
                    if s == 0:
                        pinned()
                    dve.tensor_tensor_reduce(u[s % UR][:, :], u[s % UR][:, :], c[:, :], 1.0, 0.0, ALU.mult, ALU.add,
                                             dots[:, s:s + 1]).then_inc(s_dot, 1)
                    if between and s % (GRP // 2) == 1:
                        between(s // (GRP // 2))
                dve.wait_ge(s_gelu, n + 2)
                dve.wait_ge(s_diag, n * GRP + 1)

            s_fv, s_tv, s_ix = sem("e_h_mean_square"), sem("e_tail_mean_square"), sem("e_half_indices")

            def coefs(n, g):
                dve.tensor_tensor(coef[:, :], gl[:, :], gates[:, ds(g * GRP, GRP)], ALU.mult).then_inc(s_coef, 1)

            dve.sem_inc(s_dot, UR)
            dve.sem_inc(s_topk, 2)
            dve.wait_ge(s_w, 16 * 8)
            dve.wait_ge(s_const, 2)
            dve.wait_ge(s_iota, 1)
            front_h(0)
            with dve.Fori(0, PH // 2) as j:
                for e in range(2):
                    head(0, j, e)
            select(0)
            with dve.Fori(0, NT) as t:
                sum_read(t, t * NSEL + VR)
                switch(t)
                tail(t, t + 1)
                for seg in range(4):
                    with dve.Fori(seg * SEG, (seg + 1) * SEG) as g:
                        n = t * GROUPS + g
                        group(n, (lambda e: head(t + 1, g - 2 * SEG, e)) if seg == 2 else None)
                        coefs(n, g)
                    if seg == 0:
                        front_h(t + 1)
                    if seg == 2:
                        select(t + 1)
            sum_read(NT, NT * NSEL + VR)
            tail(NT, NT)


HEAD_STEPS = 18
SELECT_STEPS = 18


FROM_PROJECTION = dict(ident=[P, P], vec=[P, NVEC], cw=[P, TAPS * CONV_TILES], zs=[P, RWKV_TILES, T],
                       cv=[P, CONV_TILES, T])
FROM_PREPARATION = dict(qq=[P, PAIRS, T], bb=[P, PAIRS, T], gg=[P, PAIRS, T], bv=[P, PAIRS, T],
                        pc=[P, PAIRS, NC], headones=[P, P])


def program(nc, io, out):
    dram = {"gates": nc.dram_tensor("mixer_gates", (GATE_TILES, P, T), F32).ap(),
            "mix": nc.dram_tensor("mixed", (NT, P, KT, P), F32).ap(),
            "h": nc.dram_tensor("h_after_mixer", (NT, P, D), F32).ap(),
            "out": out}
    with ExitStack() as ctx:
        sb = {name: ctx.enter_context(nc.sbuf_tensor(name, shape, F32)) for name, shape in FROM_PROJECTION.items()}
        project_in(nc, io, sb, dram)
        for name, shape in FROM_PREPARATION.items():
            sb[name] = ctx.enter_context(nc.sbuf_tensor(name, shape, F32))
        prepare_recurrence(nc, io, sb)
        recurrence(nc, io, sb)
        mix(nc, io, sb, dram)
    experts(nc, io, dram)


VEC_INPUTS = dict(mu="rwkv_mu", w0="rwkv_w0", a0="rwkv_a0", k_k="rwkv_k_k", k_a="rwkv_k_a", r_k="rwkv_r_k",
                  lnx_g="rwkv_lnx_g", lnx_b="rwkv_lnx_b", dw_b="conv_dw_b", ln_g="conv_ln_g", ln_b="conv_ln_b",
                  mix_g="norm_mix_g", ffn_g="norm_ffn_g", ple_g="ple_norm_g")


def column_tiles(w):
    k, n = w.shape
    return w.reshape(k // P, P, n // P, P).transpose(2, 1, 0, 3)


def row_tiles(w):
    k, n = w.shape
    return w.reshape(k // P, P, n).transpose(1, 0, 2)


def layout(a):
    vec = np.concatenate([a[VEC_INPUTS[name]][0].reshape(-1, P) for name, _ in VECS]).T
    return {
        "x": a["x"][0].reshape(NT, P, D),
        "xT": a["x"][0].T.reshape(KT, P, T),
        "w_in": column_tiles(a["w_in"][0]),
        "vec": vec,
        "dw_w": a["conv_dw_w"][0].reshape(-1, P).T,
        "wa_up": np.concatenate([a["rwkv_w_up"][0], a["rwkv_a_up"][0]], 0),
        "g_up": a["rwkv_g_up"][0],
        "w_r": column_tiles(a["rwkv_w_o"][0]),
        "w_c": column_tiles(a["conv_w_o"][0]),
        "w_out": row_tiles(a["w_out"][0]),
        "w_q": row_tiles(a["peer_w_q"][0]),
        "w_ple": row_tiles(a["ple_w_gate"][0]),
        "w_proj": row_tiles(a["ple_w_proj"][0]),
        "keys": a["peer_sub_keys"][0].transpose(1, 3, 0, 2).reshape(P, PH, NKEY),
        "g_ffn": a["norm_ffn_g"],
        "g_fin": a["final_norm_g"][None],
        "pT": a["p"][0, 0].reshape(NT, P, PLE // P, P).transpose(0, 3, 2, 1),
        "u_tab": a["peer_u"][0],
        "v_tab": a["peer_v"][0],
    }


def kernel(**inputs):
    import concourse.bacc as _bacc
    from concourse.bass_utils import run_bass_kernel_spmd as _run

    nc = _bacc.Bacc("TRN2", target_bir_lowering=False, num_devices=1)
    arrays, io = {}, {}
    for name, a in layout({name: np.asarray(a) for name, a in inputs.items()}).items():
        a = np.ascontiguousarray(a)
        arrays[f"in_{name}"] = a
        io[name] = nc.dram_tensor(f"in_{name}", a.shape, mybir.dt.from_np(a.dtype), kind="ExternalInput").ap()
    out = nc.dram_tensor("out_0", (1, T, D), F32, kind="ExternalOutput").ap()
    program(nc, io, out.rearrange("a (n p) d -> (a n) p d", p=P))
    result = _run(nc, [arrays], core_ids=[0])
    return result.results[0]["out_0"]
```

```python
from contextlib import ExitStack, contextmanager

import numpy as np

import concourse.bass as bass
from concourse import mybir

F32 = mybir.dt.float32
U32 = mybir.dt.uint32
ALU = mybir.AluOpType
ACT = mybir.ActivationFunctionType
AX = mybir.AxisListType

P = 128
D = 1024
T = 1024
KT = D // P
NT = T // P
HALF = 512
NH = T // HALF

HEADS, HD = 8, 64
RW = HEADS * HD
PAIRS = RW // P
RWKV_TILES = (3 * RW + 64 + 64 + 128) // P
RWKV_COLS = RWKV_TILES * P
CONV_W = 512
CONV_TILES = CONV_W // P
TAPS = 31
PADT = TAPS - 1
GATE_TILES = 2 * D // P
GN_EPS, LN_EPS, RMS_EPS = 64e-5, 1e-5, 1e-6
CH = 64
NC = T // CH
DECAY = float(np.exp(-0.5))

PH, NKEY, PHALF, TOPK = 8, 128, 64, 16
NSEL = PH * TOPK
NEXP = NKEY * NKEY
PLE = 256
LOWEST = -3.0e38

VECS = [("mu", RWKV_TILES), ("w0", PAIRS), ("a0", PAIRS), ("k_k", PAIRS), ("k_a", PAIRS),
        ("r_k", PAIRS), ("lnx_g", PAIRS), ("lnx_b", PAIRS), ("dw_b", CONV_TILES),
        ("ln_g", CONV_TILES), ("ln_b", CONV_TILES), ("mix_g", KT), ("ffn_g", KT), ("ple_g", KT)]
COL, _n = {}, 0
for _name, _rows in VECS:
    COL[_name] = _n
    _n += _rows
NVEC = _n


def ds(start, size):
    return bass.ds(start, size)


def at(tile, i):
    return tile[:, ds(i, 1), :].rearrange("p a t -> p (a t)")


def one(tensor, i):
    if isinstance(i, int):
        return tensor[i]
    axes = "abcd"[:len(tensor.shape) - 1]
    return tensor[ds(i, 1)].rearrange(f"i {' '.join(axes)} -> (i {axes[0]}) {' '.join(axes[1:])}")


def col(tile, i):
    return tile[:, ds(i, 1)]


@contextmanager
def semaphores(nc):
    taken = []

    def sem(name):
        taken.append(nc.alloc_semaphore(name))
        return taken[-1]

    yield sem
    nc.clear_and_free_semaphores(taken)
    nc.all_engine_barrier()


class Link:

    def __init__(self, eng, sem, turn=0, each=0, start=0):
        self.eng, self.sem, self.turn, self.each, self.start, self.k = eng, sem, turn, each, start, 0

    def value(self, k):
        return self.turn * self.each + (self.start + k) if self.each else self.start + k

    def mark(self, ins):
        self.k += 1
        ins.then_inc(self.sem, 1)
        return self.k

    def wait(self, k=None):
        self.eng.wait_ge(self.sem, self.value(self.k if k is None else k))

    def __call__(self, ins):
        self.mark(ins)
        self.wait()


def bcast(ap, axis, n):
    return ap.unsqueeze(axis).to_broadcast([*ap.shape[:axis], n, *ap.shape[axis:]])


def project_in(nc, io, sb, dram):
    with ExitStack() as ctx:
        def buf(name, shape, dt=F32):
            return ctx.enter_context(nc.sbuf_tensor(name, shape, dt))

        sem = ctx.enter_context(semaphores(nc))

        ident, vec, cw, zs, cv = sb["ident"], sb["vec"], sb["cw"], sb["zs"], sb["cv"]
        ones = buf("a_ones", [P, P])
        sq = buf("a_sq", [P, 2, T])
        rstd = buf("a_rstd", [P, T])
        aT = buf("a_aT", [P, KT, T])
        w = [buf(f"a_w{i}", [P, KT, P]) for i in range(4)]
        zp = [buf(f"a_zp{i}", [P, T + 1]) for i in range(2)]
        dz = [buf(f"a_dz{i}", [P, T]) for i in range(2)]
        cg = buf("a_cg", [P, T])
        hp = buf("a_hp", [P, CONV_TILES, PADT + T])
        gt = [buf(f"a_gt{i}", [P, T]) for i in range(2)]
        ps = [ctx.enter_context(nc.psum_tensor(f"a_ps{i}", [P, T], F32)) for i in range(4)]

        s_ident = sem("a_identity_made")
        s_ones = sem("a_ones_made")
        s_vec = sem("a_constants_in")
        s_x = [sem(f"a_x_in{i}") for i in range(KT)]
        s_sq = sem("a_x_squared")
        s_sum = sem("a_squares_summed")
        s_var = sem("a_variance_inverted")
        s_rstd = sem("a_rstd_ready")
        s_aT = sem("a_aT_ready")
        s_w = [sem(f"a_w_in{i}") for i in range(4)]
        s_mm = sem("a_z_tile_in_psum")
        s_free = [sem(f"a_psum_tile_free{i}") for i in range(4)]
        s_pad = sem("a_pads_zeroed")
        s_zcp = sem("a_z_tile_copied")
        s_dz = sem("a_z_difference_ready")
        s_zs = sem("a_z_shifted")
        s_sig = sem("a_conv_gate_ready")
        s_h = sem("a_conv_input_ready")
        s_tap = sem("a_conv_tap_done")
        s_dve = sem("a_vector_step")
        s_act = sem("a_scalar_step")
        s_gate = sem("a_mixer_gate_ready")
        s_gout = [sem(f"a_mixer_gate_out{i}") for i in range(2)]

        TILES = RWKV_TILES + 2 * CONV_TILES + GATE_TILES
        cols = [m * P for m in range(RWKV_TILES)]
        for i in range(CONV_TILES):
            cols += [RWKV_COLS + i * P, RWKV_COLS + CONV_W + i * P]
        gates_at = RWKV_COLS + 2 * CONV_W
        win = io["w_in"]
        block = ctx.enter_context(nc.Block())

        @block.gpsimd
        def _(pool):
            pool.memset(ident[:, :], 0.0).then_inc(s_ident, 1)
            pool.memset(ones[:, :], 1.0).then_inc(s_ones, 1)
            for i in range(2):
                pool.memset(zp[i][:, 0:1], 0.0).then_inc(s_pad, 1)
            pool.memset(hp[:, :, 0:PADT], 0.0).then_inc(s_pad, 1)
            pool.wait_ge(s_ident, 1)
            pool.affine_select(out=ident[:, :], in_=ident[:, :], compare_op=ALU.not_equal, fill=1.0,
                               base=0, pattern=[[-1, P]], channel_multiplier=1).then_inc(s_ident, 1)

        @block.sync
        def _(sp):
            for k in range(KT):
                sp.dma_start(aT[:, k, :], io["xT"][k]).then_inc(s_x[k], 16)
            sp.dma_start(vec[:, :], io["vec"]).then_inc(s_vec, 16)
            sp.dma_start(cw[:, :], io["dw_w"]).then_inc(s_vec, 16)
            for m in range(4):
                sp.dma_start(w[m][:, :, :], win[cols[m] // P]).then_inc(s_w[m], 16)
            for m in range(4, len(cols)):
                sp.wait_ge(s_mm, m - 3)
                sp.dma_start(w[m % 4][:, :, :], win[cols[m] // P]).then_inc(s_w[m % 4], 16)
            first = len(cols)
            with sp.Fori(0, GATE_TILES // 4) as q:
                for i in range(4):
                    slot = (first + i) % 4
                    sp.wait_ge(s_mm, q * 4 + (first + i - 3))
                    sp.dma_start(w[slot][:, :, :], win[ds(q * 4 + (gates_at // P + i), 1)].rearrange("a p k c -> (a p) k c"))\
                        .then_inc(s_w[slot], 16)

        @block.tensor
        def _(pe):
            pe.wait_ge(s_ones, 1)
            for k in range(KT):
                pe.wait_ge(s_sq, k + 1)
                for h in range(NH):
                    last = pe.matmul(ps[0][:, h * HALF:(h + 1) * HALF], ones[:, :], sq[:, k % 2, h * HALF:(h + 1) * HALF],
                                     start=(k == 0), stop=(k == KT - 1))
                last.then_inc(s_sum, 1)
            pe.wait_ge(s_aT, KT)

            def z_tile(m, q):
                pe.wait_ge(s_w[m % 4], q * 16 + 16 * (m // 4 + 1))
                pe.wait_ge(s_free[m % 4], q + (m // 4 + 1))
                for h in range(NH):
                    for k in range(KT):
                        last = pe.matmul(ps[m % 4][:, h * HALF:(h + 1) * HALF], w[m % 4][:, k, :],
                                         aT[:, k, h * HALF:(h + 1) * HALF], start=(k == 0), stop=(k == KT - 1))
                last.then_inc(s_mm, 1)

            with pe.Fori(0, TILES // 4) as q:
                for m in range(4):
                    z_tile(m, q)
            for m in range(TILES // 4 * 4, TILES):
                z_tile(m, 0)

        @block.scalar
        def _(act):
            for i in range(4):
                act.sem_inc(s_free[i], 1)
            for k in range(KT):
                act.wait_ge(s_x[k], 16)
                if k >= 2:
                    act.wait_ge(s_sum, k - 1)
                act.activation(sq[:, k % 2, :], aT[:, k, :], ACT.Square).then_inc(s_sq, 1)
            act.wait_ge(s_var, 1)
            act.activation(rstd[:, :], rstd[:, :], ACT.Sqrt).then_inc(s_rstd, 1)

            def z_copy(q, m):
                act.wait_ge(s_mm, q * 4 + (m + 1))
                act.wait_ge(s_dz, q * 4 + (m + 1))
                act.activation(zp[m % 2][:, 1:T + 1], ps[m % 4][:, :], ACT.Copy).then_inc(s_zcp, 1)
                act.wait_ge(s_zcp, q * 4 + (m + 1))
                act.sem_inc(s_free[m % 4], 1)

            with act.Fori(0, RWKV_TILES // 4) as q:
                for m in range(4):
                    z_copy(q, m)
            for m in range(RWKV_TILES // 4 * 4, RWKV_TILES):
                z_copy(0, m)
            for i in range(CONV_TILES):
                m = RWKV_TILES + 2 * i
                act.wait_ge(s_mm, m + 2)
                if i:
                    act.wait_ge(s_h, i)
                act.activation(cg[:, :], ps[(m + 1) % 4][:, :], ACT.Sigmoid).then_inc(s_sig, 1)
            first = RWKV_TILES + 2 * CONV_TILES
            with act.Fori(0, GATE_TILES // 4) as q:
                for i in range(4):
                    m = first + i
                    act.wait_ge(s_mm, q * 4 + (m + 1))
                    act.wait_ge(s_gout[i % 2], q * 32 + 16 * (i // 2 + 1))
                    act.activation(gt[i % 2][:, :], ps[m % 4][:, :], ACT.Sigmoid).then_inc(s_gate, 1)
                    act.wait_ge(s_gate, q * 4 + (i + 1))
                    act.sem_inc(s_free[m % 4], 1)
                    act.dma_start(dram["gates"][ds(q * 4 + i, 1), :, :].rearrange("a p t -> (a p) t"),
                                  gt[i % 2][:, :]).then_inc(s_gout[i % 2], 16)
            for i in range(2):
                act.wait_ge(s_gout[i], 16 * (GATE_TILES // 2 + 1))

        @block.vector
        def _(dve):
            dve.sem_inc(s_dz, 2)
            for i in range(2):
                dve.sem_inc(s_gout[i], 16)
            link = Link(dve, s_dve)
            dve.wait_ge(s_sum, KT)
            link(dve.tensor_scalar(rstd[:, :], ps[0][:, :], 1.0 / D, RMS_EPS, ALU.mult, ALU.add))
            link(dve.reciprocal(rstd[:, :], rstd[:, :]))
            dve.sem_inc(s_var, 1)
            dve.wait_ge(s_rstd, 1)
            dve.wait_ge(s_vec, 32)
            for k in range(KT):
                g = vec[:, COL["mix_g"] + k:COL["mix_g"] + k + 1]
                dve.scalar_tensor_tensor(out=aT[:, k, :], in0=aT[:, k, :], scalar=g, in1=rstd[:, :],
                                         op0=ALU.mult, op1=ALU.mult).then_inc(s_aT, 1)

            def z_shift(q, m):
                dve.wait_ge(s_zcp, q * 4 + (m + 1))
                a = dz[m % 2]
                dve.tensor_tensor(a[:, :], zp[m % 2][:, 0:T], zp[m % 2][:, 1:T + 1], ALU.subtract).then_inc(s_tap, 1)
                dve.wait_ge(s_tap, q * 4 + (m + 1))
                dve.scalar_tensor_tensor(out=at(zs, q * 4 + m),
                                         in0=a[:, :],
                                         scalar=col(vec, q * 4 + (COL["mu"] + m)),
                                         in1=zp[m % 2][:, 1:T + 1], op0=ALU.mult, op1=ALU.add).then_inc(s_dz, 1)

            dve.wait_ge(s_pad, 3)
            with dve.Fori(0, RWKV_TILES // 4) as q:
                for m in range(4):
                    z_shift(q, m)
                    dve.wait_ge(s_dz, q * 4 + (m + 3))
            for m in range(RWKV_TILES // 4 * 4, RWKV_TILES):
                z_shift(0, m)
                dve.wait_ge(s_dz, m + 3)
            for i in range(CONV_TILES):
                m = RWKV_TILES + 2 * i
                dve.wait_ge(s_sig, i + 1)
                dve.tensor_tensor(hp[:, i, PADT:PADT + T], ps[m % 4][:, :], cg[:, :], ALU.mult).then_inc(s_h, 1)
                dve.wait_ge(s_h, i + 1)
                for k in range(2):
                    dve.sem_inc(s_free[(m + k) % 4], 1)
            taps = RWKV_TILES
            with dve.Fori(0, CONV_TILES) as i:
                link = Link(dve, s_tap, i, TAPS, start=taps)

                def tap(j):
                    return col(cw, i + j * CONV_TILES)

                hin = at(hp, i)
                acc = at(cv, i)
                link(dve.tensor_scalar(acc, hin[:, 0:T], tap(0), col(vec, i + COL["dw_b"]), ALU.mult, ALU.add))
                for j in range(1, TAPS):
                    link(dve.scalar_tensor_tensor(out=acc, in0=hin[:, j:j + T], scalar=tap(j), in1=acc,
                                                  op0=ALU.mult, op1=ALU.add))




def prepare_recurrence(nc, io, sb):
    with ExitStack() as ctx:
        def buf(name, shape, dt=F32):
            return ctx.enter_context(nc.sbuf_tensor(name, shape, dt))

        sem = ctx.enter_context(semaphores(nc))

        vec, zs, cv = sb["vec"], sb["zs"], sb["cv"]
        qq, bb, gg, bv, pc = sb["qq"], sb["bb"], sb["gg"], sb["bv"], sb["pc"]
        wa_up = buf("b_wa_up", [P, RW])
        g_up = buf("b_g_up", [P, RW])
        headones = sb["headones"]
        ones = buf("b_ones", [P, P])
        keep = buf("b_keep", [P, T])
        kk = buf("b_kk", [P, T])
        sq = buf("b_sq", [P, T])
        nrm = buf("b_nrm", [P, T])
        am = buf("b_am", [P, T])
        rk = buf("b_rk", [P, T])
        run = buf("b_run", [P, T])
        bef = buf("b_bef", [P, T])
        dec = buf("b_dec", [P, T])
        inv = buf("b_inv", [P, T])
        ps = [ctx.enter_context(nc.psum_tensor(f"b_ps{i}", [P, T], F32)) for i in range(4)]

        s_const = sem("b_constants_made")
        s_up = sem("b_up_weights_in")
        s_lora = sem("b_lora_inputs_ready")
        s_wmm, s_amm, s_gmm = sem("b_w_in_psum"), sem("b_a_in_psum"), sem("b_g_in_psum")
        s_w, s_a, s_g = sem("b_w_ready"), sem("b_a_ready"), sem("b_g_ready")
        s_kk, s_sq, s_ssum = sem("b_kk_raw"), sem("b_kk_squared"), sem("b_kk_square_sum")
        s_nrm, s_rn = sem("b_kk_norm_inverted"), sem("b_kk_norm_ready")
        s_rk, s_rsum, s_bv = sem("b_rk_ready"), sem("b_bonus_sum"), sem("b_bonus_ready")
        s_run, s_bef, s_exp = sem("b_running_sum"), sem("b_sum_before"), sem("b_exponentials")
        s_used = sem("b_exponentials_used")
        s_dve = sem("b_vector_step")
        s_mean, s_diff, s_dsq = sem("b_conv_mean"), sem("b_conv_centred"), sem("b_conv_squared")
        s_var, s_vinv, s_rstd = sem("b_conv_variance"), sem("b_conv_variance_inverted"), sem("b_conv_rstd")
        s_nc, s_silu = sem("b_conv_normed"), sem("b_conv_silu")
        block = ctx.enter_context(nc.Block())

        def vcol(name, i, rows=slice(0, P)):
            return vec[rows, COL[name] + i:COL[name] + i + 1]

        @block.sync
        def _(sp):
            sp.dma_start(wa_up[:, :], io["wa_up"]).then_inc(s_up, 16)
            sp.dma_start(g_up[:, :], io["g_up"]).then_inc(s_up, 16)

        @block.gpsimd
        def _(pool):
            pool.memset(keep[:, :], 1.0).then_inc(s_const, 1)
            pool.memset(ones[:, :], 1.0).then_inc(s_const, 1)
            pool.memset(headones[:, :], 0.0).then_inc(s_const, 1)
            pool.wait_ge(s_const, 3)
            pool.memset(keep[:, :].rearrange("p (c t) -> p c t", t=CH)[:, :, 0:1], 0.0).then_inc(s_const, 1)
            for e in range(2):
                pool.wait_ge(s_const, 4 + e)
                pool.memset(headones[e * HD:(e + 1) * HD, e * HD:(e + 1) * HD], 1.0).then_inc(s_const, 1)

        @block.tensor
        def _(pe):
            pe.wait_ge(s_up, 32)
            pe.wait_ge(s_lora, 2)
            for i in range(PAIRS):
                c = slice(i * P, (i + 1) * P)
                if i:
                    pe.wait_ge(s_w, i)
                for h in range(NH):
                    t = slice(h * HALF, (h + 1) * HALF)
                    last = pe.matmul(ps[0][:, t], wa_up[0:64, c], zs[0:64, 12, t], start=True, stop=True)
                last.then_inc(s_wmm, 1)
                if i:
                    pe.wait_ge(s_a, i)
                for h in range(NH):
                    t = slice(h * HALF, (h + 1) * HALF)
                    last = pe.matmul(ps[1][:, t], wa_up[64:P, c], zs[64:P, 12, t], start=True, stop=True)
                last.then_inc(s_amm, 1)
                if i:
                    pe.wait_ge(s_nrm, i)
                for h in range(NH):
                    t = slice(h * HALF, (h + 1) * HALF)
                    last = pe.matmul(ps[2][:, t], g_up[:, c], zs[:, 13, t], start=True, stop=True)
                last.then_inc(s_gmm, 1)
                pe.wait_ge(s_const, 6)
                pe.wait_ge(s_sq, i + 1)
                pe.wait_ge(s_g, i + 1)
                for h in range(NH):
                    t = slice(h * HALF, (h + 1) * HALF)
                    last = pe.matmul(ps[2][:, t], headones[:, :], sq[:, t], start=True, stop=True)
                last.then_inc(s_ssum, 1)
                pe.wait_ge(s_rk, i + 1)
                if i:
                    pe.wait_ge(s_bv, i)
                for h in range(NH):
                    t = slice(h * HALF, (h + 1) * HALF)
                    last = pe.matmul(ps[3][:, t], headones[:, :], rk[:, t], start=True, stop=True)
                last.then_inc(s_rsum, 1)
            pe.wait_ge(s_w, PAIRS)
            for i in range(CONV_TILES):
                for h in range(NH):
                    t = slice(h * HALF, (h + 1) * HALF)
                    last = pe.matmul(ps[0][:, t], ones[:, :], cv[:, i, t], start=(i == 0), stop=(i == CONV_TILES - 1),
                                     skip_group_check=True)
            last.then_inc(s_mean, 1)
            pe.wait_ge(s_a, PAIRS)
            for i in range(CONV_TILES):
                pe.wait_ge(s_dsq, i + 1)
                for h in range(NH):
                    t = slice(h * HALF, (h + 1) * HALF)
                    last = pe.matmul(ps[1][:, t], ones[:, :], (sq, rk)[i % 2][:, t], start=(i == 0), stop=(i == CONV_TILES - 1),
                                     skip_group_check=True)
                last.then_inc(s_var, 1)

        @block.scalar
        def _(act):
            act.activation(zs[0:64, 12, :], zs[0:64, 12, :], ACT.Tanh).then_inc(s_lora, 1)
            act.activation(zs[:, 13, :], zs[:, 13, :], ACT.Sigmoid).then_inc(s_lora, 1)
            for i in range(PAIRS):
                act.wait_ge(s_wmm, i + 1)
                act.activation(qq[:, i, :], ps[0][:, :], ACT.Sigmoid, bias=vcol("w0", i)).then_inc(s_w, 1)
                act.wait_ge(s_amm, i + 1)
                act.activation(bb[:, i, :], ps[1][:, :], ACT.Sigmoid, bias=vcol("a0", i)).then_inc(s_a, 1)
                act.wait_ge(s_gmm, i + 1)
                act.activation(gg[:, i, :], ps[2][:, :], ACT.Copy).then_inc(s_g, 1)
                act.wait_ge(s_kk, i + 1)
                if i:
                    act.wait_ge(s_ssum, i)
                act.activation(sq[:, :], kk[:, :], ACT.Square).then_inc(s_sq, 1)
                act.wait_ge(s_bef, i + 1)
                if i:
                    act.wait_ge(s_used, i)
                act.activation(dec[:, :], run[:, :], ACT.Exp, scale=-DECAY).then_inc(s_exp, 1)
                act.activation(inv[:, :], run[:, :], ACT.Exp, scale=DECAY).then_inc(s_exp, 1)
                act.activation(bef[:, :], bef[:, :], ACT.Exp, scale=-DECAY).then_inc(s_exp, 1)
                act.wait_ge(s_nrm, i + 1)
                act.activation(nrm[:, :], nrm[:, :], ACT.Sqrt).then_inc(s_rn, 1)
            for i in range(CONV_TILES):
                act.wait_ge(s_diff, i + 1)
                if i == 0:
                    act.wait_ge(s_ssum, PAIRS)
                if i == 1:
                    act.wait_ge(s_rsum, PAIRS)
                if i >= 2:
                    act.wait_ge(s_var, i - 1)
                act.activation((sq, rk)[i % 2][:, :], cv[:, i, :], ACT.Square).then_inc(s_dsq, 1)
            act.wait_ge(s_vinv, 1)
            act.activation(nrm[:, :], nrm[:, :], ACT.Sqrt).then_inc(s_rstd, 1)
            for i in range(CONV_TILES):
                act.wait_ge(s_nc, i + 1)
                act.activation(cv[:, i, :], cv[:, i, :], ACT.Silu, scale=vcol("ln_g", i), bias=vcol("ln_b", i)).then_inc(s_silu, 1)

        @block.vector
        def _(dve):
            link = Link(dve, s_dve)
            for i in range(PAIRS):
                r, k, v = zs[:, i, :], zs[:, PAIRS + i, :], zs[:, 2 * PAIRS + i, :]
                dve.tensor_scalar(kk[:, :], k, vcol("k_k", i), None, ALU.mult).then_inc(s_kk, 1)
                dve.wait_ge(s_const, 6)
                dve.wait_ge(s_w, i + 1)
                dve.tensor_tensor_scan(run[:, :], keep[:, :], qq[:, i, :], 0.0, ALU.mult, ALU.add).then_inc(s_run, 1)
                dve.wait_ge(s_run, i + 1)
                dve.tensor_tensor(bef[:, :], run[:, :], qq[:, i, :], ALU.subtract).then_inc(s_bef, 1)
                dve.wait_ge(s_a, i + 1)
                link(dve.tensor_scalar(am[:, :], bb[:, i, :], -1.0, vcol("k_a", i), ALU.add, ALU.mult))
                dve.wait_ge(s_kk, i + 1)
                link(dve.scalar_tensor_tensor(out=k, in0=am[:, :], scalar=1.0, in1=k, op0=ALU.add, op1=ALU.mult))
                if i:
                    dve.wait_ge(s_rsum, i)
                dve.scalar_tensor_tensor(out=rk[:, :], in0=r, scalar=vcol("r_k", i), in1=k, op0=ALU.mult,
                                         op1=ALU.mult).then_inc(s_rk, 1)
                dve.wait_ge(s_ssum, i + 1)
                link(dve.tensor_scalar(nrm[:, :], ps[2][:, :], 1e-24, None, ALU.max))
                dve.reciprocal(nrm[:, :], nrm[:, :]).then_inc(s_nrm, 1)
                dve.wait_ge(s_rsum, i + 1)
                dve.tensor_tensor(bv[:, i, :], ps[3][:, :], v, ALU.mult).then_inc(s_bv, 1)
                dve.wait_ge(s_exp, 3 * (i + 1))
                dve.wait_ge(s_rk, i + 1)
                link(dve.tensor_tensor(r, r, dec[:, :], ALU.mult))
                link(dve.tensor_copy(pc[:, i, :], dec[:, :].rearrange("p (c t) -> p c t", t=CH)[:, :, CH - 1]))
                link(dve.tensor_tensor(k, k, inv[:, :], ALU.mult))
                dve.wait_ge(s_rn, i + 1)
                link(dve.tensor_tensor(kk[:, :], kk[:, :], nrm[:, :], ALU.mult))
                link(dve.tensor_tensor(bb[:, i, :], bb[:, i, :], kk[:, :], ALU.mult))
                link(dve.tensor_tensor(bb[:, i, :], bb[:, i, :], inv[:, :], ALU.mult))
                link(dve.scalar_tensor_tensor(out=qq[:, i, :], in0=kk[:, :], scalar=-1.0, in1=bef[:, :], op0=ALU.mult,
                                              op1=ALU.mult))
                dve.sem_inc(s_used, 1)
            dve.wait_ge(s_mean, 1)
            link(dve.tensor_scalar(am[:, :], ps[0][:, :], 1.0 / CONV_W, None, ALU.mult))
            for i in range(CONV_TILES):
                dve.tensor_tensor(cv[:, i, :], cv[:, i, :], am[:, :], ALU.subtract).then_inc(s_diff, 1)
            dve.wait_ge(s_var, CONV_TILES)
            link(dve.tensor_scalar(nrm[:, :], ps[1][:, :], 1.0 / CONV_W, LN_EPS, ALU.mult, ALU.add))
            dve.reciprocal(nrm[:, :], nrm[:, :]).then_inc(s_vinv, 1)
            dve.wait_ge(s_rstd, 1)
            for i in range(CONV_TILES):
                dve.wait_ge(s_diff, i + 1)
                dve.wait_ge(s_dsq, i + 1)
                dve.tensor_tensor(cv[:, i, :], cv[:, i, :], nrm[:, :], ALU.mult).then_inc(s_nc, 1)



MASKS = 16
SUB = 16


def recurrence(nc, io, sb):
    with ExitStack() as ctx:
        def buf(name, shape, dt=F32):
            return ctx.enter_context(nc.sbuf_tensor(name, shape, dt))

        sem = ctx.enter_context(semaphores(nc))

        ident, zs, qq, bb, pc = sb["ident"], sb["zs"], sb["qq"], sb["bb"], sb["pc"]
        U = 2 * PAIRS
        qr = buf("c_qr", [P, PAIRS, 2, 2, CH])
        bk = buf("c_bk", [P, PAIRS, 2, 2, CH])
        vs = buf("c_vs", [P, PAIRS, CH + P])
        gs = buf("c_gs", [P, 2, 2, PAIRS, P])
        bt = buf("c_bt", [P, 2, PAIRS, P])
        xs = buf("c_xs", [P, 2, PAIRS, 2, HD])
        rs = buf("c_rs", [CH, PAIRS, 2, HD])
        st = buf("c_st", [P, PAIRS, 2, HD])
        tmp = buf("c_tmp", [P, PAIRS, HD])
        m_g, m_dt = buf("c_m_g", [P, P]), buf("c_m_dt", [CH, CH])
        m_d, m_e = buf("c_m_d", [CH, CH]), buf("c_m_e", [CH, CH])
        names = ("d", "dt", "e", "z", "d2", "d2t", "ift")
        inv = [{n: buf(f"c_{n}{e}", [CH, U, CH]) for n in names} for e in range(2)]
        pg = [ctx.enter_context(nc.psum_tensor(f"c_pg{e}", [P, 2 * HALF], F32)) for e in range(2)]
        pi = [[ctx.enter_context(nc.psum_tensor(f"c_pi{e}{j}", [P, HALF], F32)) for j in range(2)] for e in range(2)]

        s_pe, s_pool = sem("c_tensor_waits_passed"), sem("c_gpsimd_waits_passed")
        s_mask = sem("c_masks_ready")
        s_ops = sem("c_operands_copied")
        s_g = sem("c_products_in_psum")
        s_gs = sem("c_products_masked")
        s_i = [sem(f"c_inverse_step{e}") for e in range(2)]
        s_ia = [sem(f"c_inverse_copied{e}") for e in range(2)]
        s_id = [sem(f"c_inverse_added{e}") for e in range(2)]
        s_tr, s_trc = sem("c_turned"), sem("c_turned_copied")
        s_seq = sem("c_chain_step")
        s_cp = sem("c_chain_copied")
        s_y = sem("c_y_copied")
        s_sum, s_st = sem("c_state_summed"), sem("c_state_ready")
        block = ctx.enter_context(nc.Block())

        def pin(eng):
            eng.sem_inc(s_pe if eng.engine == nc.tensor.engine else s_pool, 1)

        @block.gpsimd
        def _(pool):
            k = 0

            def step(ins):
                nonlocal k
                k += 1
                ins.then_inc(s_mask, 1)
                pool.wait_ge(s_mask, k)

            step(pool.memset(st[:, :, :, :], 0.0))
            step(pool.memset(xs[:, :, :, :, :], 0.0))
            step(pool.memset(vs[:, :, :], 0.0))
            for m in (m_g, m_dt, m_d, m_e):
                step(pool.memset(m[:, :], 1.0))
            step(pool.memset(m_g[0:CH, 0:CH], 0.0))
            step(pool.affine_select(out=m_g[0:CH, CH:P], in_=m_g[0:CH, CH:P], compare_op=ALU.is_ge, fill=0.0, base=0,
                                    pattern=[[1, CH]], channel_multiplier=-1))
            step(pool.affine_select(out=m_g[CH:P, 0:CH], in_=m_g[CH:P, 0:CH], compare_op=ALU.is_gt, fill=0.0, base=0,
                                    pattern=[[1, CH]], channel_multiplier=-1))
            step(pool.affine_select(out=m_g[CH:P, CH:P], in_=m_g[CH:P, CH:P], compare_op=ALU.is_ge, fill=0.0, base=0,
                                    pattern=[[1, CH]], channel_multiplier=-1))
            NB = CH // SUB

            def blocks(m):
                return m[:, :].rearrange("p (b j) -> p b j", j=SUB)

            step(pool.affine_select(out=blocks(m_dt), in_=blocks(m_dt), compare_op=ALU.is_gt, fill=0.0, base=0,
                                    pattern=[[SUB, NB], [1, SUB]], channel_multiplier=-1))
            step(pool.affine_select(out=blocks(m_dt), in_=blocks(m_dt), compare_op=ALU.is_ge, fill=0.0, base=0,
                                    pattern=[[-SUB, NB], [0, SUB]], channel_multiplier=1))
            step(pool.affine_select(out=blocks(m_d), in_=blocks(m_d), compare_op=ALU.is_gt, fill=0.0, base=0,
                                    pattern=[[-SUB, NB], [-1, SUB]], channel_multiplier=1))
            step(pool.affine_select(out=blocks(m_d), in_=blocks(m_d), compare_op=ALU.is_ge, fill=0.0, base=SUB - 1,
                                    pattern=[[SUB, NB], [0, SUB]], channel_multiplier=-1))
            step(pool.affine_select(out=blocks(m_e), in_=blocks(m_e), compare_op=ALU.is_ge, fill=0.0, base=-SUB,
                                    pattern=[[-SUB, NB], [0, SUB]], channel_multiplier=1))
            masks = k
            assert masks == MASKS
            with pool.Fori(0, NT) as t:
                pool.wait_ge(s_seq, t * 8 + 1)
                pin(pool)
                tok = ds(t * P, P)

                def chunks(a):
                    return a[:, :, tok].rearrange("p i (c t) -> p i c t", t=CH)

                pool.tensor_copy(qr[:, :, :, 0, :], chunks(qq)).then_inc(s_ops, 1)
                pool.tensor_copy(bk[:, :, :, 0, :], chunks(bb)).then_inc(s_ops, 1)
                pool.tensor_copy(qr[:, :, :, 1, :], chunks(zs[:, 0:PAIRS, :])).then_inc(s_ops, 1)
                pool.tensor_copy(bk[:, :, :, 1, :], chunks(zs[:, PAIRS:2 * PAIRS, :])).then_inc(s_ops, 1)
                pool.tensor_copy(vs[:, :, CH:], zs[:, 2 * PAIRS:3 * PAIRS, tok]).then_inc(s_ops, 1)

        @block.tensor
        def _(pe):
            pe.sem_inc(s_seq, 1)
            with pe.Fori(0, NT) as t:
                def inverse(e, step, *products):
                    for out, a, b in products:
                        for u in range(U):
                            o = pi[e][out][0:CH, u * CH:(u + 1) * CH]
                            if b is None:
                                last = pe.transpose(o, inv[e][a][:, u, :], ident[0:CH, 0:CH])
                            else:
                                last = pe.matmul(o, inv[e][a][:, u, :], inv[e][b][:, u, :], start=True, stop=True)
                    last.then_inc(s_i[e], 1)

                def after_copy(e, n):
                    pe.wait_ge(s_ia[e], t * 10 + n)
                    pin(pe)

                def after_add(e, n):
                    pe.wait_ge(s_id[e], t * 9 + n)
                    pin(pe)

                pe.wait_ge(s_ops, t * 5 + 4)
                pe.wait_ge(s_y, t * 2 + 1)
                pe.wait_ge(s_sum, t * 4 + 1)
                pin(pe)
                for e in range(2):
                    h = slice(e * HD, (e + 1) * HD)
                    for c in range(2):
                        for i in range(PAIRS):
                            u = c * PAIRS + i
                            last = pe.matmul(pg[e][:, u * P:(u + 1) * P], bk[h, i, c, :, :], qr[h, i, c, :, :],
                                             start=True, stop=True)
                    last.then_inc(s_g, 1)
                for e in range(2):
                    h = slice(e * HD, (e + 1) * HD)
                    for c in range(2):
                        for i in range(PAIRS):
                            u = c * PAIRS + i
                            last = pe.matmul(pi[e][0][0:CH, u * CH:(u + 1) * CH], qr[h, i, c, 0, :], bk[h, i, c, 0, :],
                                             start=True, stop=True)
                    last.then_inc(s_i[e], 1)
                for e in range(2):
                    after_add(e, 4)
                    inverse(e, 2, (0, "dt", "d"), (1, "d", "dt"))
                pe.wait_ge(s_ops, t * 5 + 5)
                pe.wait_ge(s_gs, t * 2 + 2)
                pin(pe)
                for c in range(2):
                    for i in range(PAIRS):
                        u = c * PAIRS + i
                        last = pe.transpose(pg[0][:, u * P:(u + 1) * P], bk[:, i, c, :, :].rearrange("p a t -> p (a t)"), ident[:, :])
                last.then_inc(s_tr, 1)
                for c in range(2):
                    for i in range(PAIRS):
                        u = c * PAIRS + i
                        last = pe.transpose(pg[1][:, u * P:(u + 1) * P], vs[:, i, c * CH:c * CH + P], ident[:, :])
                last.then_inc(s_tr, 1)
                for e in range(2):
                    after_copy(e, 2)
                    inverse(e, 3, (0, "d2t", "d2"), (1, "d2", "d2t"))
                for e in range(2):
                    after_copy(e, 4)
                    inverse(e, 4, (0, "d2", "z"), (1, "dt", "d"))
                for e in range(2):
                    after_copy(e, 5)
                    after_add(e, 5)
                    inverse(e, 5, (0, "d", "z"))
                for e in range(2):
                    after_add(e, 6)
                    inverse(e, 6, (1, "d2t", "z"))
                for e in range(2):
                    after_add(e, 7)
                    inverse(e, 7, (0, "z", "e"), (1, "e", "z"))
                for e in range(2):
                    after_copy(e, 7)
                    after_add(e, 8)
                    inverse(e, 8, (0, "dt", "d2"), (1, "z", None))
                for e in range(2):
                    after_copy(e, 9)
                    inverse(e, 9, (0, "d2t", "ift"))
                for e in range(2):
                    after_add(e, 9)
                    inverse(e, 10, (1, "d", "ift"))
                for c in range(2):
                    pe.wait_ge(s_trc, t * 2 + 2)
                    pe.wait_ge(s_st, t * 4 + (2 * c + 1) if c == 0 else t * 4 + 3)
                    pe.wait_ge(s_st, t * 4 + 2 * c + 2)
                    pin(pe)
                    for i in range(PAIRS):
                        pe.matmul(pg[0][0:CH, i * P:(i + 1) * P], qr[:, i, c, 0, :], st[:, i, :, :], start=True, stop=False)
                        for e in range(2):
                            last = pe.matmul(pg[0][0:CH, i * P + e * HD:i * P + (e + 1) * HD], gs[:, e, c, i, 0:CH],
                                             xs[:, c, i, e, :], start=False, stop=(e == 1))
                    last.then_inc(s_seq, 1)
                    pe.wait_ge(s_cp, t * 4 + (2 * c + 1))
                    if c == 0:
                        for e in range(2):
                            pe.wait_ge(s_ia[e], t * 10 + 10)
                    pin(pe)
                    for i in range(PAIRS):
                        for e in range(2):
                            last = pe.matmul(pg[0][0:CH, HALF + i * P + e * HD:HALF + i * P + (e + 1) * HD],
                                             inv[e]["e"][:, c * PAIRS + i, :], rs[:, i, e, :], start=True, stop=True)
                    last.then_inc(s_seq, 1)
                    pe.wait_ge(s_cp, t * 4 + (2 * c + 2))
                    if c == 1:
                        pe.wait_ge(s_y, t * 2 + 2)
                    pin(pe)
                    for i in range(PAIRS):
                        pe.matmul(pg[1][:, i * CH:(i + 1) * CH], st[:, i, :, :].rearrange("p e v -> p (e v)"), qr[:, i, c, 1, :],
                                  start=(i == 0), stop=False, skip_group_check=True)
                    for i in range(PAIRS):
                        for e in range(2):
                            last = pe.matmul(pg[1][e * HD:(e + 1) * HD, i * CH:(i + 1) * CH], xs[:, c, i, e, :],
                                             gs[:, e, c, i, CH:P], start=False, stop=(i == PAIRS - 1), skip_group_check=True)
                    last.then_inc(s_seq, 1)
                    for i in range(PAIRS):
                        for e in range(2):
                            last = pe.matmul(pg[1][e * HD:(e + 1) * HD, HALF + i * HD:HALF + (i + 1) * HD],
                                             bt[:, c, i, e * HD:(e + 1) * HD], xs[:, c, i, e, :], start=True, stop=True)
                    last.then_inc(s_seq, 1)

        @block.scalar
        def _(act):
            act.sem_inc(s_y, 1)
            with act.Fori(0, NT) as t:
                def copies(e, step, *pairs):
                    act.wait_ge(s_i[e], t * 10 + step)
                    for src, dst in pairs:
                        act.activation(inv[e][dst][:, :, :], pi[e][src][0:CH, :].rearrange("p (u t) -> p u t", t=CH),
                                       ACT.Copy).then_inc(s_ia[e], 1)

                for e in range(2):
                    copies(e, 2, (0, "d2"), (1, "d2t"))
                act.wait_ge(s_tr, t * 2 + 2)
                act.activation(bt[:, :, :, :], pg[0][:, :].rearrange("p (c i k) -> p c i k", c=2, i=PAIRS), ACT.Copy).then_inc(s_trc, 1)
                act.activation(xs[CH:P, :, :, :, :].rearrange("p c i e v -> p (c i e v)"), pg[1][CH:P, :], ACT.Copy).then_inc(s_trc, 1)
                for e in range(2):
                    copies(e, 3, (0, "d"), (1, "dt"))
                for e in range(2):
                    copies(e, 4, (1, "d2t"))
                for e in range(2):
                    copies(e, 7, (0, "d2"), (1, "dt"))
                for e in range(2):
                    copies(e, 8, (0, "d2t"), (1, "d"))
                for e in range(2):
                    copies(e, 10, (1, "e"))
                for c in range(2):
                    act.wait_ge(s_seq, t * 8 + (4 * c + 2))
                    act.activation(rs[:, :, :, :].rearrange("p i e v -> p (i e v)"), pg[0][0:CH, 0:HALF], ACT.Copy).then_inc(s_cp, 1)
                    act.wait_ge(s_seq, t * 8 + (4 * c + 3))
                    act.activation(xs[0:CH, c, :, :, :].rearrange("p i e v -> p (i e v)"), pg[0][0:CH, HALF:], ACT.Copy).then_inc(s_cp, 1)
                    act.wait_ge(s_seq, t * 8 + (4 * c + 4))
                    act.activation(zs[:, 0:PAIRS, ds(t * P + c * CH, CH)], pg[1][:, 0:PAIRS * CH].rearrange("p (i t) -> p i t", t=CH),
                                   ACT.Copy).then_inc(s_y, 1)

        @block.vector
        def _(dve):
            dve.wait_ge(s_mask, MASKS)
            dve.sem_inc(s_st, 2)
            dve.sem_inc(s_sum, 1)
            with dve.Fori(0, NT) as t:
                def mask(m, shape):
                    return m.unsqueeze(1).to_broadcast(shape)

                def add(e, step, src, other, dst, n):
                    dve.wait_ge(s_i[e], t * 10 + step)
                    dve.wait_ge(s_id[e], t * 9 + n - 1)
                    dve.tensor_tensor(inv[e][dst][:, :, :], pi[e][src][0:CH, :].rearrange("p (u t) -> p u t", t=CH),
                                      inv[e][other][:, :, :], ALU.add).then_inc(s_id[e], 1)

                for e in range(2):
                    g = pg[e][:, :].rearrange("p (u t) -> p u t", t=P)
                    dve.wait_ge(s_g, t * 2 + (e + 1))
                    dve.tensor_tensor(gs[:, e, :, :, :].rearrange("p c i t -> p (c i) t"), g, mask(m_g[:, :], [P, U, P]),
                                      ALU.mult).then_inc(s_gs, 1)
                    dve.tensor_tensor(inv[e]["dt"][:, :, :], g[0:CH, :, 0:CH], mask(m_dt[:, :], [CH, U, CH]),
                                      ALU.mult).then_inc(s_id[e], 1)
                for e in range(2):
                    p = pi[e][0][0:CH, :].rearrange("p (u t) -> p u t", t=CH)
                    dve.wait_ge(s_i[e], t * 10 + 1)
                    dve.tensor_tensor(inv[e]["d"][:, :, :], p, mask(m_d[:, :], [CH, U, CH]), ALU.mult).then_inc(s_id[e], 1)
                    dve.tensor_tensor(inv[e]["e"][:, :, :], p, mask(m_e[:, :], [CH, U, CH]), ALU.mult).then_inc(s_id[e], 1)
                    dve.wait_ge(s_id[e], t * 9 + 1)
                    dve.tensor_tensor(inv[e]["z"][:, :, :], inv[e]["dt"][:, :, :], mask(ident[0:CH, 0:CH], [CH, U, CH]),
                                      ALU.add).then_inc(s_id[e], 1)
                for e in range(2):
                    add(e, 4, 0, "z", "z", 5)
                for e in range(2):
                    add(e, 5, 0, "z", "z", 6)
                for e in range(2):
                    add(e, 6, 1, "z", "z", 7)
                for e in range(2):
                    dve.wait_ge(s_ia[e], t * 10 + 7)
                    dve.tensor_tensor(inv[e]["ift"][:, :, :], inv[e]["dt"][:, :, :],
                                      mask(ident[0:CH, 0:CH], [CH, U, CH]), ALU.add).then_inc(s_id[e], 1)
                for e in range(2):
                    add(e, 9, 0, "ift", "ift", 9)
                for c in range(2):
                    dve.wait_ge(s_seq, t * 8 + (4 * c + 5))
                    for e in range(2):
                        h = slice(e * HD, (e + 1) * HD)
                        dve.tensor_tensor(tmp[h, :, :], pg[1][h, HALF:HALF + PAIRS * HD].rearrange("p (i v) -> p i v", v=HD),
                                          st[h, :, e, :], ALU.add).then_inc(s_sum, 1)
                    for e in range(2):
                        h = slice(e * HD, (e + 1) * HD)
                        dve.wait_ge(s_sum, t * 4 + (2 * c + e + 2))
                        dve.tensor_tensor(st[h, :, e, :], tmp[h, :, :], pc[h, :, ds(t * 2 + c, 1)].to_broadcast([HD, PAIRS, HD]),
                                          ALU.mult).then_inc(s_st, 1)




def mix(nc, io, sb, dram):
    with ExitStack() as ctx:
        def buf(name, shape, dt=F32):
            return ctx.enter_context(nc.sbuf_tensor(name, shape, dt))

        sem = ctx.enter_context(semaphores(nc))

        vec, zs, cv, gg, bv, headones = (sb[n] for n in ("vec", "zs", "cv", "gg", "bv", "headones"))
        sq = buf("d_sq", [P, T])
        rstd = buf("d_rstd", [P, T])
        wr = [buf(f"d_wr{i}", [P, PAIRS, P]) for i in range(2)]
        wc = [buf(f"d_wc{i}", [P, CONV_TILES, P]) for i in range(2)]
        gr = [buf(f"d_gr{i}", [P, T]) for i in range(2)]
        gc = [buf(f"d_gc{i}", [P, T]) for i in range(2)]
        pr = [ctx.enter_context(nc.psum_tensor(f"d_pr{i}", [P, T], F32)) for i in range(2)]
        pc = [ctx.enter_context(nc.psum_tensor(f"d_pc{i}", [P, T], F32)) for i in range(2)]
        s_mean, s_cen, s_sq = sem("d_y_mean"), sem("d_y_centred"), sem("d_y_squared")
        s_var, s_vinv, s_rstd = sem("d_y_variance"), sem("d_y_variance_inverted"), sem("d_y_rstd")
        s_norm, s_y = sem("d_y_normed"), sem("d_y_ready")
        s_dve = sem("d_vector_step")
        s_wr = [sem(f"d_w_r_in{i}") for i in range(2)]
        s_wc = [sem(f"d_w_c_in{i}") for i in range(2)]
        s_gr = [sem(f"d_gate_r_in{i}") for i in range(2)]
        s_gc = [sem(f"d_gate_c_in{i}") for i in range(2)]
        s_mm = sem("d_outputs_in_psum")
        s_free = sem("d_psum_free")
        s_mul, s_mix = sem("d_gated"), sem("d_mixed")
        s_out = [sem(f"d_mix_out{i}") for i in range(2)]
        block = ctx.enter_context(nc.Block())

        @block.sync
        def _(sp):
            def loads(m, i):
                sp.dma_start(wr[i][:, :, :], one(io["w_r"], m)).then_inc(s_wr[i], 16)
                sp.dma_start(wc[i][:, :, :], one(io["w_c"], m)).then_inc(s_wc[i], 16)

            def gate_loads(m, i):
                sp.dma_start(gr[i][:, :], one(dram["gates"], m)).then_inc(s_gr[i], 16)
                sp.dma_start(gc[i][:, :], one(dram["gates"], m + KT)).then_inc(s_gc[i], 16)

            for i in range(2):
                loads(i, i)
                gate_loads(i, i)
            with sp.Fori(0, KT // 2 - 1) as q:
                for i in range(2):
                    sp.wait_ge(s_mm, q * 2 + (i + 1))
                    loads(q * 2 + (i + 2), i)
                    sp.wait_ge(s_out[i], q * 16 + 16)
                    gate_loads(q * 2 + (i + 2), i)

        @block.tensor
        def _(pe):
            for i in range(PAIRS):
                y = zs[:, i, :]
                if i >= 2:
                    pe.wait_ge(s_cen, i - 1)
                for h in range(NH):
                    t = slice(h * HALF, (h + 1) * HALF)
                    last = pe.matmul(pr[i % 2][:, t], headones[:, :], y[:, t], start=True, stop=True)
                last.then_inc(s_mean, 1)
                pe.wait_ge(s_sq, i + 1)
                if i >= 2:
                    pe.wait_ge(s_vinv, i - 1)
                for h in range(NH):
                    t = slice(h * HALF, (h + 1) * HALF)
                    last = pe.matmul(pc[i % 2][:, t], headones[:, :], sq[:, t], start=True, stop=True)
                last.then_inc(s_var, 1)
            pe.wait_ge(s_y, PAIRS)
            with pe.Fori(0, KT // 2) as q:
                for i in range(2):
                    pe.wait_ge(s_wr[i], q * 16 + 16)
                    pe.wait_ge(s_wc[i], q * 16 + 16)
                    pe.wait_ge(s_free, q * 2 + (i + 1))
                    for w, x, p, n in ((wr, zs, pr, PAIRS), (wc, cv, pc, CONV_TILES)):
                        for h in range(NH):
                            t = slice(h * HALF, (h + 1) * HALF)
                            for k in range(n):
                                last = pe.matmul(p[i][:, t], w[i][:, k, :], x[:, k, t], start=(k == 0), stop=(k == n - 1))
                    last.then_inc(s_mm, 1)

        @block.scalar
        def _(act):
            for i in range(PAIRS):
                act.wait_ge(s_cen, i + 1)
                if i:
                    act.wait_ge(s_var, i)
                act.activation(sq[:, :], zs[:, i, :], ACT.Square).then_inc(s_sq, 1)
                act.wait_ge(s_vinv, i + 1)
                act.activation(rstd[:, :], rstd[:, :], ACT.Sqrt).then_inc(s_rstd, 1)
            with act.Fori(0, KT // 2) as q:
                for i in range(2):
                    act.wait_ge(s_mix, q * 2 + (i + 1))
                    act.dma_start(dram["mix"][:, :, ds(q * 2 + i, 1), :].rearrange("t p a c -> p t (a c)"),
                                  gr[i][:, :].rearrange("p (t c) -> p t c", c=P)).then_inc(s_out[i], 16)
            for i in range(2):
                act.wait_ge(s_out[i], 16 * (KT // 2))

        @block.vector
        def _(dve):
            link = Link(dve, s_dve)
            for i in range(PAIRS):
                y = zs[:, i, :]
                dve.wait_ge(s_mean, i + 1)
                dve.scalar_tensor_tensor(out=y, in0=pr[i % 2][:, :], scalar=-1.0 / HD, in1=y, op0=ALU.mult,
                                         op1=ALU.add).then_inc(s_cen, 1)
                dve.wait_ge(s_var, i + 1)
                link(dve.tensor_scalar(rstd[:, :], pc[i % 2][:, :], 1.0 / HD, GN_EPS, ALU.mult, ALU.add))
                dve.reciprocal(rstd[:, :], rstd[:, :]).then_inc(s_vinv, 1)
                dve.wait_ge(s_rstd, i + 1)
                link(dve.scalar_tensor_tensor(out=y, in0=y, scalar=vec[:, COL["lnx_g"] + i:COL["lnx_g"] + i + 1],
                                              in1=rstd[:, :], op0=ALU.mult, op1=ALU.mult))
                link(dve.scalar_tensor_tensor(out=y, in0=y, scalar=vec[:, COL["lnx_b"] + i:COL["lnx_b"] + i + 1],
                                              in1=bv[:, i, :], op0=ALU.add, op1=ALU.add))
                dve.tensor_tensor(y, y, gg[:, i, :], ALU.mult).then_inc(s_y, 1)
            dve.sem_inc(s_free, 2)
            with dve.Fori(0, KT // 2) as q:
                for i in range(2):
                    dve.wait_ge(s_mm, q * 2 + (i + 1))
                    dve.wait_ge(s_gr[i], q * 16 + 16)
                    dve.wait_ge(s_gc[i], q * 16 + 16)
                    dve.tensor_tensor(gr[i][:, :], gr[i][:, :], pr[i][:, :], ALU.mult).then_inc(s_mul, 1)
                    dve.tensor_tensor(gc[i][:, :], gc[i][:, :], pc[i][:, :], ALU.mult).then_inc(s_mul, 1)
                    dve.wait_ge(s_mul, q * 4 + (2 * i + 2))
                    dve.sem_inc(s_free, 1)
                    dve.tensor_tensor(gr[i][:, :], gr[i][:, :], gc[i][:, :], ALU.add).then_inc(s_mix, 1)



GRP = 8
GROUPS = NSEL // GRP
UR, VR, DR = 4, GRP, 4
KS = TOPK // 2
HEAD_AT = {6: 0, 7: 1, 8: 2, 9: 3, 11: 4, 12: 5, 13: 6, 14: 7}
HEAD_STEPS = 17
SELECT_STEPS = 10


def experts(nc, io, dram):
    with ExitStack() as ctx:
        def buf(name, shape, dt=F32):
            return ctx.enter_context(nc.sbuf_tensor(name, shape, dt))

        sem = ctx.enter_context(semaphores(nc))

        def psum(name, shape):
            return ctx.enter_context(nc.psum_tensor(name, shape, F32))

        ident, vec = buf("e_ident", [P, P]), buf("e_vec", [P, NVEC])
        w_out, w_q, w_ple = (buf(f"e_{n}", [P, KT, D]) for n in ("w_out", "w_q", "w_ple"))
        w_proj = buf("e_w_proj", [P, PLE // P, D])
        keys = buf("e_keys", [P, PH, NKEY])
        g_ffn, g_fin = buf("e_g_ffn", [P, D]), buf("e_g_fin", [P, D])
        mixt = buf("e_mix", [P, KT, P])
        qT = mixt
        xin = buf("e_x", [P, D])
        actT = buf("e_actT", [P, KT, P])
        c = buf("e_c", [P, D])
        hh, gt = buf("e_hh", [P, D]), buf("e_gt", [P, D])
        pt = buf("e_pt", [P, PLE // P, P])
        u = [buf(f"e_u{i}", [P, D]) for i in range(UR)]
        v = [buf(f"e_v{i}", [P, D]) for i in range(VR)]
        dg = [buf(f"e_dg{i}", [P, P]) for i in range(DR)]
        dots, gl, coef = buf("e_dots", [P, GRP]), buf("e_gelu", [P, GRP]), buf("e_coef", [P, GRP])
        zero = buf("e_zero", [P, HALF], mybir.dt.bfloat16)
        st = buf("e_stats", [P, 8])
        sc = buf("e_sc", [P, 2, NKEY])
        sc2 = buf("e_sc2", [P, 2, NKEY])
        cand, cand2 = buf("e_cand", [P, TOPK, TOPK]), buf("e_cand2", [P, TOPK * TOPK])
        tv, ti = buf("e_tv", [P, 2, TOPK]), buf("e_ti", [P, 2, TOPK], U32)
        ix = buf("e_ix", [P, 2, PH, TOPK])
        best, pos = buf("e_best", [P, PH, TOPK]), buf("e_pos", [P, PH, TOPK], U32)
        half = buf("e_half", [P, PH, TOPK], U32)
        halff = buf("e_halff", [P, PH, TOPK])
        pick = buf("e_pick", [P, 2, PH, TOPK])
        iot, ioti = buf("e_iota", [P, TOPK]), buf("e_iotai", [P, TOPK], mybir.dt.int32)
        ex = buf("e_exp", [P, PH, TOPK])
        ssum = buf("e_ssum", [P, PH])
        gates = buf("e_gates", [P, NSEL])
        idx_n, idx = buf("e_idx_next", [P, NSEL], U32), buf("e_idx", [P, NSEL], U32)
        stage = [buf(f"e_idx_group{e}", [P, GRP], U32) for e in range(2)]
        oh = actT

        pd = psum("e_pd", [P, D])
        acc = psum("e_acc", [P, D])
        ps = psum("e_ps", [P, 2, PH, NKEY])

        s_const, s_w, s_iota = sem("e_constants"), sem("e_weights_in"), sem("e_iota")
        s_ident = sem("e_identity_made")
        s_zero = sem("e_sum_cleared")
        s_mixin, s_xin = sem("e_mix_in"), sem("e_x_in")
        s_hps, s_h, s_hout = sem("e_h_in_psum"), sem("e_h_ready"), sem("e_h_out")
        s_sq, s_var, s_rstd = sem("e_h_squared"), sem("e_h_variance"), sem("e_h_rstd")
        s_hn, s_ctr, s_cT = sem("e_h_normed"), sem("e_c_turned"), sem("e_cT_ready")
        s_qps, s_qT, s_sc = sem("e_q_in_psum"), sem("e_qT_ready"), sem("e_scores_in_psum")
        s_head, s_topk = sem("e_head_copied"), sem("e_head_used")
        s_k = sem("e_topk_step")
        s_fv, s_tv = sem("e_h_mean_square"), sem("e_tail_mean_square")
        s_sub, s_exp, s_in = sem("e_score_less_max"), sem("e_exp"), sem("e_indices_ready")
        s_gsum = sem("e_gate_step")
        s_fin = sem("e_select_step")
        s_icp, s_istage = sem("e_indices_copied"), sem("e_group_indices")
        s_pool = sem("e_gpsimd_waits_passed")
        s_dve = sem("e_vector_waits_passed")
        s_sp = sem("e_sync_waits_passed")
        s_cur = sem("e_tile_switched")
        s_u = [sem(f"e_u_in{i}") for i in range(UR)]
        s_v = [sem(f"e_v_in{i}") for i in range(VR)]
        s_dot, s_gelu, s_coef = sem("e_dot"), sem("e_gelu"), sem("e_coef")
        s_diag, s_vmm = sem("e_diag"), sem("e_v_added")
        s_hhin, s_hh, s_ptin = sem("e_tail_h_in"), sem("e_tail_h_ready"), sem("e_p_in")
        s_tsq, s_tvar, s_trstd = sem("e_tail_squared"), sem("e_tail_variance"), sem("e_tail_rstd")
        s_tn, s_ttr, s_tT = sem("e_tail_normed"), sem("e_tail_turned"), sem("e_tailT_ready")
        s_gps, s_gate = sem("e_gate_in_psum"), sem("e_gate_ready")
        s_pps, s_gp, s_h3 = sem("e_proj_in_psum"), sem("e_gated_proj"), sem("e_last_h")
        s_out, s_outd = sem("e_out_ready"), sem("e_out_stored")

        block = ctx.enter_context(nc.Block())

        @block.sync
        def _(sp):
            for dst, name in ((w_out, "w_out"), (w_q, "w_q"), (keys, "keys"), (w_ple, "w_ple"), (w_proj, "w_proj")):
                sp.dma_start(dst[:, :, :], io[name]).then_inc(s_w, 16)
            sp.dma_start(vec[:, :], io["vec"]).then_inc(s_w, 16)
            sp.dma_start(g_ffn[:, :], io["g_ffn"].to_broadcast([P, D])).then_inc(s_w, 16)
            sp.dma_start(g_fin[:, :], io["g_fin"].to_broadcast([P, D])).then_inc(s_w, 16)
            sp.dma_start(pt[:, :, :], io["pT"][NT - 1]).then_inc(s_ptin, 16)
            sp.dma_start(hh[:, :], io["x"][NT - 1]).then_inc(s_hhin, 16)

            def after(semaphore, count):
                sp.wait_ge(semaphore, count)
                sp.sem_inc(s_sp, 1)

            def mix_load(tile):
                sp.dma_start(mixt[:, :, :], one(dram["mix"], tile)).then_inc(s_mixin, 16)

            sp.dma_start(xin[:, :], io["x"][0]).then_inc(s_xin, 16)
            mix_load(0)
            sp.wait_ge(s_h, 1)
            sp.dma_start(dram["h"][0], xin[:, :]).then_inc(s_hout, 16)
            sp.wait_ge(s_sc, 1)
            mix_load(1)
            with sp.Fori(0, NT) as t:
                after(s_cur, t + 1)
                sp.dma_start(xin[:, :], one(io["x"], (t + 1) & (NT - 1))).then_inc(s_xin, 16)
                after(s_h, t + 2)
                sp.dma_start(one(dram["h"], (t + 1) & (NT - 1)), xin[:, :]).then_inc(s_hout, 16)
                after(s_sc, t + 2)
                mix_load((t + 2) & (NT - 1))
                after(s_pps, t + 1)
                sp.dma_start(pt[:, :, :], one(io["pT"], t)).then_inc(s_ptin, 16)
                after(s_out, t + 1)
                sp.dma_start(one(dram["out"], (t + (NT - 1)) & (NT - 1)), gt[:, :]).then_inc(s_outd, 16)
                after(s_outd, t * 16 + 16)
                after(s_hout, t * 16 + 16)
                sp.dma_start(hh[:, :], one(dram["h"], t)).then_inc(s_hhin, 16)
            sp.wait_ge(s_out, NT + 1)
            sp.wait_ge(s_outd, 16 * NT)
            sp.dma_start(one(dram["out"], NT - 1), gt[:, :]).then_inc(s_outd, 16)
            sp.wait_ge(s_outd, 16 * (NT + 1))
            sp.wait_ge(s_hout, 16 * (NT + 1))

        @block.gpsimd
        def _(pool):
            pool.memset(zero[:, :], 0.0).then_inc(s_const, 1)
            pool.memset(ident[:, :], 0.0).then_inc(s_ident, 1)
            pool.wait_ge(s_ident, 1)
            pool.affine_select(out=ident[:, :], in_=ident[:, :], compare_op=ALU.not_equal, fill=1.0,
                               base=0, pattern=[[-1, P]], channel_multiplier=1).then_inc(s_ident, 1)
            pool.iota(ioti[:, :], [[1, TOPK]], base=0, channel_multiplier=0).then_inc(s_const, 1)
            pool.wait_ge(s_const, 2)
            pool.tensor_copy(iot[:, :], ioti[:, :]).then_inc(s_iota, 1)
            pool.sem_inc(s_istage, 1)
            with pool.Fori(0, NT) as t:
                pool.wait_ge(s_in, t + 1)
                pool.wait_ge(s_istage, t * GROUPS + 1)
                pool.sem_inc(s_pool, 1)
                pool.tensor_copy(idx[:, :], idx_n[:, :]).then_inc(s_icp, 1)
                with pool.Fori(0, GROUPS // 2) as pair:
                    for e in range(2):
                        n = t * GROUPS + pair * 2 + e
                        pool.wait_ge(s_icp, t + 1)
                        pool.sem_inc(s_pool, 1)
                        pool.tensor_copy(stage[e][:, :], idx[:, ds(pair * (2 * GRP) + e * GRP, GRP)]).then_inc(s_istage, 1)
                        pool.wait_ge(s_istage, n + 2)
                        for s in range(GRP):
                            pool.wait_ge(s_dot, n * GRP + (s + 1))
                            pool.sem_inc(s_pool, 1)
                            pool.indirect_dma_start(out=u[s % UR][:, :], out_offset=None, in_=io["u_tab"],
                                                    in_offset=bass.IndirectOffsetOnAxis(ap=stage[e][:, s:s + 1], axis=0))\
                                .then_inc(s_u[s % UR], 16)
                        for s in range(GRP):
                            pool.wait_ge(s_vmm, n * GRP + (s + 1))
                            pool.sem_inc(s_pool, 1)
                            pool.indirect_dma_start(out=v[s][:, :], out_offset=None, in_=io["v_tab"],
                                                    in_offset=bass.IndirectOffsetOnAxis(ap=stage[e][:, s:s + 1], axis=0))\
                                .then_inc(s_v[s], 16)

        @block.tensor
        def _(pe):
            def turned(src, n, s_src, s_dst):
                pe.wait_ge(s_src, n + 1)
                for k in range(KT):
                    last = pe.transpose(pd[:, k * P:(k + 1) * P], src[:, k * P:(k + 1) * P], ident[:, :])
                last.then_inc(s_dst, 1)

            def product(lhs, w, kt, halves=(0, 1)):
                for h in halves:
                    for k in range(kt):
                        last = pe.matmul(pd[:, h * HALF:(h + 1) * HALF], lhs[:, k, :], w[:, k, h * HALF:(h + 1) * HALF],
                                         start=(k == 0), stop=(k == kt - 1))
                return last

            def mixed(n, halves=(0, 1)):
                if 0 in halves:
                    pe.wait_ge(s_mixin, n * 16 + 16)
                last = product(mixt, w_out, KT, halves)
                if 1 in halves:
                    last.then_inc(s_hps, 1)

            def queries(n, heads):
                if 0 in heads:
                    pe.wait_ge(s_cT, n + 1)
                for h in heads:
                    for k in range(KT):
                        last = pe.matmul(pd[:, h * P:(h + 1) * P], w_q[:, k, h * P:(h + 1) * P], actT[:, k, :],
                                         start=(k == 0), stop=(k == KT - 1))
                if PH - 1 in heads:
                    last.then_inc(s_qps, 1)

            def scores(n):
                pe.wait_ge(s_qT, n + 1)
                for p in range(2):
                    r = slice(p * PHALF, (p + 1) * PHALF)
                    for h in range(PH):
                        last = pe.matmul(ps[:, p, h, :], qT[r, h, :], keys[r, h, :], start=True, stop=True)
                last.then_inc(s_sc, 1)

            def ple_gate(n, halves=(0, 1)):
                if 0 in halves:
                    pe.wait_ge(s_tT, n + 1)
                last = product(actT, w_ple, KT, halves)
                if 1 in halves:
                    last.then_inc(s_gps, 1)

            def ple_proj(n):
                pe.wait_ge(s_ptin, n * 16 + 16)
                pe.wait_ge(s_gate, n + 1)
                product(pt, w_proj, PLE // P).then_inc(s_pps, 1)

            def group(n):
                for s in range(GRP):
                    pe.wait_ge(s_diag, n * GRP + (s + 2))
                    pe.wait_ge(s_v[s], n * 16 + 16)
                    for h in range(D // HALF):
                        cols = slice(h * HALF, (h + 1) * HALF)
                        last = pe.matmul(acc[:, cols], dg[s % DR][:, :], v[s][:, cols], start=False, stop=False,
                                         skip_group_check=True)
                    last.then_inc(s_vmm, 1)

            def clear():
                for h in range(D // HALF):
                    last = pe.matmul(acc[:, h * HALF:(h + 1) * HALF], zero[:, 0:P], zero[:, :], start=True, stop=False,
                                     skip_group_check=True)
                last.then_inc(s_zero, 1)

            pe.sem_inc(s_vmm, VR)
            pe.wait_ge(s_w, 16 * 8)
            pe.wait_ge(s_const, 2)
            pe.wait_ge(s_ident, 2)
            clear()
            mixed(0)
            turned(xin, 0, s_hn, s_ctr)
            queries(0, range(PH))
            scores(0)
            mixed(1)
            with pe.Fori(0, NT) as t:
                for g in range(GROUPS):
                    if g == 0:
                        pe.wait_ge(s_hh, t + 1)
                        clear()
                    group(t * GROUPS + g)
                    if g == 2:
                        turned(xin, t + 1, s_hn, s_ctr)
                    if g == 3:
                        queries(t + 1, range(PH // 2))
                    if g == 4:
                        queries(t + 1, range(PH // 2, PH))
                    if g == 5:
                        scores(t + 1)
                    if g == 6:
                        turned(gt, t, s_tn, s_ttr)
                    if g == 7:
                        ple_gate(t, (0,))
                    if g == 8:
                        ple_gate(t, (1,))
                    if g == 9:
                        ple_proj(t)
                    if g == 14:
                        pe.wait_ge(s_gp, t + 1)
                        mixed(t + 2, (0,))
                    if g == 15:
                        mixed(t + 2, (1,))
            turned(gt, NT, s_tn, s_ttr)
            ple_gate(NT)
            ple_proj(NT)

        @block.scalar
        def _(act):
            def square(scratch, src, column, n, s_src, s_dst):
                act.wait_ge(s_src, n)
                act.activation(scratch[:, :], src[:, :], ACT.Square, accum_out=st[:, column:column + 1]).then_inc(s_dst, 1)

            def root(column, n, s_src, s_dst):
                act.wait_ge(s_src, n)
                act.activation(st[:, column:column + 1], st[:, column:column + 1], ACT.Sqrt).then_inc(s_dst, 1)

            def scaled(n, gain, s_src, s_dst):
                act.wait_ge(s_src, n + 1)
                for k in range(KT):
                    last = act.activation(actT[:, k, :], pd[:, k * P:(k + 1) * P], ACT.Copy,
                                          scale=vec[:, COL[gain] + k:COL[gain] + k + 1])
                last.then_inc(s_dst, 1)

            def queries(n):
                act.wait_ge(s_qps, n + 1)
                act.activation(qT[:, :, :].rearrange("p h t -> p (h t)"), pd[:, :], ACT.Copy).then_inc(s_qT, 1)

            def head(n, h):
                if h == 0:
                    act.wait_ge(s_sc, n + 1)
                act.wait_ge(s_topk, n * PH + (h + 1))
                act.activation(sc[:, :, :], ps[:, :, h, :], ACT.Copy).then_inc(s_head, 1)

            def gate_exp(n):
                act.wait_ge(s_sub, n + 1)
                act.activation(ex[:, :, :], ex[:, :, :], ACT.Exp).then_inc(s_exp, 1)

            def ple_gate(n):
                act.wait_ge(s_gps, n + 1)
                act.activation(gt[:, :], pd[:, :], ACT.Sigmoid).then_inc(s_gate, 1)

            def gelu(n):
                act.wait_ge(s_dot, n * GRP + (GRP + UR))
                act.activation(gl[:, :], dots[:, :], ACT.Gelu).then_inc(s_gelu, 1)

            def diagonals(n):
                act.wait_ge(s_coef, n + 1)
                for s in range(GRP):
                    act.wait_ge(s_vmm, n * GRP + (s + 1 + VR - DR))
                    act.activation(dg[s % DR][:, :], ident[:, :], ACT.Copy, scale=coef[:, s:s + 1]).then_inc(s_diag, 1)

            act.sem_inc(s_gelu, 1)
            act.sem_inc(s_diag, 1)
            act.wait_ge(s_w, 16 * 8)
            act.wait_ge(s_ident, 2)
            root(1, 1, s_var, s_rstd)
            scaled(0, "ffn_g", s_ctr, s_cT)
            queries(0)
            for h in range(PH):
                head(0, h)
            gate_exp(0)
            with act.Fori(0, NT) as t:
                for g in range(GROUPS):
                    gelu(t * GROUPS + g)
                    if g == 2:
                        root(1, t + 2, s_var, s_rstd)
                    if g == 6:
                        root(3, t * 2 + 1, s_tvar, s_trstd)
                    if g == 12:
                        root(5, t * 2 + 2, s_tvar, s_trstd)
                    diagonals(t * GROUPS + g)
                    if g == 2:
                        scaled(t + 1, "ffn_g", s_ctr, s_cT)
                    if g == 4:
                        queries(t + 1)
                        square(gt, hh, 2, t + 1, s_hh, s_tsq)
                    if g + 1 in HEAD_AT:
                        head(t + 1, HEAD_AT[g + 1])
                    if g == 6:
                        scaled(t, "ple_g", s_ttr, s_tT)
                    if g == 8:
                        ple_gate(t)
                    if g == 10:
                        square(gt, hh, 4, t + 1, s_h3, s_tsq)
                    if g == 15:
                        gate_exp(t + 1)
            act.wait_ge(s_outd, NT * 16)
            square(gt, hh, 2, NT + 1, s_hh, s_tsq)
            root(3, NT * 2 + 1, s_tvar, s_trstd)
            scaled(NT, "ple_g", s_ttr, s_tT)
            ple_gate(NT)
            square(gt, hh, 4, NT + 1, s_h3, s_tsq)
            root(5, NT * 2 + 2, s_tvar, s_trstd)

        @block.vector
        def _(dve):
            def pinned():
                dve.sem_inc(s_dve, 1)

            def variance(column, n, s_src, s_own, s_dst):
                dve.wait_ge(s_src, n)
                dve.tensor_scalar(st[:, column + 1:column + 2], st[:, column:column + 1], 1.0 / D, RMS_EPS, ALU.mult, ALU.add)\
                    .then_inc(s_own, 1)
                dve.wait_ge(s_own, n)
                dve.reciprocal(st[:, column + 1:column + 2], st[:, column + 1:column + 2]).then_inc(s_dst, 1)

            def front_h(n):
                dve.wait_ge(s_hps, n + 1)
                dve.wait_ge(s_xin, n * 16 + 16)
                dve.tensor_tensor(xin[:, :], pd[:, :], xin[:, :], ALU.add).then_inc(s_h, 1)
                dve.wait_ge(s_h, n + 1)
                pinned()
                dve.tensor_tensor_reduce(gt[:, :], xin[:, :], xin[:, :], 1.0, 0.0, ALU.mult, ALU.add, st[:, 0:1]).then_inc(s_sq, 1)
                variance(0, n + 1, s_sq, s_fv, s_var)

            def front_norm(n):
                dve.wait_ge(s_rstd, n + 1)
                dve.wait_ge(s_hout, n * 16 + 16)
                dve.tensor_scalar(xin[:, :], xin[:, :], st[:, 1:2], None, ALU.mult).then_inc(s_hn, 1)

            def head(n, h):
                link = Link(dve, s_k, n, PH * HEAD_STEPS, start=h * HEAD_STEPS)

                def stage():
                    link.wait()
                    pinned()

                dve.wait_ge(s_head, n * PH + (h + 1))
                pinned()
                for p in range(2):
                    link.mark(dve.max(tv[:, p, 0:KS], sc[:, p, :]))
                stage()
                for p in range(2):
                    link.mark(dve.max_index(ti[:, p, 0:KS], tv[:, p, 0:KS], sc[:, p, :]))
                    link.mark(dve.match_replace(sc2[:, p, :], tv[:, p, 0:KS], sc[:, p, :], LOWEST))
                stage()
                dve.sem_inc(s_topk, 1)
                for p in range(2):
                    link.mark(dve.max(tv[:, p, KS:], sc2[:, p, :]))
                stage()
                for p in range(2):
                    link.mark(dve.max_index(ti[:, p, KS:], tv[:, p, KS:], sc2[:, p, :]))
                link.mark(dve.tensor_tensor(cand[:, :, :], tv[:, 0, :].unsqueeze(2).to_broadcast([P, TOPK, TOPK]),
                                            tv[:, 1, :].unsqueeze(1).to_broadcast([P, TOPK, TOPK]), ALU.add))
                stage()
                flat = cand[:, :, :].rearrange("p a b -> p (a b)")
                link.mark(dve.tensor_copy(ix[:, :, h, :], ti[:, :, :]))
                link.mark(dve.max(best[:, h, 0:KS], flat))
                stage()
                link.mark(dve.max_index(pos[:, h, 0:KS], best[:, h, 0:KS], flat))
                link.mark(dve.match_replace(cand2[:, :], best[:, h, 0:KS], flat, LOWEST))
                stage()
                link.mark(dve.max(best[:, h, KS:], cand2[:, :]))
                stage()
                link.mark(dve.max_index(pos[:, h, KS:], best[:, h, KS:], cand2[:, :]))
                assert link.k == HEAD_STEPS, link.k

            def select(n, q):
                link = Link(dve, s_fin, n, 2 * SELECT_STEPS, start=q * SELECT_STEPS)
                hs = slice(q * (PH // 2), (q + 1) * (PH // 2))
                dve.wait_ge(s_k, n * (PH * HEAD_STEPS) + (q + 1) * (PH // 2) * HEAD_STEPS)
                for p in range(2):
                    op, by = ((ALU.logical_shift_right, 4), (ALU.bitwise_and, TOPK - 1))[p]
                    link(dve.tensor_scalar(half[:, hs, :], pos[:, hs, :], by, None, op))
                    link(dve.tensor_copy(halff[:, hs, :], half[:, hs, :]))
                    rows = oh[:, :, :].rearrange("p k t -> p (k t)").rearrange("p (h j c) -> p h j c", h=PH // 2, j=TOPK)
                    shape = [P, PH // 2, TOPK, TOPK]
                    link(dve.tensor_tensor(rows, halff[:, hs, :].unsqueeze(3).to_broadcast(shape),
                                           iot[:, :].unsqueeze(1).unsqueeze(1).to_broadcast(shape), ALU.is_equal))
                    link(dve.tensor_tensor(rows, rows, ix[:, p, hs, :].unsqueeze(2).to_broadcast(shape), ALU.mult))
                    link(dve.tensor_reduce(pick[:, p, hs, :], rows, AX.X, ALU.add))

            def indices(n):
                dve.wait_ge(s_icp, n)
                dve.scalar_tensor_tensor(out=idx_n[:, :], in0=pick[:, 0, :, :].rearrange("p h j -> p (h j)"),
                                         scalar=float(NKEY), in1=pick[:, 1, :, :].rearrange("p h j -> p (h j)"),
                                         op0=ALU.mult, op1=ALU.add).then_inc(s_in, 1)

            def less_max(n):
                dve.wait_ge(s_k, (n + 1) * (PH * HEAD_STEPS))
                dve.tensor_tensor(ex[:, :, :], best[:, :, :], best[:, :, 0:1].to_broadcast([P, PH, TOPK]),
                                  ALU.subtract).then_inc(s_sub, 1)

            def make_c(n):
                dve.wait_ge(s_hn, n + 1)
                dve.tensor_tensor(c[:, :], xin[:, :], g_ffn[:, :], ALU.mult).then_inc(s_cur, 1)
                dve.wait_ge(s_cur, n + 1)
                pinned()

            def make_gates(n):
                link = Link(dve, s_gsum, n, 3)
                dve.wait_ge(s_exp, n + 1)
                link(dve.tensor_reduce(ssum[:, :], ex[:, :, :], AX.X, ALU.add))
                link(dve.reciprocal(ssum[:, :], ssum[:, :]))
                link(dve.tensor_tensor(gates[:, :].rearrange("p (h j) -> p h j", h=PH), ex[:, :, :],
                                       ssum[:, :].unsqueeze(2).to_broadcast([P, PH, TOPK]), ALU.mult))

            def sum_read(n):
                dve.wait_ge(s_hhin, n * 16 + 16)
                dve.wait_ge(s_vmm, n * NSEL + VR)
                dve.wait_ge(s_zero, n + 1)
                dve.tensor_tensor(hh[:, :], hh[:, :], acc[:, :], ALU.add).then_inc(s_hh, 1)

            def tail_norm(n):
                dve.wait_ge(s_trstd, n * 2 + 1)
                dve.tensor_scalar(gt[:, :], hh[:, :], st[:, 3:4], None, ALU.mult).then_inc(s_tn, 1)

            def tail_add(n):
                dve.wait_ge(s_pps, n + 1)
                dve.wait_ge(s_gate, n + 1)
                dve.tensor_tensor(gt[:, :], gt[:, :], pd[:, :], ALU.mult).then_inc(s_gp, 1)
                dve.wait_ge(s_gp, n + 1)
                dve.tensor_tensor(hh[:, :], hh[:, :], gt[:, :], ALU.add).then_inc(s_h3, 1)

            def tail_out(n):
                dve.wait_ge(s_trstd, n * 2 + 2)
                dve.scalar_tensor_tensor(out=gt[:, :], in0=hh[:, :], scalar=st[:, 5:6], in1=g_fin[:, :],
                                         op0=ALU.mult, op1=ALU.mult).then_inc(s_out, 1)

            def group_dots(n):
                dve.wait_ge(s_gelu, n + 1)
                for s in range(GRP):
                    dve.wait_ge(s_u[s % UR], n * (16 * GRP // UR) + 16 * (s // UR + 1))
                    if s == 0:
                        pinned()
                    dve.tensor_tensor_reduce(u[s % UR][:, :], u[s % UR][:, :], c[:, :], 1.0, 0.0, ALU.mult, ALU.add,
                                             dots[:, s:s + 1]).then_inc(s_dot, 1)

            def coefficients(n, g):
                dve.wait_ge(s_gelu, n + 2)
                dve.wait_ge(s_diag, n * GRP + 1)
                dve.tensor_tensor(coef[:, :], gl[:, :], gates[:, g * GRP:(g + 1) * GRP], ALU.mult).then_inc(s_coef, 1)

            dve.sem_inc(s_dot, UR)
            dve.sem_inc(s_topk, 1)
            dve.wait_ge(s_w, 16 * 8)
            dve.wait_ge(s_const, 2)
            dve.wait_ge(s_iota, 1)
            front_h(0)
            front_norm(0)
            for h in range(PH):
                head(0, h)
            less_max(0)
            for q in range(2):
                select(0, q)
            indices(0)
            with dve.Fori(0, NT) as t:
                make_c(t)
                for g in range(GROUPS):
                    n = t * GROUPS + g
                    group_dots(n)
                    if g == 0:
                        sum_read(t)
                        make_gates(t)
                    coefficients(n, g)
                    if g == 1:
                        front_h(t + 1)
                    if g == 2:
                        front_norm(t + 1)
                    if g == 5:
                        variance(2, t * 2 + 1, s_tsq, s_tv, s_tvar)
                    if g == 6:
                        tail_norm(t)
                    if g in HEAD_AT:
                        head(t + 1, HEAD_AT[g])
                    if g == 10:
                        tail_add(t)
                        select(t + 1, 0)
                    if g == 11:
                        variance(4, t * 2 + 2, s_tsq, s_tv, s_tvar)
                    if g == 12:
                        tail_out(t)
                    if g == 15:
                        less_max(t + 1)
                        select(t + 1, 1)
                        indices(t + 1)
            sum_read(NT)
            variance(2, NT * 2 + 1, s_tsq, s_tv, s_tvar)
            tail_norm(NT)
            tail_add(NT)
            variance(4, NT * 2 + 2, s_tsq, s_tv, s_tvar)
            tail_out(NT)


FROM_PROJECTION = dict(ident=[P, P], vec=[P, NVEC], cw=[P, TAPS * CONV_TILES], zs=[P, RWKV_TILES, T],
                       cv=[P, CONV_TILES, T])
FROM_PREPARATION = dict(qq=[P, PAIRS, T], bb=[P, PAIRS, T], gg=[P, PAIRS, T], bv=[P, PAIRS, T],
                        pc=[P, PAIRS, NC], headones=[P, P])


def program(nc, io, out):
    dram = {"gates": nc.dram_tensor("mixer_gates", (GATE_TILES, P, T), F32).ap(),
            "mix": nc.dram_tensor("mixed", (NT, P, KT, P), F32).ap(),
            "h": nc.dram_tensor("h_after_mixer", (NT, P, D), F32).ap(),
            "out": out}
    with ExitStack() as ctx:
        sb = {name: ctx.enter_context(nc.sbuf_tensor(name, shape, F32)) for name, shape in FROM_PROJECTION.items()}
        project_in(nc, io, sb, dram)
        for name, shape in FROM_PREPARATION.items():
            sb[name] = ctx.enter_context(nc.sbuf_tensor(name, shape, F32))
        prepare_recurrence(nc, io, sb)
        recurrence(nc, io, sb)
        mix(nc, io, sb, dram)
    experts(nc, io, dram)


VEC_INPUTS = dict(mu="rwkv_mu", w0="rwkv_w0", a0="rwkv_a0", k_k="rwkv_k_k", k_a="rwkv_k_a", r_k="rwkv_r_k",
                  lnx_g="rwkv_lnx_g", lnx_b="rwkv_lnx_b", dw_b="conv_dw_b", ln_g="conv_ln_g", ln_b="conv_ln_b",
                  mix_g="norm_mix_g", ffn_g="norm_ffn_g", ple_g="ple_norm_g")


def column_tiles(w):
    k, n = w.shape
    return w.reshape(k // P, P, n // P, P).transpose(2, 1, 0, 3)


def row_tiles(w):
    k, n = w.shape
    return w.reshape(k // P, P, n).transpose(1, 0, 2)


def layout(a):
    vec = np.concatenate([a[VEC_INPUTS[name]][0].reshape(-1, P) for name, _ in VECS]).T
    return {
        "x": a["x"][0].reshape(NT, P, D),
        "xT": a["x"][0].T.reshape(KT, P, T),
        "w_in": column_tiles(a["w_in"][0]),
        "vec": vec,
        "dw_w": a["conv_dw_w"][0].reshape(-1, P).T,
        "wa_up": np.concatenate([a["rwkv_w_up"][0], a["rwkv_a_up"][0]], 0),
        "g_up": a["rwkv_g_up"][0],
        "w_r": column_tiles(a["rwkv_w_o"][0]),
        "w_c": column_tiles(a["conv_w_o"][0]),
        "w_out": row_tiles(a["w_out"][0]),
        "w_q": row_tiles(a["peer_w_q"][0]),
        "w_ple": row_tiles(a["ple_w_gate"][0]),
        "w_proj": row_tiles(a["ple_w_proj"][0]),
        "keys": a["peer_sub_keys"][0].transpose(1, 3, 0, 2).reshape(P, PH, NKEY),
        "g_ffn": a["norm_ffn_g"],
        "g_fin": a["final_norm_g"][None],
        "pT": a["p"][0, 0].reshape(NT, P, PLE // P, P).transpose(0, 3, 2, 1),
        "u_tab": a["peer_u"][0],
        "v_tab": a["peer_v"][0],
    }


def kernel(**inputs):
    import concourse.bacc as _bacc
    from concourse.bass_utils import run_bass_kernel_spmd as _run

    nc = _bacc.Bacc("TRN2", target_bir_lowering=False, num_devices=1)
    arrays, io = {}, {}
    for name, a in layout({name: np.asarray(a) for name, a in inputs.items()}).items():
        a = np.ascontiguousarray(a)
        arrays[f"in_{name}"] = a
        io[name] = nc.dram_tensor(f"in_{name}", a.shape, mybir.dt.from_np(a.dtype), kind="ExternalInput").ap()
    out = nc.dram_tensor("out_0", (1, T, D), F32, kind="ExternalOutput").ap()
    program(nc, io, out.rearrange("a (n p) d -> (a n) p d", p=P))
    result = _run(nc, [arrays], core_ids=[0])
    return result.results[0]["out_0"]
```

```python
from contextlib import ExitStack, contextmanager

import numpy as np

import concourse.bass as bass
from concourse import mybir

F32 = mybir.dt.float32
U32 = mybir.dt.uint32
ALU = mybir.AluOpType
ACT = mybir.ActivationFunctionType
AX = mybir.AxisListType

P = 128
D = 1024
T = 1024
KT = D // P
NT = T // P
HALF = 512
NH = T // HALF

HEADS, HD = 8, 64
RW = HEADS * HD
PAIRS = RW // P
RWKV_TILES = (3 * RW + 64 + 64 + 128) // P
RWKV_COLS = RWKV_TILES * P
CONV_W = 512
CONV_TILES = CONV_W // P
TAPS = 31
PADT = TAPS - 1
GATE_TILES = 2 * D // P
GN_EPS, LN_EPS, RMS_EPS = 64e-5, 1e-5, 1e-6
CH = 64
NC = T // CH
DECAY = float(np.exp(-0.5))

PH, NKEY, PHALF, TOPK = 8, 128, 64, 16
NSEL = PH * TOPK
PLE = 256
LOWEST = -3.0e38

VECS = [("mu", RWKV_TILES), ("w0", PAIRS), ("a0", PAIRS), ("k_k", PAIRS), ("k_a", PAIRS),
        ("r_k", PAIRS), ("lnx_g", PAIRS), ("lnx_b", PAIRS), ("dw_b", CONV_TILES),
        ("ln_g", CONV_TILES), ("ln_b", CONV_TILES), ("mix_g", KT), ("ffn_g", KT), ("ple_g", KT)]
COL, _n = {}, 0
for _name, _rows in VECS:
    COL[_name] = _n
    _n += _rows
NVEC = _n


def ds(start, size):
    return bass.ds(start, size)


def at(tile, i):
    return tile[:, ds(i, 1), :].rearrange("p a t -> p (a t)")


def one(tensor, i):
    if isinstance(i, int):
        return tensor[i]
    axes = "abcd"[:len(tensor.shape) - 1]
    return tensor[ds(i, 1)].rearrange(f"i {' '.join(axes)} -> (i {axes[0]}) {' '.join(axes[1:])}")


def col(tile, i):
    return tile[:, ds(i, 1)]


@contextmanager
def semaphores(nc):
    taken = []

    def sem(name):
        taken.append(nc.alloc_semaphore(name))
        return taken[-1]

    yield sem
    nc.clear_and_free_semaphores(taken)
    nc.all_engine_barrier()


class Link:

    def __init__(self, eng, sem, turn=0, each=0, start=0):
        self.eng, self.sem, self.turn, self.each, self.start, self.k = eng, sem, turn, each, start, 0

    def value(self, k):
        return self.turn * self.each + (self.start + k) if self.each else self.start + k

    def mark(self, ins):
        self.k += 1
        ins.then_inc(self.sem, 1)
        return self.k

    def wait(self, k=None):
        self.eng.wait_ge(self.sem, self.value(self.k if k is None else k))

    def __call__(self, ins):
        self.mark(ins)
        self.wait()


def bcast(ap, axis, n):
    return ap.unsqueeze(axis).to_broadcast([*ap.shape[:axis], n, *ap.shape[axis:]])


def project_in(nc, io, sb, dram, aT, small):
    with ExitStack() as ctx:
        def buf(name, shape, dt=F32):
            return ctx.enter_context(nc.sbuf_tensor(name, shape, dt))

        sem = ctx.enter_context(semaphores(nc))

        ident, vec, cw, zs, cv = sb["ident"], sb["vec"], sb["cw"], sb["zs"], sb["cv"]
        ones = buf("a_ones", [P, P])
        sq = small[:, 0:2, :]
        rstd = buf("a_rstd", [P, T])
        w = [small[:, 2 + i, :].rearrange("p (k c) -> p k c", c=P) for i in range(4)]
        zp = [buf(f"a_zp{i}", [P, T + 1]) for i in range(2)]
        dz = [buf(f"a_dz{i}", [P, T]) for i in range(2)]
        cg = buf("a_cg", [P, T])
        hp = buf("a_hp", [P, CONV_TILES, PADT + T])
        gt = [small[:, 6 + i, :] for i in range(2)]
        ps = [ctx.enter_context(nc.psum_tensor(f"a_ps{i}", [P, T], F32)) for i in range(4)]

        s_ident = sem("a_identity_made")
        s_ones = sem("a_ones_made")
        s_vec = sem("a_constants_in")
        s_x = [sem(f"a_x_in{i}") for i in range(KT)]
        s_sq = sem("a_x_squared")
        s_sum = sem("a_squares_summed")
        s_var = sem("a_variance_inverted")
        s_rstd = sem("a_rstd_ready")
        s_aT = sem("a_aT_ready")
        s_w = [sem(f"a_w_in{i}") for i in range(4)]
        s_mm = sem("a_z_tile_in_psum")
        s_free = [sem(f"a_psum_tile_free{i}") for i in range(4)]
        s_pad = sem("a_pads_zeroed")
        s_zcp = sem("a_z_tile_copied")
        s_dz = sem("a_z_difference_ready")
        s_sig = sem("a_conv_gate_ready")
        s_h = sem("a_conv_input_ready")
        s_tap = sem("a_conv_tap_done")
        s_dve = sem("a_vector_step")
        s_gate = sem("a_mixer_gate_ready")
        s_gout = [sem(f"a_mixer_gate_out{i}") for i in range(2)]

        TILES = RWKV_TILES + 2 * CONV_TILES + GATE_TILES
        cols = [m * P for m in range(RWKV_TILES)]
        for i in range(CONV_TILES):
            cols += [RWKV_COLS + i * P, RWKV_COLS + CONV_W + i * P]
        gates_at = RWKV_COLS + 2 * CONV_W
        win = io["w_in"]
        block = ctx.enter_context(nc.Block())

        @block.gpsimd
        def _(pool):
            pool.memset(ident[:, :], 0.0).then_inc(s_ident, 1)
            pool.memset(ones[:, :], 1.0).then_inc(s_ones, 1)
            for i in range(2):
                pool.memset(zp[i][:, 0:1], 0.0).then_inc(s_pad, 1)
            pool.memset(hp[:, :, 0:PADT], 0.0).then_inc(s_pad, 1)
            pool.wait_ge(s_ident, 1)
            pool.affine_select(out=ident[:, :], in_=ident[:, :], compare_op=ALU.not_equal, fill=1.0,
                               base=0, pattern=[[-1, P]], channel_multiplier=1).then_inc(s_ident, 1)

        @block.sync
        def _(sp):
            for k in range(KT):
                sp.dma_start(aT[:, k, :], io["xT"][k]).then_inc(s_x[k], 16)
            sp.dma_start(vec[:, :], io["vec"]).then_inc(s_vec, 16)
            sp.dma_start(cw[:, :], io["dw_w"]).then_inc(s_vec, 16)
            for m in range(4):
                sp.dma_start(w[m][:, :, :], win[cols[m] // P]).then_inc(s_w[m], 16)
            for m in range(4, len(cols)):
                sp.wait_ge(s_mm, m - 3)
                sp.dma_start(w[m % 4][:, :, :], win[cols[m] // P]).then_inc(s_w[m % 4], 16)
            first = len(cols)
            with sp.Fori(0, GATE_TILES // 4) as q:
                for i in range(4):
                    slot = (first + i) % 4
                    sp.wait_ge(s_mm, q * 4 + (first + i - 3))
                    sp.dma_start(w[slot][:, :, :], win[ds(q * 4 + (gates_at // P + i), 1)].rearrange("a p k c -> (a p) k c"))\
                        .then_inc(s_w[slot], 16)

        @block.tensor
        def _(pe):
            pe.wait_ge(s_ones, 1)
            for k in range(KT):
                pe.wait_ge(s_sq, k + 1)
                for h in range(NH):
                    last = pe.matmul(ps[0][:, h * HALF:(h + 1) * HALF], ones[:, :], sq[:, k % 2, h * HALF:(h + 1) * HALF],
                                     start=(k == 0), stop=(k == KT - 1))
                last.then_inc(s_sum, 1)
            pe.wait_ge(s_aT, KT)

            def z_tile(m, q):
                pe.wait_ge(s_w[m % 4], q * 16 + 16 * (m // 4 + 1))
                pe.wait_ge(s_free[m % 4], q + (m // 4 + 1))
                for h in range(NH):
                    for k in range(KT):
                        last = pe.matmul(ps[m % 4][:, h * HALF:(h + 1) * HALF], w[m % 4][:, k, :],
                                         aT[:, k, h * HALF:(h + 1) * HALF], start=(k == 0), stop=(k == KT - 1))
                last.then_inc(s_mm, 1)

            with pe.Fori(0, TILES // 4) as q:
                for m in range(4):
                    z_tile(m, q)
            for m in range(TILES // 4 * 4, TILES):
                z_tile(m, 0)

        @block.scalar
        def _(act):
            for i in range(4):
                act.sem_inc(s_free[i], 1)
            for k in range(KT):
                act.wait_ge(s_x[k], 16)
                if k >= 2:
                    act.wait_ge(s_sum, k - 1)
                act.activation(sq[:, k % 2, :], aT[:, k, :], ACT.Square).then_inc(s_sq, 1)
            act.wait_ge(s_var, 1)
            act.activation(rstd[:, :], rstd[:, :], ACT.Sqrt).then_inc(s_rstd, 1)

            def z_copy(q, m):
                act.wait_ge(s_mm, q * 4 + (m + 1))
                act.wait_ge(s_dz, q * 4 + (m + 1))
                act.activation(zp[m % 2][:, 1:T + 1], ps[m % 4][:, :], ACT.Copy).then_inc(s_zcp, 1)
                act.wait_ge(s_zcp, q * 4 + (m + 1))
                act.sem_inc(s_free[m % 4], 1)

            with act.Fori(0, RWKV_TILES // 4) as q:
                for m in range(4):
                    z_copy(q, m)
            for m in range(RWKV_TILES // 4 * 4, RWKV_TILES):
                z_copy(0, m)
            for i in range(CONV_TILES):
                m = RWKV_TILES + 2 * i
                act.wait_ge(s_mm, m + 2)
                if i:
                    act.wait_ge(s_h, i)
                act.activation(cg[:, :], ps[(m + 1) % 4][:, :], ACT.Sigmoid).then_inc(s_sig, 1)
            first = RWKV_TILES + 2 * CONV_TILES
            with act.Fori(0, GATE_TILES // 4) as q:
                for i in range(4):
                    m = first + i
                    act.wait_ge(s_mm, q * 4 + (m + 1))
                    act.wait_ge(s_gout[i % 2], q * 32 + 16 * (i // 2 + 1))
                    act.activation(gt[i % 2][:, :], ps[m % 4][:, :], ACT.Sigmoid).then_inc(s_gate, 1)
                    act.wait_ge(s_gate, q * 4 + (i + 1))
                    act.sem_inc(s_free[m % 4], 1)
                    act.dma_start(dram["gates"][ds(q * 4 + i, 1), :, :].rearrange("a p t -> (a p) t"),
                                  gt[i % 2][:, :]).then_inc(s_gout[i % 2], 16)
            for i in range(2):
                act.wait_ge(s_gout[i], 16 * (GATE_TILES // 2 + 1))

        @block.vector
        def _(dve):
            dve.sem_inc(s_dz, 2)
            for i in range(2):
                dve.sem_inc(s_gout[i], 16)
            link = Link(dve, s_dve)
            dve.wait_ge(s_sum, KT)
            link(dve.tensor_scalar(rstd[:, :], ps[0][:, :], 1.0 / D, RMS_EPS, ALU.mult, ALU.add))
            link(dve.reciprocal(rstd[:, :], rstd[:, :]))
            dve.sem_inc(s_var, 1)
            dve.wait_ge(s_rstd, 1)
            dve.wait_ge(s_vec, 32)
            for k in range(KT):
                g = vec[:, COL["mix_g"] + k:COL["mix_g"] + k + 1]
                dve.scalar_tensor_tensor(out=aT[:, k, :], in0=aT[:, k, :], scalar=g, in1=rstd[:, :],
                                         op0=ALU.mult, op1=ALU.mult).then_inc(s_aT, 1)

            def z_shift(q, m):
                dve.wait_ge(s_zcp, q * 4 + (m + 1))
                a = dz[m % 2]
                dve.tensor_tensor(a[:, :], zp[m % 2][:, 0:T], zp[m % 2][:, 1:T + 1], ALU.subtract).then_inc(s_tap, 1)
                dve.wait_ge(s_tap, q * 4 + (m + 1))
                dve.scalar_tensor_tensor(out=at(zs, q * 4 + m),
                                         in0=a[:, :],
                                         scalar=col(vec, q * 4 + (COL["mu"] + m)),
                                         in1=zp[m % 2][:, 1:T + 1], op0=ALU.mult, op1=ALU.add).then_inc(s_dz, 1)

            dve.wait_ge(s_pad, 3)
            with dve.Fori(0, RWKV_TILES // 4) as q:
                for m in range(4):
                    z_shift(q, m)
                    dve.wait_ge(s_dz, q * 4 + (m + 3))
            for m in range(RWKV_TILES // 4 * 4, RWKV_TILES):
                z_shift(0, m)
                dve.wait_ge(s_dz, m + 3)
            for i in range(CONV_TILES):
                m = RWKV_TILES + 2 * i
                dve.wait_ge(s_sig, i + 1)
                dve.tensor_tensor(hp[:, i, PADT:PADT + T], ps[m % 4][:, :], cg[:, :], ALU.mult).then_inc(s_h, 1)
                dve.wait_ge(s_h, i + 1)
                for k in range(2):
                    dve.sem_inc(s_free[(m + k) % 4], 1)
            taps = RWKV_TILES
            with dve.Fori(0, CONV_TILES) as i:
                link = Link(dve, s_tap, i, TAPS, start=taps)

                def tap(j):
                    return col(cw, i + j * CONV_TILES)

                hin = at(hp, i)
                acc = at(cv, i)
                link(dve.tensor_scalar(acc, hin[:, 0:T], tap(0), col(vec, i + COL["dw_b"]), ALU.mult, ALU.add))
                for j in range(1, TAPS):
                    link(dve.scalar_tensor_tensor(out=acc, in0=hin[:, j:j + T], scalar=tap(j), in1=acc,
                                                  op0=ALU.mult, op1=ALU.add))




def prepare_recurrence(nc, io, sb):
    with ExitStack() as ctx:
        def buf(name, shape, dt=F32):
            return ctx.enter_context(nc.sbuf_tensor(name, shape, dt))

        sem = ctx.enter_context(semaphores(nc))

        vec, zs, cv = sb["vec"], sb["zs"], sb["cv"]
        qq, bb, gg, bv, pc = sb["qq"], sb["bb"], sb["gg"], sb["bv"], sb["pc"]
        wa_up = buf("b_wa_up", [P, RW])
        g_up = buf("b_g_up", [P, RW])
        headones = sb["headones"]
        ones = buf("b_ones", [P, P])
        keep = buf("b_keep", [P, T])
        kk = buf("b_kk", [P, T])
        sq = buf("b_sq", [P, T])
        nrm = buf("b_nrm", [P, T])
        am = buf("b_am", [P, T])
        rk = buf("b_rk", [P, T])
        run = buf("b_run", [P, T])
        bef = buf("b_bef", [P, T])
        dec = buf("b_dec", [P, T])
        inv = buf("b_inv", [P, T])
        ps = [ctx.enter_context(nc.psum_tensor(f"b_ps{i}", [P, T], F32)) for i in range(4)]

        s_const = sem("b_constants_made")
        s_up = sem("b_up_weights_in")
        s_lora = sem("b_lora_inputs_ready")
        s_wmm, s_amm, s_gmm = sem("b_w_in_psum"), sem("b_a_in_psum"), sem("b_g_in_psum")
        s_w, s_a, s_g = sem("b_w_ready"), sem("b_a_ready"), sem("b_g_ready")
        s_kk, s_sq, s_ssum = sem("b_kk_raw"), sem("b_kk_squared"), sem("b_kk_square_sum")
        s_nrm, s_rn = sem("b_kk_norm_inverted"), sem("b_kk_norm_ready")
        s_rk, s_rsum, s_bv = sem("b_rk_ready"), sem("b_bonus_sum"), sem("b_bonus_ready")
        s_run, s_bef, s_exp = sem("b_running_sum"), sem("b_sum_before"), sem("b_exponentials")
        s_used = sem("b_exponentials_used")
        s_dve = sem("b_vector_step")
        s_mean, s_diff, s_dsq = sem("b_conv_mean"), sem("b_conv_centred"), sem("b_conv_squared")
        s_var, s_vinv, s_rstd = sem("b_conv_variance"), sem("b_conv_variance_inverted"), sem("b_conv_rstd")
        s_nc, s_silu = sem("b_conv_normed"), sem("b_conv_silu")
        block = ctx.enter_context(nc.Block())

        def vcol(name, i, rows=slice(0, P)):
            return vec[rows, COL[name] + i:COL[name] + i + 1]

        @block.sync
        def _(sp):
            sp.dma_start(wa_up[:, :], io["wa_up"]).then_inc(s_up, 16)
            sp.dma_start(g_up[:, :], io["g_up"]).then_inc(s_up, 16)

        @block.gpsimd
        def _(pool):
            pool.memset(keep[:, :], 1.0).then_inc(s_const, 1)
            pool.memset(ones[:, :], 1.0).then_inc(s_const, 1)
            pool.memset(headones[:, :], 0.0).then_inc(s_const, 1)
            pool.wait_ge(s_const, 3)
            pool.memset(keep[:, :].rearrange("p (c t) -> p c t", t=CH)[:, :, 0:1], 0.0).then_inc(s_const, 1)
            for e in range(2):
                pool.wait_ge(s_const, 4 + e)
                pool.memset(headones[e * HD:(e + 1) * HD, e * HD:(e + 1) * HD], 1.0).then_inc(s_const, 1)

        @block.tensor
        def _(pe):
            pe.wait_ge(s_up, 32)
            pe.wait_ge(s_lora, 2)
            for i in range(PAIRS):
                c = slice(i * P, (i + 1) * P)
                if i:
                    pe.wait_ge(s_w, i)
                for h in range(NH):
                    t = slice(h * HALF, (h + 1) * HALF)
                    last = pe.matmul(ps[0][:, t], wa_up[0:64, c], zs[0:64, 12, t], start=True, stop=True)
                last.then_inc(s_wmm, 1)
                if i:
                    pe.wait_ge(s_a, i)
                for h in range(NH):
                    t = slice(h * HALF, (h + 1) * HALF)
                    last = pe.matmul(ps[1][:, t], wa_up[64:P, c], zs[64:P, 12, t], start=True, stop=True)
                last.then_inc(s_amm, 1)
                if i:
                    pe.wait_ge(s_nrm, i)
                for h in range(NH):
                    t = slice(h * HALF, (h + 1) * HALF)
                    last = pe.matmul(ps[2][:, t], g_up[:, c], zs[:, 13, t], start=True, stop=True)
                last.then_inc(s_gmm, 1)
                pe.wait_ge(s_const, 6)
                pe.wait_ge(s_sq, i + 1)
                pe.wait_ge(s_g, i + 1)
                for h in range(NH):
                    t = slice(h * HALF, (h + 1) * HALF)
                    last = pe.matmul(ps[2][:, t], headones[:, :], sq[:, t], start=True, stop=True)
                last.then_inc(s_ssum, 1)
                pe.wait_ge(s_rk, i + 1)
                if i:
                    pe.wait_ge(s_bv, i)
                for h in range(NH):
                    t = slice(h * HALF, (h + 1) * HALF)
                    last = pe.matmul(ps[3][:, t], headones[:, :], rk[:, t], start=True, stop=True)
                last.then_inc(s_rsum, 1)
            pe.wait_ge(s_w, PAIRS)
            for i in range(CONV_TILES):
                for h in range(NH):
                    t = slice(h * HALF, (h + 1) * HALF)
                    last = pe.matmul(ps[0][:, t], ones[:, :], cv[:, i, t], start=(i == 0), stop=(i == CONV_TILES - 1),
                                     skip_group_check=True)
            last.then_inc(s_mean, 1)
            pe.wait_ge(s_a, PAIRS)
            for i in range(CONV_TILES):
                pe.wait_ge(s_dsq, i + 1)
                for h in range(NH):
                    t = slice(h * HALF, (h + 1) * HALF)
                    last = pe.matmul(ps[1][:, t], ones[:, :], (sq, rk)[i % 2][:, t], start=(i == 0), stop=(i == CONV_TILES - 1),
                                     skip_group_check=True)
                last.then_inc(s_var, 1)

        @block.scalar
        def _(act):
            act.activation(zs[0:64, 12, :], zs[0:64, 12, :], ACT.Tanh).then_inc(s_lora, 1)
            act.activation(zs[:, 13, :], zs[:, 13, :], ACT.Sigmoid).then_inc(s_lora, 1)
            for i in range(PAIRS):
                act.wait_ge(s_wmm, i + 1)
                act.activation(qq[:, i, :], ps[0][:, :], ACT.Sigmoid, bias=vcol("w0", i)).then_inc(s_w, 1)
                act.wait_ge(s_amm, i + 1)
                act.activation(bb[:, i, :], ps[1][:, :], ACT.Sigmoid, bias=vcol("a0", i)).then_inc(s_a, 1)
                act.wait_ge(s_gmm, i + 1)
                act.activation(gg[:, i, :], ps[2][:, :], ACT.Copy).then_inc(s_g, 1)
                act.wait_ge(s_kk, i + 1)
                if i:
                    act.wait_ge(s_ssum, i)
                act.activation(sq[:, :], kk[:, :], ACT.Square).then_inc(s_sq, 1)
                act.wait_ge(s_bef, i + 1)
                if i:
                    act.wait_ge(s_used, i)
                act.activation(dec[:, :], run[:, :], ACT.Exp, scale=-DECAY).then_inc(s_exp, 1)
                act.activation(inv[:, :], run[:, :], ACT.Exp, scale=DECAY).then_inc(s_exp, 1)
                act.activation(bef[:, :], bef[:, :], ACT.Exp, scale=-DECAY).then_inc(s_exp, 1)
                act.wait_ge(s_nrm, i + 1)
                act.activation(nrm[:, :], nrm[:, :], ACT.Sqrt).then_inc(s_rn, 1)
            for i in range(CONV_TILES):
                act.wait_ge(s_diff, i + 1)
                if i == 0:
                    act.wait_ge(s_ssum, PAIRS)
                if i == 1:
                    act.wait_ge(s_rsum, PAIRS)
                if i >= 2:
                    act.wait_ge(s_var, i - 1)
                act.activation((sq, rk)[i % 2][:, :], cv[:, i, :], ACT.Square).then_inc(s_dsq, 1)
            act.wait_ge(s_vinv, 1)
            act.activation(nrm[:, :], nrm[:, :], ACT.Sqrt).then_inc(s_rstd, 1)
            for i in range(CONV_TILES):
                act.wait_ge(s_nc, i + 1)
                act.activation(cv[:, i, :], cv[:, i, :], ACT.Silu, scale=vcol("ln_g", i), bias=vcol("ln_b", i)).then_inc(s_silu, 1)

        @block.vector
        def _(dve):
            link = Link(dve, s_dve)
            for i in range(PAIRS):
                r, k, v = zs[:, i, :], zs[:, PAIRS + i, :], zs[:, 2 * PAIRS + i, :]
                dve.tensor_scalar(kk[:, :], k, vcol("k_k", i), None, ALU.mult).then_inc(s_kk, 1)
                dve.wait_ge(s_const, 6)
                dve.wait_ge(s_w, i + 1)
                dve.tensor_tensor_scan(run[:, :], keep[:, :], qq[:, i, :], 0.0, ALU.mult, ALU.add).then_inc(s_run, 1)
                dve.wait_ge(s_run, i + 1)
                dve.tensor_tensor(bef[:, :], run[:, :], qq[:, i, :], ALU.subtract).then_inc(s_bef, 1)
                dve.wait_ge(s_a, i + 1)
                link(dve.tensor_scalar(am[:, :], bb[:, i, :], -1.0, vcol("k_a", i), ALU.add, ALU.mult))
                dve.wait_ge(s_kk, i + 1)
                link(dve.scalar_tensor_tensor(out=k, in0=am[:, :], scalar=1.0, in1=k, op0=ALU.add, op1=ALU.mult))
                if i:
                    dve.wait_ge(s_rsum, i)
                dve.scalar_tensor_tensor(out=rk[:, :], in0=r, scalar=vcol("r_k", i), in1=k, op0=ALU.mult,
                                         op1=ALU.mult).then_inc(s_rk, 1)
                dve.wait_ge(s_ssum, i + 1)
                link(dve.tensor_scalar(nrm[:, :], ps[2][:, :], 1e-24, None, ALU.max))
                dve.reciprocal(nrm[:, :], nrm[:, :]).then_inc(s_nrm, 1)
                dve.wait_ge(s_rsum, i + 1)
                dve.tensor_tensor(bv[:, i, :], ps[3][:, :], v, ALU.mult).then_inc(s_bv, 1)
                dve.wait_ge(s_exp, 3 * (i + 1))
                dve.wait_ge(s_rk, i + 1)
                link(dve.tensor_tensor(r, r, dec[:, :], ALU.mult))
                link(dve.tensor_copy(pc[:, i, :], dec[:, :].rearrange("p (c t) -> p c t", t=CH)[:, :, CH - 1]))
                link(dve.tensor_tensor(k, k, inv[:, :], ALU.mult))
                dve.wait_ge(s_rn, i + 1)
                link(dve.tensor_tensor(kk[:, :], kk[:, :], nrm[:, :], ALU.mult))
                link(dve.tensor_tensor(bb[:, i, :], bb[:, i, :], kk[:, :], ALU.mult))
                link(dve.tensor_tensor(bb[:, i, :], bb[:, i, :], inv[:, :], ALU.mult))
                link(dve.scalar_tensor_tensor(out=qq[:, i, :], in0=kk[:, :], scalar=-1.0, in1=bef[:, :], op0=ALU.mult,
                                              op1=ALU.mult))
                dve.sem_inc(s_used, 1)
            dve.wait_ge(s_mean, 1)
            link(dve.tensor_scalar(am[:, :], ps[0][:, :], 1.0 / CONV_W, None, ALU.mult))
            for i in range(CONV_TILES):
                dve.tensor_tensor(cv[:, i, :], cv[:, i, :], am[:, :], ALU.subtract).then_inc(s_diff, 1)
            dve.wait_ge(s_var, CONV_TILES)
            link(dve.tensor_scalar(nrm[:, :], ps[1][:, :], 1.0 / CONV_W, LN_EPS, ALU.mult, ALU.add))
            dve.reciprocal(nrm[:, :], nrm[:, :]).then_inc(s_vinv, 1)
            dve.wait_ge(s_rstd, 1)
            for i in range(CONV_TILES):
                dve.wait_ge(s_diff, i + 1)
                dve.wait_ge(s_dsq, i + 1)
                dve.tensor_tensor(cv[:, i, :], cv[:, i, :], nrm[:, :], ALU.mult).then_inc(s_nc, 1)



MASKS = 16
SUB = 16


def recurrence(nc, io, sb):
    with ExitStack() as ctx:
        def buf(name, shape, dt=F32):
            return ctx.enter_context(nc.sbuf_tensor(name, shape, dt))

        sem = ctx.enter_context(semaphores(nc))

        ident, zs, qq, bb, pc = sb["ident"], sb["zs"], sb["qq"], sb["bb"], sb["pc"]
        U = 2 * PAIRS
        qr = buf("c_qr", [P, PAIRS, 2, 2, CH])
        bk = buf("c_bk", [P, PAIRS, 2, 2, CH])
        vs = buf("c_vs", [P, PAIRS, CH + P])
        gs = buf("c_gs", [P, 2, 2, PAIRS, P])
        bt = buf("c_bt", [P, 2, PAIRS, P])
        xs = buf("c_xs", [P, 2, PAIRS, 2, HD])
        rs = buf("c_rs", [CH, PAIRS, 2, HD])
        st = buf("c_st", [P, PAIRS, 2, HD])
        tmp = buf("c_tmp", [P, PAIRS, HD])
        m_g, m_dt = buf("c_m_g", [P, P]), buf("c_m_dt", [CH, CH])
        m_d, m_e = buf("c_m_d", [CH, CH]), buf("c_m_e", [CH, CH])
        names = ("d", "dt", "e", "z", "d2", "d2t", "ift")
        inv = [{n: buf(f"c_{n}{e}", [CH, U, CH]) for n in names} for e in range(2)]
        pg = [ctx.enter_context(nc.psum_tensor(f"c_pg{e}", [P, 2 * HALF], F32)) for e in range(2)]
        pi = [[ctx.enter_context(nc.psum_tensor(f"c_pi{e}{j}", [P, HALF], F32)) for j in range(2)] for e in range(2)]

        s_pe, s_pool = sem("c_tensor_waits_passed"), sem("c_gpsimd_waits_passed")
        s_mask = sem("c_masks_ready")
        s_ops, s_q, s_r = sem("c_bkv_copied"), sem("c_q_copied"), sem("c_r_copied")
        s_g = sem("c_products_in_psum")
        s_gs = sem("c_products_masked")
        s_i = [sem(f"c_inverse_step{e}") for e in range(2)]
        s_ia = [sem(f"c_inverse_copied{e}") for e in range(2)]
        s_id = [sem(f"c_inverse_added{e}") for e in range(2)]
        s_tr, s_trc = sem("c_turned"), sem("c_turned_copied")
        s_seq = sem("c_chain_step")
        s_cp = sem("c_chain_copied")
        s_y = sem("c_y_copied")
        s_sum, s_st = sem("c_state_summed"), sem("c_state_ready")
        block = ctx.enter_context(nc.Block())

        def pin(eng):
            eng.sem_inc(s_pe if eng.engine == nc.tensor.engine else s_pool, 1)

        def chunks(a):
            return a.rearrange("p i (c t) -> p i c t", t=CH)

        @block.gpsimd
        def _(pool):
            k = 0

            def step(ins):
                nonlocal k
                k += 1
                ins.then_inc(s_mask, 1)
                pool.wait_ge(s_mask, k)

            step(pool.memset(st[:, :, :, :], 0.0))
            step(pool.memset(xs[:, :, :, :, :], 0.0))
            step(pool.memset(vs[:, :, :], 0.0))
            for m in (m_g, m_dt, m_d, m_e):
                step(pool.memset(m[:, :], 1.0))
            step(pool.memset(m_g[0:CH, 0:CH], 0.0))
            step(pool.affine_select(out=m_g[0:CH, CH:P], in_=m_g[0:CH, CH:P], compare_op=ALU.is_ge, fill=0.0, base=0,
                                    pattern=[[1, CH]], channel_multiplier=-1))
            step(pool.affine_select(out=m_g[CH:P, 0:CH], in_=m_g[CH:P, 0:CH], compare_op=ALU.is_gt, fill=0.0, base=0,
                                    pattern=[[1, CH]], channel_multiplier=-1))
            step(pool.affine_select(out=m_g[CH:P, CH:P], in_=m_g[CH:P, CH:P], compare_op=ALU.is_ge, fill=0.0, base=0,
                                    pattern=[[1, CH]], channel_multiplier=-1))
            NB = CH // SUB

            def blocks(m):
                return m[:, :].rearrange("p (b j) -> p b j", j=SUB)

            step(pool.affine_select(out=blocks(m_dt), in_=blocks(m_dt), compare_op=ALU.is_gt, fill=0.0, base=0,
                                    pattern=[[SUB, NB], [1, SUB]], channel_multiplier=-1))
            step(pool.affine_select(out=blocks(m_dt), in_=blocks(m_dt), compare_op=ALU.is_ge, fill=0.0, base=0,
                                    pattern=[[-SUB, NB], [0, SUB]], channel_multiplier=1))
            step(pool.affine_select(out=blocks(m_d), in_=blocks(m_d), compare_op=ALU.is_gt, fill=0.0, base=0,
                                    pattern=[[-SUB, NB], [-1, SUB]], channel_multiplier=1))
            step(pool.affine_select(out=blocks(m_d), in_=blocks(m_d), compare_op=ALU.is_ge, fill=0.0, base=SUB - 1,
                                    pattern=[[SUB, NB], [0, SUB]], channel_multiplier=-1))
            step(pool.affine_select(out=blocks(m_e), in_=blocks(m_e), compare_op=ALU.is_ge, fill=0.0, base=-SUB,
                                    pattern=[[-SUB, NB], [0, SUB]], channel_multiplier=1))
            masks = k
            assert masks == MASKS
            with pool.Fori(0, NT) as t:
                pool.wait_ge(s_tr, t * 2 + 1)
                pin(pool)
                tok = ds(t * P, P)
                pool.tensor_copy(bk[:, :, :, 0, :], chunks(bb[:, :, tok])).then_inc(s_ops, 1)
                pool.tensor_copy(bk[:, :, :, 1, :], chunks(zs[:, PAIRS:2 * PAIRS, tok])).then_inc(s_ops, 1)
                pool.tensor_copy(vs[:, :, CH:], zs[:, 2 * PAIRS:3 * PAIRS, tok]).then_inc(s_ops, 1)

        @block.tensor
        def _(pe):
            pe.sem_inc(s_seq, 1)
            pe.sem_inc(s_tr, 1)
            with pe.Fori(0, NT) as t:
                def inverse(e, step, *products):
                    for out, a, b in products:
                        for u in range(U):
                            o = pi[e][out][0:CH, u * CH:(u + 1) * CH]
                            if b is None:
                                last = pe.transpose(o, inv[e][a][:, u, :], ident[0:CH, 0:CH])
                            else:
                                last = pe.matmul(o, inv[e][a][:, u, :], inv[e][b][:, u, :], start=True, stop=True)
                    last.then_inc(s_i[e], 1)

                def after_copy(e, n):
                    pe.wait_ge(s_ia[e], t * 10 + n)
                    pin(pe)

                def after_add(e, n):
                    pe.wait_ge(s_id[e], t * 9 + n)
                    pin(pe)

                pe.wait_ge(s_ops, t * 3 + 2)
                pe.wait_ge(s_q, t + 1)
                pe.wait_ge(s_r, t + 1)
                pe.wait_ge(s_y, t * 2 + 1)
                pe.wait_ge(s_sum, t * 4 + 1)
                pin(pe)
                for e in range(2):
                    h = slice(e * HD, (e + 1) * HD)
                    for c in range(2):
                        for i in range(PAIRS):
                            u = c * PAIRS + i
                            last = pe.matmul(pg[e][:, u * P:(u + 1) * P], bk[h, i, c, :, :], qr[h, i, c, :, :],
                                             start=True, stop=True)
                    last.then_inc(s_g, 1)
                for e in range(2):
                    h = slice(e * HD, (e + 1) * HD)
                    for c in range(2):
                        for i in range(PAIRS):
                            u = c * PAIRS + i
                            last = pe.matmul(pi[e][0][0:CH, u * CH:(u + 1) * CH], qr[h, i, c, 0, :], bk[h, i, c, 0, :],
                                             start=True, stop=True)
                    last.then_inc(s_i[e], 1)
                for e in range(2):
                    after_add(e, 4)
                    inverse(e, 2, (0, "dt", "d"), (1, "d", "dt"))
                pe.wait_ge(s_ops, t * 3 + 3)
                pe.wait_ge(s_gs, t * 2 + 2)
                pin(pe)
                for c in range(2):
                    for i in range(PAIRS):
                        u = c * PAIRS + i
                        last = pe.transpose(pg[0][:, u * P:(u + 1) * P], bk[:, i, c, :, :].rearrange("p a t -> p (a t)"), ident[:, :])
                last.then_inc(s_tr, 1)
                for c in range(2):
                    for i in range(PAIRS):
                        u = c * PAIRS + i
                        last = pe.transpose(pg[1][:, u * P:(u + 1) * P], vs[:, i, c * CH:c * CH + P], ident[:, :])
                last.then_inc(s_tr, 1)
                for e in range(2):
                    after_copy(e, 2)
                    inverse(e, 3, (0, "d2t", "d2"), (1, "d2", "d2t"))
                for e in range(2):
                    after_copy(e, 4)
                    inverse(e, 4, (0, "d2", "z"), (1, "dt", "d"))
                for e in range(2):
                    after_copy(e, 5)
                    after_add(e, 5)
                    inverse(e, 5, (0, "d", "z"))
                for e in range(2):
                    after_add(e, 6)
                    inverse(e, 6, (1, "d2t", "z"))
                for e in range(2):
                    after_add(e, 7)
                    inverse(e, 7, (0, "z", "e"), (1, "e", "z"))
                for e in range(2):
                    after_copy(e, 7)
                    after_add(e, 8)
                    inverse(e, 8, (0, "dt", "d2"), (1, "z", None))
                for e in range(2):
                    after_copy(e, 9)
                    inverse(e, 9, (0, "d2t", "ift"))
                for e in range(2):
                    after_add(e, 9)
                    inverse(e, 10, (1, "d", "ift"))
                for c in range(2):
                    pe.wait_ge(s_trc, t * 2 + 2)
                    pe.wait_ge(s_st, t * 4 + (2 * c + 1) if c == 0 else t * 4 + 3)
                    pe.wait_ge(s_st, t * 4 + 2 * c + 2)
                    pin(pe)
                    for i in range(PAIRS):
                        pe.matmul(pg[0][0:CH, i * P:(i + 1) * P], qr[:, i, c, 0, :], st[:, i, :, :], start=True, stop=False)
                        for e in range(2):
                            last = pe.matmul(pg[0][0:CH, i * P + e * HD:i * P + (e + 1) * HD], gs[:, e, c, i, 0:CH],
                                             xs[:, c, i, e, :], start=False, stop=(e == 1))
                    last.then_inc(s_seq, 1)
                    pe.wait_ge(s_cp, t * 4 + (2 * c + 1))
                    if c == 0:
                        for e in range(2):
                            pe.wait_ge(s_ia[e], t * 10 + 10)
                    pin(pe)
                    for i in range(PAIRS):
                        for e in range(2):
                            last = pe.matmul(pg[0][0:CH, HALF + i * P + e * HD:HALF + i * P + (e + 1) * HD],
                                             inv[e]["e"][:, c * PAIRS + i, :], rs[:, i, e, :], start=True, stop=True)
                    last.then_inc(s_seq, 1)
                    pe.wait_ge(s_cp, t * 4 + (2 * c + 2))
                    if c == 1:
                        pe.wait_ge(s_y, t * 2 + 2)
                    pin(pe)
                    for i in range(PAIRS):
                        pe.matmul(pg[1][:, i * CH:(i + 1) * CH], st[:, i, :, :].rearrange("p e v -> p (e v)"), qr[:, i, c, 1, :],
                                  start=(i == 0), stop=False, skip_group_check=True)
                    for i in range(PAIRS):
                        for e in range(2):
                            last = pe.matmul(pg[1][e * HD:(e + 1) * HD, i * CH:(i + 1) * CH], xs[:, c, i, e, :],
                                             gs[:, e, c, i, CH:P], start=False, stop=(i == PAIRS - 1), skip_group_check=True)
                    last.then_inc(s_seq, 1)
                    for i in range(PAIRS):
                        for e in range(2):
                            last = pe.matmul(pg[1][e * HD:(e + 1) * HD, HALF + i * HD:HALF + (i + 1) * HD],
                                             bt[:, c, i, e * HD:(e + 1) * HD], xs[:, c, i, e, :], start=True, stop=True)
                    last.then_inc(s_seq, 1)

        @block.scalar
        def _(act):
            act.sem_inc(s_y, 1)

            def r_copy(turn):
                act.activation(qr[:, :, :, 1, :], chunks(zs[:, 0:PAIRS, ds(turn * P, P)]), ACT.Copy).then_inc(s_r, 1)

            r_copy(0)
            with act.Fori(0, NT) as t:
                def copies(e, step, *pairs):
                    act.wait_ge(s_i[e], t * 10 + step)
                    for src, dst in pairs:
                        act.activation(inv[e][dst][:, :, :], pi[e][src][0:CH, :].rearrange("p (u t) -> p u t", t=CH),
                                       ACT.Copy).then_inc(s_ia[e], 1)

                for e in range(2):
                    copies(e, 2, (0, "d2"), (1, "d2t"))
                act.wait_ge(s_tr, t * 2 + 3)
                act.activation(bt[:, :, :, :], pg[0][:, :].rearrange("p (c i k) -> p c i k", c=2, i=PAIRS), ACT.Copy).then_inc(s_trc, 1)
                act.activation(xs[CH:P, :, :, :, :].rearrange("p c i e v -> p (c i e v)"), pg[1][CH:P, :], ACT.Copy).then_inc(s_trc, 1)
                for e in range(2):
                    copies(e, 3, (0, "d"), (1, "dt"))
                for e in range(2):
                    copies(e, 4, (1, "d2t"))
                for e in range(2):
                    copies(e, 7, (0, "d2"), (1, "dt"))
                for e in range(2):
                    copies(e, 8, (0, "d2t"), (1, "d"))
                for e in range(2):
                    copies(e, 10, (1, "e"))
                for c in range(2):
                    act.wait_ge(s_seq, t * 8 + (4 * c + 2))
                    act.activation(rs[:, :, :, :].rearrange("p i e v -> p (i e v)"), pg[0][0:CH, 0:HALF], ACT.Copy).then_inc(s_cp, 1)
                    act.wait_ge(s_seq, t * 8 + (4 * c + 3))
                    act.activation(xs[0:CH, c, :, :, :].rearrange("p i e v -> p (i e v)"), pg[0][0:CH, HALF:], ACT.Copy).then_inc(s_cp, 1)
                    act.wait_ge(s_seq, t * 8 + (4 * c + 4))
                    if c == 1:
                        r_copy((t + 1) & (NT - 1))
                    act.activation(zs[:, 0:PAIRS, ds(t * P + c * CH, CH)], pg[1][:, 0:PAIRS * CH].rearrange("p (i t) -> p i t", t=CH),
                                   ACT.Copy).then_inc(s_y, 1)

        @block.vector
        def _(dve):
            dve.wait_ge(s_mask, MASKS)
            dve.sem_inc(s_st, 2)
            dve.sem_inc(s_sum, 1)

            def q_copy(turn):
                dve.tensor_copy(qr[:, :, :, 0, :], chunks(qq[:, :, ds(turn * P, P)])).then_inc(s_q, 1)

            q_copy(0)
            with dve.Fori(0, NT) as t:
                def mask(m, shape):
                    return m.unsqueeze(1).to_broadcast(shape)

                def add(e, step, src, other, dst, n):
                    dve.wait_ge(s_i[e], t * 10 + step)
                    dve.wait_ge(s_id[e], t * 9 + n - 1)
                    dve.tensor_tensor(inv[e][dst][:, :, :], pi[e][src][0:CH, :].rearrange("p (u t) -> p u t", t=CH),
                                      inv[e][other][:, :, :], ALU.add).then_inc(s_id[e], 1)

                for e in range(2):
                    g = pg[e][:, :].rearrange("p (u t) -> p u t", t=P)
                    dve.wait_ge(s_g, t * 2 + (e + 1))
                    dve.tensor_tensor(gs[:, e, :, :, :].rearrange("p c i t -> p (c i) t"), g, mask(m_g[:, :], [P, U, P]),
                                      ALU.mult).then_inc(s_gs, 1)
                    dve.tensor_tensor(inv[e]["dt"][:, :, :], g[0:CH, :, 0:CH], mask(m_dt[:, :], [CH, U, CH]),
                                      ALU.mult).then_inc(s_id[e], 1)
                for e in range(2):
                    p = pi[e][0][0:CH, :].rearrange("p (u t) -> p u t", t=CH)
                    dve.wait_ge(s_i[e], t * 10 + 1)
                    dve.tensor_tensor(inv[e]["d"][:, :, :], p, mask(m_d[:, :], [CH, U, CH]), ALU.mult).then_inc(s_id[e], 1)
                    dve.tensor_tensor(inv[e]["e"][:, :, :], p, mask(m_e[:, :], [CH, U, CH]), ALU.mult).then_inc(s_id[e], 1)
                    dve.wait_ge(s_id[e], t * 9 + 1)
                    dve.tensor_tensor(inv[e]["z"][:, :, :], inv[e]["dt"][:, :, :], mask(ident[0:CH, 0:CH], [CH, U, CH]),
                                      ALU.add).then_inc(s_id[e], 1)
                for e in range(2):
                    add(e, 4, 0, "z", "z", 5)
                for e in range(2):
                    add(e, 5, 0, "z", "z", 6)
                for e in range(2):
                    add(e, 6, 1, "z", "z", 7)
                for e in range(2):
                    dve.wait_ge(s_ia[e], t * 10 + 7)
                    dve.tensor_tensor(inv[e]["ift"][:, :, :], inv[e]["dt"][:, :, :],
                                      mask(ident[0:CH, 0:CH], [CH, U, CH]), ALU.add).then_inc(s_id[e], 1)
                for e in range(2):
                    add(e, 9, 0, "ift", "ift", 9)
                for c in range(2):
                    if c == 1:
                        dve.wait_ge(s_seq, t * 8 + 8)
                        q_copy((t + 1) & (NT - 1))
                    dve.wait_ge(s_seq, t * 8 + (4 * c + 5))
                    for e in range(2):
                        h = slice(e * HD, (e + 1) * HD)
                        dve.tensor_tensor(tmp[h, :, :], pg[1][h, HALF:HALF + PAIRS * HD].rearrange("p (i v) -> p i v", v=HD),
                                          st[h, :, e, :], ALU.add).then_inc(s_sum, 1)
                    for e in range(2):
                        h = slice(e * HD, (e + 1) * HD)
                        dve.wait_ge(s_sum, t * 4 + (2 * c + e + 2))
                        dve.tensor_tensor(st[h, :, e, :], tmp[h, :, :], pc[h, :, ds(t * 2 + c, 1)].to_broadcast([HD, PAIRS, HD]),
                                          ALU.mult).then_inc(s_st, 1)




def mix(nc, io, sb, dram, w_out, w_q):
    with ExitStack() as ctx:
        def buf(name, shape, dt=F32):
            return ctx.enter_context(nc.sbuf_tensor(name, shape, dt))

        sem = ctx.enter_context(semaphores(nc))

        vec, zs, cv, gg, bv, headones = (sb[n] for n in ("vec", "zs", "cv", "gg", "bv", "headones"))
        sq = buf("d_sq", [P, T])
        rstd = buf("d_rstd", [P, T])
        wr = [buf(f"d_wr{i}", [P, PAIRS, P]) for i in range(2)]
        wc = [buf(f"d_wc{i}", [P, CONV_TILES, P]) for i in range(2)]
        gr = [buf(f"d_gr{i}", [P, T]) for i in range(2)]
        gc = [buf(f"d_gc{i}", [P, T]) for i in range(2)]
        pr = [ctx.enter_context(nc.psum_tensor(f"d_pr{i}", [P, T], F32)) for i in range(2)]
        pc = [ctx.enter_context(nc.psum_tensor(f"d_pc{i}", [P, T], F32)) for i in range(2)]
        s_mean, s_cen, s_sq = sem("d_y_mean"), sem("d_y_centred"), sem("d_y_squared")
        s_var, s_vinv, s_rstd = sem("d_y_variance"), sem("d_y_variance_inverted"), sem("d_y_rstd")
        s_y = sem("d_y_ready")
        s_dve = sem("d_vector_step")
        s_wr = [sem(f"d_w_r_in{i}") for i in range(2)]
        s_wc = [sem(f"d_w_c_in{i}") for i in range(2)]
        s_gr = [sem(f"d_gate_r_in{i}") for i in range(2)]
        s_gc = [sem(f"d_gate_c_in{i}") for i in range(2)]
        s_conv, s_cg = sem("d_conv_in_psum"), sem("d_conv_gated")
        s_mm = sem("d_y_output_in_psum")
        s_mul, s_mix = sem("d_y_gated"), sem("d_mixed")
        s_out = [sem(f"d_mix_out{i}") for i in range(2)]
        s_next = sem("d_next_weights_in")
        block = ctx.enter_context(nc.Block())

        @block.sync
        def _(sp):
            for m in range(KT):
                if m >= 2:
                    sp.wait_ge(s_conv, m - 1)
                    sp.wait_ge(s_cg, m - 1)
                sp.dma_start(wc[m % 2][:, :, :], io["w_c"][m]).then_inc(s_wc[m % 2], 16)
                sp.dma_start(gc[m % 2][:, :], dram["gates"][m + KT]).then_inc(s_gc[m % 2], 16)
                if m < 2:
                    sp.dma_start(wr[m][:, :, :], io["w_r"][m]).then_inc(s_wr[m], 16)
                    sp.dma_start(gr[m][:, :], dram["gates"][m]).then_inc(s_gr[m], 16)
                if m == 2:
                    sp.dma_start(w_out[:, :, :], io["w_out"]).then_inc(s_next, 16)
            sp.wait_ge(s_y, PAIRS)
            sp.dma_start(w_q[:, :, :], io["w_q"]).then_inc(s_next, 16)
            with sp.Fori(0, KT // 2 - 1) as q:
                for i in range(2):
                    sp.wait_ge(s_mm, q * 2 + (i + 1))
                    sp.dma_start(wr[i][:, :, :], one(io["w_r"], q * 2 + (i + 2))).then_inc(s_wr[i], 16)
                    sp.wait_ge(s_out[i], q * 16 + 16)
                    sp.dma_start(gr[i][:, :], one(dram["gates"], q * 2 + (i + 2))).then_inc(s_gr[i], 16)
            sp.wait_ge(s_next, 32)

        @block.tensor
        def _(pe):
            def head_sums(out, x, s_done):
                for h in range(NH):
                    t = slice(h * HALF, (h + 1) * HALF)
                    last = pe.matmul(out[:, t], headones[:, :], x[:, t], start=True, stop=True)
                last.then_inc(s_done, 1)

            def product(out, w, x, n, s_done):
                for h in range(NH):
                    t = slice(h * HALF, (h + 1) * HALF)
                    for k in range(n):
                        last = pe.matmul(out[:, t], w[:, k, :], x[:, k, t], start=(k == 0), stop=(k == n - 1))
                last.then_inc(s_done, 1)

            head_sums(pr[0], zs[:, 0, :], s_mean)
            for i in range(PAIRS):
                pe.wait_ge(s_sq, i + 1)
                if i:
                    pe.wait_ge(s_vinv, i)
                head_sums(pr[1], sq, s_var)
                if i + 1 < PAIRS:
                    pe.wait_ge(s_cen, i + 1)
                    head_sums(pr[0], zs[:, i + 1, :], s_mean)
                for m in (2 * i, 2 * i + 1):
                    pe.wait_ge(s_wc[m % 2], 16 * (m // 2 + 1))
                    if m >= 2:
                        pe.wait_ge(s_cg, m - 1)
                    product(pc[m % 2], wc[m % 2], cv, CONV_TILES, s_conv)
            pe.wait_ge(s_y, PAIRS)
            with pe.Fori(0, KT // 2) as q:
                for i in range(2):
                    pe.wait_ge(s_wr[i], q * 16 + 16)
                    pe.wait_ge(s_mul, q * 2 + (i + 1))
                    product(pr[i], wr[i], zs, PAIRS, s_mm)

        @block.scalar
        def _(act):
            def square(i):
                act.wait_ge(s_cen, i + 1)
                if i:
                    act.wait_ge(s_var, i)
                act.activation(sq[:, :], zs[:, i, :], ACT.Square).then_inc(s_sq, 1)

            square(0)
            for i in range(PAIRS):
                act.wait_ge(s_vinv, i + 1)
                act.activation(rstd[:, :], rstd[:, :], ACT.Sqrt).then_inc(s_rstd, 1)
                if i + 1 < PAIRS:
                    square(i + 1)
            with act.Fori(0, KT // 2) as q:
                for i in range(2):
                    act.wait_ge(s_mix, q * 2 + (i + 1))
                    act.dma_start(dram["mix"][:, :, ds(q * 2 + i, 1), :].rearrange("t p a c -> p t (a c)"),
                                  gr[i][:, :].rearrange("p (t c) -> p t c", c=P)).then_inc(s_out[i], 16)
            for i in range(2):
                act.wait_ge(s_out[i], 16 * (KT // 2))

        @block.vector
        def _(dve):
            link = Link(dve, s_dve)

            def centre(i):
                dve.wait_ge(s_mean, i + 1)
                dve.scalar_tensor_tensor(out=zs[:, i, :], in0=pr[0][:, :], scalar=-1.0 / HD, in1=zs[:, i, :], op0=ALU.mult,
                                         op1=ALU.add).then_inc(s_cen, 1)

            centre(0)
            for i in range(PAIRS):
                y = zs[:, i, :]
                dve.wait_ge(s_var, i + 1)
                link(dve.tensor_scalar(rstd[:, :], pr[1][:, :], 1.0 / HD, GN_EPS, ALU.mult, ALU.add))
                dve.reciprocal(rstd[:, :], rstd[:, :]).then_inc(s_vinv, 1)
                if i + 1 < PAIRS:
                    centre(i + 1)
                dve.wait_ge(s_rstd, i + 1)
                link(dve.scalar_tensor_tensor(out=y, in0=y, scalar=vec[:, COL["lnx_g"] + i:COL["lnx_g"] + i + 1],
                                              in1=rstd[:, :], op0=ALU.mult, op1=ALU.mult))
                link(dve.scalar_tensor_tensor(out=y, in0=y, scalar=vec[:, COL["lnx_b"] + i:COL["lnx_b"] + i + 1],
                                              in1=bv[:, i, :], op0=ALU.add, op1=ALU.add))
                dve.tensor_tensor(y, y, gg[:, i, :], ALU.mult).then_inc(s_y, 1)
                for m in (2 * i, 2 * i + 1):
                    dve.wait_ge(s_conv, m + 1)
                    dve.wait_ge(s_gc[m % 2], 16 * (m // 2 + 1))
                    dve.tensor_tensor(zs[:, PAIRS + m, :], gc[m % 2][:, :], pc[m % 2][:, :], ALU.mult).then_inc(s_cg, 1)
            dve.wait_ge(s_cg, KT)
            dve.sem_inc(s_mul, 2)
            with dve.Fori(0, KT // 2) as q:
                for i in range(2):
                    dve.wait_ge(s_mm, q * 2 + (i + 1))
                    dve.wait_ge(s_gr[i], q * 16 + 16)
                    dve.tensor_tensor(gr[i][:, :], gr[i][:, :], pr[i][:, :], ALU.mult).then_inc(s_mul, 1)
                    dve.wait_ge(s_mul, q * 2 + (i + 3))
                    dve.tensor_tensor(gr[i][:, :], gr[i][:, :], at(zs, q * 2 + (PAIRS + i)), ALU.add).then_inc(s_mix, 1)



GRP = 8
GROUPS = NSEL // GRP
UR, VR, DR = 4, GRP, 4
KS = TOPK // 2
AHEAD = 3
IR = 4
HEAD_STEPS = 17
SELECT_STEPS = 11


def experts(nc, io, dram, w_out, w_q):
    with ExitStack() as ctx:
        def buf(name, shape, dt=F32):
            return ctx.enter_context(nc.sbuf_tensor(name, shape, dt))

        sem = ctx.enter_context(semaphores(nc))

        def psum(name, shape):
            return ctx.enter_context(nc.psum_tensor(name, shape, F32))

        ident, vec = buf("e_ident", [P, P]), buf("e_vec", [P, NVEC])
        w_ple = buf("e_w_ple", [P, KT, D])
        w_proj = buf("e_w_proj", [P, PLE // P, D])
        keys = buf("e_keys", [P, PH, NKEY])
        g_ffn, g_fin = buf("e_g_ffn", [P, D]), buf("e_g_fin", [P, D])
        mixt = buf("e_mix", [P, KT, P])
        qT = mixt
        xin = buf("e_x", [P, D])
        actT = buf("e_actT", [P, KT, P])
        c = buf("e_c", [P, D])
        hh, gt = buf("e_hh", [P, D]), buf("e_gt", [P, D])
        pt = buf("e_pt", [P, PLE // P, P])
        u = [buf(f"e_u{i}", [P, D]) for i in range(UR)]
        v = [buf(f"e_v{i}", [P, D]) for i in range(VR)]
        dg = [buf(f"e_dg{i}", [P, P]) for i in range(DR)]
        dots, gl, coef = buf("e_dots", [P, GRP]), buf("e_gelu", [P, GRP]), buf("e_coef", [P, GRP])
        zero = buf("e_zero", [P, HALF], mybir.dt.bfloat16)
        st = buf("e_stats", [P, 8])
        sc = buf("e_sc", [P, 2, NKEY])
        sc2 = buf("e_sc2", [P, 2, NKEY])
        cand, cand2 = buf("e_cand", [P, TOPK, TOPK]), buf("e_cand2", [P, TOPK * TOPK])
        tv, ti = buf("e_tv", [P, 2, TOPK]), buf("e_ti", [P, 2, TOPK], U32)
        ix = buf("e_ix", [P, 2, PH, TOPK])
        best, pos = buf("e_best", [P, PH, TOPK]), buf("e_pos", [P, PH, TOPK], U32)
        half = buf("e_half", [P, 2, TOPK], U32)
        halff = buf("e_halff", [P, 2, TOPK])
        pick = buf("e_pick", [P, 2, TOPK])
        oh = buf("e_onehot", [P, 2, TOPK, TOPK])
        iot, ioti = buf("e_iota", [P, TOPK]), buf("e_iotai", [P, TOPK], mybir.dt.int32)
        ex = buf("e_exp", [P, PH, TOPK])
        ssum = buf("e_ssum", [P, PH])
        gates = buf("e_gates", [P, NSEL])
        idx = [buf(f"e_idx{i}", [P, TOPK], U32) for i in range(IR)]

        pd = psum("e_pd", [P, D])
        acc = psum("e_acc", [P, D])
        ps = psum("e_ps", [P, 2, PH, NKEY])

        s_const, s_iota = sem("e_constants"), sem("e_iota")
        s_w_q, s_w_tail = sem("e_query_weights_in"), sem("e_tail_weights_in")
        s_ident = sem("e_identity_made")
        s_zero = sem("e_sum_cleared")
        s_mixin, s_xin = sem("e_mix_in"), sem("e_x_in")
        s_hps, s_h, s_hout = sem("e_h_in_psum"), sem("e_h_ready"), sem("e_h_out")
        s_sq, s_var, s_rstd = sem("e_h_squared"), sem("e_h_variance"), sem("e_h_rstd")
        s_hn, s_ctr, s_cT = sem("e_h_normed"), sem("e_c_turned"), sem("e_cT_ready")
        s_qps, s_qT, s_sc = sem("e_q_in_psum"), sem("e_qT_ready"), sem("e_scores_in_psum")
        s_head, s_topk = sem("e_head_copied"), sem("e_head_used")
        s_k = sem("e_topk_step")
        s_fv, s_tv = sem("e_h_mean_square"), sem("e_tail_mean_square")
        s_sub, s_exp, s_in = sem("e_score_less_max"), sem("e_exp"), sem("e_indices_ready")
        s_fin = sem("e_select_step")
        s_pool = sem("e_gpsimd_waits_passed")
        s_dve = sem("e_vector_waits_passed")
        s_sp = sem("e_sync_waits_passed")
        s_cur = sem("e_tile_switched")
        s_u = [sem(f"e_u_in{i}") for i in range(UR)]
        s_v = [sem(f"e_v_in{i}") for i in range(VR)]
        s_dot, s_gelu, s_coef = sem("e_dot"), sem("e_gelu"), sem("e_coef")
        s_diag, s_vmm = sem("e_diag"), sem("e_v_added")
        s_hhin, s_hh, s_ptin = sem("e_tail_h_in"), sem("e_tail_h_ready"), sem("e_p_in")
        s_tsq, s_tvar, s_trstd = sem("e_tail_squared"), sem("e_tail_variance"), sem("e_tail_rstd")
        s_tn, s_ttr, s_tT = sem("e_tail_normed"), sem("e_tail_turned"), sem("e_tailT_ready")
        s_gps, s_gate = sem("e_gate_in_psum"), sem("e_gate_ready")
        s_pps, s_gp, s_h3 = sem("e_proj_in_psum"), sem("e_gated_proj"), sem("e_last_h")
        s_out, s_outd = sem("e_out_ready"), sem("e_out_stored")

        block = ctx.enter_context(nc.Block())

        @block.sync
        def _(sp):
            def mix_load(tile):
                sp.dma_start(mixt[:, :, :], one(dram["mix"], tile)).then_inc(s_mixin, 16)

            mix_load(0)
            sp.dma_start(xin[:, :], io["x"][0]).then_inc(s_xin, 16)
            sp.dma_start(vec[:, :], io["vec"]).then_inc(s_w_q, 16)
            sp.dma_start(keys[:, :, :], io["keys"]).then_inc(s_w_q, 16)
            sp.dma_start(g_ffn[:, :], io["g_ffn"].to_broadcast([P, D])).then_inc(s_w_q, 16)
            sp.dma_start(hh[:, :], io["x"][NT - 1]).then_inc(s_hhin, 16)
            sp.dma_start(pt[:, :, :], io["pT"][NT - 1]).then_inc(s_ptin, 16)
            sp.dma_start(w_ple[:, :, :], io["w_ple"]).then_inc(s_w_tail, 16)
            sp.dma_start(w_proj[:, :, :], io["w_proj"]).then_inc(s_w_tail, 16)
            sp.dma_start(g_fin[:, :], io["g_fin"].to_broadcast([P, D])).then_inc(s_w_tail, 16)

            def after(semaphore, count):
                sp.wait_ge(semaphore, count)
                sp.sem_inc(s_sp, 1)

            sp.wait_ge(s_h, 1)
            sp.dma_start(dram["h"][0], xin[:, :]).then_inc(s_hout, 16)
            with sp.Fori(0, NT) as t:
                after(s_sc, t + 1)
                mix_load((t + 1) & (NT - 1))
                after(s_cur, t + 1)
                sp.dma_start(xin[:, :], one(io["x"], (t + 1) & (NT - 1))).then_inc(s_xin, 16)
                after(s_h, t + 2)
                sp.dma_start(one(dram["h"], (t + 1) & (NT - 1)), xin[:, :]).then_inc(s_hout, 16)
                after(s_pps, t + 1)
                sp.dma_start(pt[:, :, :], one(io["pT"], t)).then_inc(s_ptin, 16)
                after(s_out, t + 1)
                sp.dma_start(one(dram["out"], (t + (NT - 1)) & (NT - 1)), gt[:, :]).then_inc(s_outd, 16)
                after(s_outd, t * 16 + 16)
                after(s_hout, t * 16 + 16)
                sp.dma_start(hh[:, :], one(dram["h"], t)).then_inc(s_hhin, 16)
            sp.wait_ge(s_out, NT + 1)
            sp.wait_ge(s_outd, 16 * NT)
            sp.dma_start(one(dram["out"], NT - 1), gt[:, :]).then_inc(s_outd, 16)
            sp.wait_ge(s_outd, 16 * (NT + 1))
            sp.wait_ge(s_hout, 16 * (NT + 1))

        @block.gpsimd
        def _(pool):
            pool.memset(zero[:, :], 0.0).then_inc(s_const, 1)
            pool.memset(ident[:, :], 0.0).then_inc(s_ident, 1)
            pool.wait_ge(s_ident, 1)
            pool.affine_select(out=ident[:, :], in_=ident[:, :], compare_op=ALU.not_equal, fill=1.0,
                               base=0, pattern=[[-1, P]], channel_multiplier=1).then_inc(s_ident, 1)
            pool.iota(ioti[:, :], [[1, TOPK]], base=0, channel_multiplier=0).then_inc(s_const, 1)
            pool.wait_ge(s_const, 2)
            pool.tensor_copy(iot[:, :], ioti[:, :]).then_inc(s_iota, 1)
            with pool.Fori(0, NT * PH // IR) as q:
                for i in range(IR):
                    for e in range(TOPK // GRP):
                        n = q * (IR * TOPK // GRP) + (i * TOPK // GRP + e)
                        for s in range(GRP):
                            if s == 0 and e == 0:
                                pool.wait_ge(s_in, q * IR + (i + 1))
                            pool.wait_ge(s_dot, n * GRP + (s + 1))
                            pool.sem_inc(s_pool, 1)
                            pool.indirect_dma_start(out=u[s % UR][:, :], out_offset=None, in_=io["u_tab"],
                                                    in_offset=bass.IndirectOffsetOnAxis(ap=idx[i][:, e * GRP + s:e * GRP + s + 1], axis=0))\
                                .then_inc(s_u[s % UR], 16)
                        for s in range(GRP):
                            pool.wait_ge(s_vmm, n * GRP + (s + 1))
                            pool.sem_inc(s_pool, 1)
                            pool.indirect_dma_start(out=v[s][:, :], out_offset=None, in_=io["v_tab"],
                                                    in_offset=bass.IndirectOffsetOnAxis(ap=idx[i][:, e * GRP + s:e * GRP + s + 1], axis=0))\
                                .then_inc(s_v[s], 16)

        @block.tensor
        def _(pe):
            def turned(src, n, s_src, s_dst):
                pe.wait_ge(s_src, n + 1)
                for k in range(KT):
                    last = pe.transpose(pd[:, k * P:(k + 1) * P], src[:, k * P:(k + 1) * P], ident[:, :])
                last.then_inc(s_dst, 1)

            def product(lhs, w, kt, halves=(0, 1)):
                for h in halves:
                    for k in range(kt):
                        last = pe.matmul(pd[:, h * HALF:(h + 1) * HALF], lhs[:, k, :], w[:, k, h * HALF:(h + 1) * HALF],
                                         start=(k == 0), stop=(k == kt - 1))
                return last

            def mixed(n, halves=(0, 1)):
                if 0 in halves:
                    pe.wait_ge(s_mixin, n * 16 + 16)
                last = product(mixt, w_out, KT, halves)
                if 1 in halves:
                    last.then_inc(s_hps, 1)

            def queries(n, heads):
                if 0 in heads:
                    pe.wait_ge(s_cT, n + 1)
                for h in heads:
                    for k in range(KT):
                        last = pe.matmul(pd[:, h * P:(h + 1) * P], w_q[:, k, h * P:(h + 1) * P], actT[:, k, :],
                                         start=(k == 0), stop=(k == KT - 1))
                if PH - 1 in heads:
                    last.then_inc(s_qps, 1)

            def scores(n):
                pe.wait_ge(s_qT, n + 1)
                for p in range(2):
                    r = slice(p * PHALF, (p + 1) * PHALF)
                    for h in range(PH):
                        last = pe.matmul(ps[:, p, h, :], qT[r, h, :], keys[r, h, :], start=True, stop=True)
                last.then_inc(s_sc, 1)

            def ple_gate(n, halves=(0, 1)):
                if 0 in halves:
                    pe.wait_ge(s_tT, n + 1)
                last = product(actT, w_ple, KT, halves)
                if 1 in halves:
                    last.then_inc(s_gps, 1)

            def ple_proj(n):
                pe.wait_ge(s_ptin, n * 16 + 16)
                pe.wait_ge(s_gate, n + 1)
                product(pt, w_proj, PLE // P).then_inc(s_pps, 1)

            def group(n):
                for s in range(GRP):
                    pe.wait_ge(s_diag, n * GRP + (s + 2))
                    pe.wait_ge(s_v[s], n * 16 + 16)
                    for h in range(D // HALF):
                        cols = slice(h * HALF, (h + 1) * HALF)
                        last = pe.matmul(acc[:, cols], dg[s % DR][:, :], v[s][:, cols], start=False, stop=False,
                                         skip_group_check=True)
                    last.then_inc(s_vmm, 1)

            def clear():
                for h in range(D // HALF):
                    last = pe.matmul(acc[:, h * HALF:(h + 1) * HALF], zero[:, 0:P], zero[:, :], start=True, stop=False,
                                     skip_group_check=True)
                last.then_inc(s_zero, 1)

            pe.sem_inc(s_vmm, VR)
            pe.wait_ge(s_const, 2)
            pe.wait_ge(s_ident, 2)
            clear()
            mixed(0)
            pe.wait_ge(s_w_q, 16 * 3)
            turned(xin, 0, s_hn, s_ctr)
            queries(0, range(PH))
            scores(0)
            with pe.Fori(0, NT) as t:
                for g in range(GROUPS):
                    if g == 0:
                        pe.wait_ge(s_hh, t + 1)
                        clear()
                    group(t * GROUPS + g)
                    if g == 0:
                        mixed(t + 1, (0,))
                    if g == 1:
                        mixed(t + 1, (1,))
                    if g == 3:
                        turned(xin, t + 1, s_hn, s_ctr)
                    if g == 4:
                        queries(t + 1, range(PH // 2))
                    if g == 5:
                        queries(t + 1, range(PH // 2, PH))
                    if g == 7:
                        pe.wait_ge(s_qT, t + 2)
                        turned(gt, t, s_tn, s_ttr)
                    if g == 8:
                        pe.wait_ge(s_w_tail, 16 * 3)
                        ple_gate(t, (0,))
                    if g == 9:
                        ple_gate(t, (1,))
                    if g == 10:
                        ple_proj(t)
                    if g == 12:
                        pe.wait_ge(s_head, t * PH + PH)
                        scores(t + 1)
            turned(gt, NT, s_tn, s_ttr)
            ple_gate(NT)
            ple_proj(NT)

        @block.scalar
        def _(act):
            def square(scratch, src, column, n, s_src, s_dst):
                act.wait_ge(s_src, n)
                act.activation(scratch[:, :], src[:, :], ACT.Square, accum_out=st[:, column:column + 1]).then_inc(s_dst, 1)

            def root(column, n, s_src, s_dst):
                act.wait_ge(s_src, n)
                act.activation(st[:, column:column + 1], st[:, column:column + 1], ACT.Sqrt).then_inc(s_dst, 1)

            def scaled(n, gain, s_src, s_dst):
                act.wait_ge(s_src, n + 1)
                for k in range(KT):
                    last = act.activation(actT[:, k, :], pd[:, k * P:(k + 1) * P], ACT.Copy,
                                          scale=vec[:, COL[gain] + k:COL[gain] + k + 1])
                last.then_inc(s_dst, 1)

            def queries(n):
                act.wait_ge(s_qps, n + 1)
                act.activation(qT[:, :, :].rearrange("p h t -> p (h t)"), pd[:, :], ACT.Copy).then_inc(s_qT, 1)

            def head(n, h):
                if h == 0:
                    act.wait_ge(s_sc, n + 1)
                act.wait_ge(s_topk, n * PH + (h + 1))
                act.activation(sc[:, :, :], ps[:, :, h, :], ACT.Copy).then_inc(s_head, 1)

            def gate_exp(n, h):
                act.wait_ge(s_sub, n * PH + (h + 1))
                act.activation(ex[:, h, :], ex[:, h, :], ACT.Exp, accum_out=ssum[:, h:h + 1]).then_inc(s_exp, 1)

            def ple_gate(n):
                act.wait_ge(s_gps, n + 1)
                act.activation(gt[:, :], pd[:, :], ACT.Sigmoid).then_inc(s_gate, 1)

            def gelu(n):
                act.wait_ge(s_dot, n * GRP + (GRP + UR))
                act.activation(gl[:, :], dots[:, :], ACT.Gelu).then_inc(s_gelu, 1)

            def diagonals(n):
                act.wait_ge(s_coef, n + 1)
                for s in range(GRP):
                    act.wait_ge(s_vmm, n * GRP + (s + 1 + VR - DR))
                    act.activation(dg[s % DR][:, :], ident[:, :], ACT.Copy, scale=coef[:, s:s + 1]).then_inc(s_diag, 1)

            act.sem_inc(s_gelu, 1)
            act.sem_inc(s_diag, 1)
            act.wait_ge(s_w_q, 16 * 3)
            act.wait_ge(s_ident, 2)
            root(1, 1, s_var, s_rstd)
            scaled(0, "ffn_g", s_ctr, s_cT)
            queries(0)
            head(0, 0)
            gate_exp(0, 0)
            head(0, 1)
            with act.Fori(0, NT) as t:
                for g in range(GROUPS):
                    gelu(t * GROUPS + g)
                    if g % 2 == 0:
                        later, h = divmod(g // 2 + 1, PH)
                        gate_exp(t + later, h)
                    if g == 3:
                        root(1, t + 2, s_var, s_rstd)
                    if g == 7:
                        root(3, t * 2 + 1, s_tvar, s_trstd)
                    if g == 14:
                        root(5, t * 2 + 2, s_tvar, s_trstd)
                    diagonals(t * GROUPS + g)
                    if g == 3:
                        scaled(t + 1, "ffn_g", s_ctr, s_cT)
                    if g == 5:
                        queries(t + 1)
                        square(gt, hh, 2, t + 1, s_hh, s_tsq)
                    if g == 7:
                        scaled(t, "ple_g", s_ttr, s_tT)
                    if g == 9:
                        ple_gate(t)
                    if g == 12:
                        square(gt, hh, 4, t + 1, s_h3, s_tsq)
                    if g % 2 == 0:
                        later, h = divmod(g // 2 + 2, PH)
                        head(t + later, h)
            act.wait_ge(s_outd, NT * 16)
            square(gt, hh, 2, NT + 1, s_hh, s_tsq)
            root(3, NT * 2 + 1, s_tvar, s_trstd)
            scaled(NT, "ple_g", s_ttr, s_tT)
            ple_gate(NT)
            square(gt, hh, 4, NT + 1, s_h3, s_tsq)
            root(5, NT * 2 + 2, s_tvar, s_trstd)

        @block.vector
        def _(dve):
            def pinned():
                dve.sem_inc(s_dve, 1)

            def variance(column, n, s_src, s_own, s_dst):
                dve.wait_ge(s_src, n)
                dve.tensor_scalar(st[:, column + 1:column + 2], st[:, column:column + 1], 1.0 / D, RMS_EPS, ALU.mult, ALU.add)\
                    .then_inc(s_own, 1)
                dve.wait_ge(s_own, n)
                dve.reciprocal(st[:, column + 1:column + 2], st[:, column + 1:column + 2]).then_inc(s_dst, 1)

            def front_h(n):
                dve.wait_ge(s_hps, n + 1)
                dve.wait_ge(s_xin, n * 16 + 16)
                dve.tensor_tensor(xin[:, :], pd[:, :], xin[:, :], ALU.add).then_inc(s_h, 1)
                dve.wait_ge(s_h, n + 1)
                pinned()
                dve.tensor_tensor_reduce(gt[:, :], xin[:, :], xin[:, :], 1.0, 0.0, ALU.mult, ALU.add, st[:, 0:1]).then_inc(s_sq, 1)
                variance(0, n + 1, s_sq, s_fv, s_var)

            def front_norm(n):
                dve.wait_ge(s_rstd, n + 1)
                dve.wait_ge(s_hout, n * 16 + 16)
                dve.tensor_scalar(xin[:, :], xin[:, :], st[:, 1:2], None, ALU.mult).then_inc(s_hn, 1)

            def head(n, h):
                link = Link(dve, s_k, n, PH * HEAD_STEPS, start=h * HEAD_STEPS)

                def stage():
                    link.wait()
                    pinned()

                dve.wait_ge(s_head, n * PH + (h + 1))
                pinned()
                for p in range(2):
                    link.mark(dve.max(tv[:, p, 0:KS], sc[:, p, :]))
                stage()
                for p in range(2):
                    link.mark(dve.max_index(ti[:, p, 0:KS], tv[:, p, 0:KS], sc[:, p, :]))
                    link.mark(dve.match_replace(sc2[:, p, :], tv[:, p, 0:KS], sc[:, p, :], LOWEST))
                stage()
                dve.sem_inc(s_topk, 1)
                for p in range(2):
                    link.mark(dve.max(tv[:, p, KS:], sc2[:, p, :]))
                stage()
                for p in range(2):
                    link.mark(dve.max_index(ti[:, p, KS:], tv[:, p, KS:], sc2[:, p, :]))
                link.mark(dve.tensor_tensor(cand[:, :, :], tv[:, 0, :].unsqueeze(2).to_broadcast([P, TOPK, TOPK]),
                                            tv[:, 1, :].unsqueeze(1).to_broadcast([P, TOPK, TOPK]), ALU.add))
                stage()
                flat = cand[:, :, :].rearrange("p a b -> p (a b)")
                link.mark(dve.tensor_copy(ix[:, :, h, :], ti[:, :, :]))
                link.mark(dve.max(best[:, h, 0:KS], flat))
                stage()
                link.mark(dve.max_index(pos[:, h, 0:KS], best[:, h, 0:KS], flat))
                link.mark(dve.match_replace(cand2[:, :], best[:, h, 0:KS], flat, LOWEST))
                stage()
                link.mark(dve.max(best[:, h, KS:], cand2[:, :]))
                stage()
                link.mark(dve.max_index(pos[:, h, KS:], best[:, h, KS:], cand2[:, :]))
                assert link.k == HEAD_STEPS, link.k

            def less_max(n, h):
                dve.wait_ge(s_k, n * (PH * HEAD_STEPS) + (h + 1) * HEAD_STEPS)
                dve.tensor_scalar(ex[:, h, :], best[:, h, :], best[:, h, 0:1], None, ALU.subtract).then_inc(s_sub, 1)

            def select(n, h):
                link = Link(dve, s_fin, n, PH * SELECT_STEPS, start=h * SELECT_STEPS)
                square = [P, TOPK, TOPK]
                for p in range(2):
                    op, by = ((ALU.logical_shift_right, 4), (ALU.bitwise_and, TOPK - 1))[p]
                    link.mark(dve.tensor_scalar(half[:, p, :], pos[:, h, :], by, None, op))
                link.wait()
                link(dve.tensor_copy(halff[:, :, :], half[:, :, :]))
                for p in range(2):
                    link.mark(dve.tensor_tensor(oh[:, p, :, :], halff[:, p, :].unsqueeze(2).to_broadcast(square),
                                                iot[:, :].unsqueeze(1).to_broadcast(square), ALU.is_equal))
                link.wait()
                for p in range(2):
                    link.mark(dve.tensor_tensor(oh[:, p, :, :], oh[:, p, :, :],
                                                ix[:, p, h, :].unsqueeze(1).to_broadcast(square), ALU.mult))
                link.wait()
                for p in range(2):
                    link.mark(dve.tensor_reduce(pick[:, p, :], oh[:, p, :, :], AX.X, ALU.add))
                link.wait()
                dve.scalar_tensor_tensor(out=idx[h % IR][:, :], in0=pick[:, 0, :], scalar=float(NKEY), in1=pick[:, 1, :],
                                         op0=ALU.mult, op1=ALU.add).then_inc(s_in, 1)
                dve.wait_ge(s_exp, n * PH + (h + 1))
                link(dve.reciprocal(ssum[:, h:h + 1], ssum[:, h:h + 1]))
                link.mark(dve.tensor_scalar(gates[:, h * TOPK:(h + 1) * TOPK], ex[:, h, :], ssum[:, h:h + 1], None, ALU.mult))
                link.wait()
                dve.wait_ge(s_in, n * PH + (h + 1))
                assert link.k == SELECT_STEPS, link.k

            def make_c(n):
                dve.wait_ge(s_hn, n + 1)
                dve.tensor_tensor(c[:, :], xin[:, :], g_ffn[:, :], ALU.mult).then_inc(s_cur, 1)
                dve.wait_ge(s_cur, n + 1)
                pinned()

            def sum_read(n):
                dve.wait_ge(s_hhin, n * 16 + 16)
                dve.wait_ge(s_vmm, n * NSEL + VR)
                dve.wait_ge(s_zero, n + 1)
                dve.tensor_tensor(hh[:, :], hh[:, :], acc[:, :], ALU.add).then_inc(s_hh, 1)

            def tail_norm(n):
                dve.wait_ge(s_trstd, n * 2 + 1)
                dve.tensor_scalar(gt[:, :], hh[:, :], st[:, 3:4], None, ALU.mult).then_inc(s_tn, 1)

            def tail_add(n):
                dve.wait_ge(s_pps, n + 1)
                dve.wait_ge(s_gate, n + 1)
                dve.tensor_tensor(gt[:, :], gt[:, :], pd[:, :], ALU.mult).then_inc(s_gp, 1)
                dve.wait_ge(s_gp, n + 1)
                dve.tensor_tensor(hh[:, :], hh[:, :], gt[:, :], ALU.add).then_inc(s_h3, 1)

            def tail_out(n):
                dve.wait_ge(s_trstd, n * 2 + 2)
                dve.scalar_tensor_tensor(out=gt[:, :], in0=hh[:, :], scalar=st[:, 5:6], in1=g_fin[:, :],
                                         op0=ALU.mult, op1=ALU.mult).then_inc(s_out, 1)

            def group_dots(n):
                dve.wait_ge(s_gelu, n + 1)
                for s in range(GRP):
                    dve.wait_ge(s_u[s % UR], n * (16 * GRP // UR) + 16 * (s // UR + 1))
                    if s == 0:
                        pinned()
                    dve.tensor_tensor_reduce(u[s % UR][:, :], u[s % UR][:, :], c[:, :], 1.0, 0.0, ALU.mult, ALU.add,
                                             dots[:, s:s + 1]).then_inc(s_dot, 1)

            def coefficients(n, g):
                dve.wait_ge(s_gelu, n + 2)
                dve.wait_ge(s_diag, n * GRP + 1)
                dve.tensor_tensor(coef[:, :], gl[:, :], gates[:, g * GRP:(g + 1) * GRP], ALU.mult).then_inc(s_coef, 1)

            dve.sem_inc(s_dot, UR)
            dve.sem_inc(s_topk, 1)
            dve.wait_ge(s_const, 2)
            dve.wait_ge(s_iota, 1)
            front_h(0)
            front_norm(0)
            dve.wait_ge(s_w_q, 16 * 3)
            head(0, 0)
            less_max(0, 0)
            select(0, 0)
            head(0, 1)
            less_max(0, 1)
            with dve.Fori(0, NT) as t:
                make_c(t)
                for g in range(GROUPS):
                    group_dots(t * GROUPS + g)
                    if g == 0:
                        sum_read(t)
                    coefficients(t * GROUPS + g, g)
                    if g % 2 == 0:
                        later, h = divmod((g + AHEAD - 1) // 2, PH)
                        select(t + later, h)
                    if g % 2 == 1:
                        later, h = divmod((g + AHEAD) // 2, PH)
                        head(t + later, h)
                        less_max(t + later, h)
                    if g == 2:
                        front_h(t + 1)
                    if g == 3:
                        front_norm(t + 1)
                    if g == 6:
                        variance(2, t * 2 + 1, s_tsq, s_tv, s_tvar)
                    if g == 7:
                        tail_norm(t)
                    if g == 12:
                        tail_add(t)
                    if g == 13:
                        variance(4, t * 2 + 2, s_tsq, s_tv, s_tvar)
                    if g == 14:
                        dve.wait_ge(s_w_tail, 16 * 3)
                        tail_out(t)
            sum_read(NT)
            variance(2, NT * 2 + 1, s_tsq, s_tv, s_tvar)
            tail_norm(NT)
            tail_add(NT)
            variance(4, NT * 2 + 2, s_tsq, s_tv, s_tvar)
            tail_out(NT)


FROM_PROJECTION = dict(ident=[P, P], vec=[P, NVEC], cw=[P, TAPS * CONV_TILES], zs=[P, RWKV_TILES, T],
                       cv=[P, CONV_TILES, T])
FROM_PREPARATION = dict(pc=[P, PAIRS, NC], headones=[P, P])


def program(nc, io, out):
    dram = {"gates": nc.dram_tensor("mixer_gates", (GATE_TILES, P, T), F32).ap(),
            "mix": nc.dram_tensor("mixed", (NT, P, KT, P), F32).ap(),
            "h": nc.dram_tensor("h_after_mixer", (NT, P, D), F32).ap(),
            "out": out}
    with nc.sbuf_tensor("first", [P, KT, T], F32) as first, nc.sbuf_tensor("second", [P, KT, T], F32) as second:
        with ExitStack() as ctx:
            sb = {name: ctx.enter_context(nc.sbuf_tensor(name, shape, F32)) for name, shape in FROM_PROJECTION.items()}
            project_in(nc, io, sb, dram, first, second)
            for name, shape in FROM_PREPARATION.items():
                sb[name] = ctx.enter_context(nc.sbuf_tensor(name, shape, F32))
            sb["qq"], sb["bb"] = first[:, 0:PAIRS, :], first[:, PAIRS:, :]
            sb["gg"], sb["bv"] = second[:, 0:PAIRS, :], second[:, PAIRS:, :]
            prepare_recurrence(nc, io, sb)
            recurrence(nc, io, sb)
            mix(nc, io, sb, dram, first, second)
        experts(nc, io, dram, first, second)


VEC_INPUTS = dict(mu="rwkv_mu", w0="rwkv_w0", a0="rwkv_a0", k_k="rwkv_k_k", k_a="rwkv_k_a", r_k="rwkv_r_k",
                  lnx_g="rwkv_lnx_g", lnx_b="rwkv_lnx_b", dw_b="conv_dw_b", ln_g="conv_ln_g", ln_b="conv_ln_b",
                  mix_g="norm_mix_g", ffn_g="norm_ffn_g", ple_g="ple_norm_g")


def column_tiles(w):
    k, n = w.shape
    return w.reshape(k // P, P, n // P, P).transpose(2, 1, 0, 3)


def row_tiles(w):
    k, n = w.shape
    return w.reshape(k // P, P, n).transpose(1, 0, 2)


def layout(a):
    vec = np.concatenate([a[VEC_INPUTS[name]][0].reshape(-1, P) for name, _ in VECS]).T
    return {
        "x": a["x"][0].reshape(NT, P, D),
        "xT": a["x"][0].T.reshape(KT, P, T),
        "w_in": column_tiles(a["w_in"][0]),
        "vec": vec,
        "dw_w": a["conv_dw_w"][0].reshape(-1, P).T,
        "wa_up": np.concatenate([a["rwkv_w_up"][0], a["rwkv_a_up"][0]], 0),
        "g_up": a["rwkv_g_up"][0],
        "w_r": column_tiles(a["rwkv_w_o"][0]),
        "w_c": column_tiles(a["conv_w_o"][0]),
        "w_out": row_tiles(a["w_out"][0]),
        "w_q": row_tiles(a["peer_w_q"][0]),
        "w_ple": row_tiles(a["ple_w_gate"][0]),
        "w_proj": row_tiles(a["ple_w_proj"][0]),
        "keys": a["peer_sub_keys"][0].transpose(1, 3, 0, 2).reshape(P, PH, NKEY),
        "g_ffn": a["norm_ffn_g"],
        "g_fin": a["final_norm_g"][None],
        "pT": a["p"][0, 0].reshape(NT, P, PLE // P, P).transpose(0, 3, 2, 1),
        "u_tab": a["peer_u"][0],
        "v_tab": a["peer_v"][0],
    }


def kernel(**inputs):
    import concourse.bacc as _bacc
    from concourse.bass_utils import run_bass_kernel_spmd as _run

    nc = _bacc.Bacc("TRN2", target_bir_lowering=False, num_devices=1)
    arrays, io = {}, {}
    for name, a in layout({name: np.asarray(a) for name, a in inputs.items()}).items():
        a = np.ascontiguousarray(a)
        arrays[f"in_{name}"] = a
        io[name] = nc.dram_tensor(f"in_{name}", a.shape, mybir.dt.from_np(a.dtype), kind="ExternalInput").ap()
    out = nc.dram_tensor("out_0", (1, T, D), F32, kind="ExternalOutput").ap()
    program(nc, io, out.rearrange("a (n p) d -> (a n) p d", p=P))
    result = _run(nc, [arrays], core_ids=[0])
    return result.results[0]["out_0"]
```
